# Optimizing a Trainium2 kernel written in Bass

```python
import math
import jax, jax.numpy as jnp
from jax import lax
import numpy as np
import jax
import jax.numpy as jnp

D_MODEL = 1024
BATCH = 1
SEQ = 256
DEPTH = 2

N_META = 16
DN_HEADS = 4
DN_DK = 128
DN_DV = 128
DN_KEY = DN_HEADS * DN_DK
DN_VAL = DN_HEADS * DN_DV
CONV_W = 4
CHUNK = 64
SA_HEADS = 8
SA_DH = 64
SA_W = SA_HEADS * SA_DH
IDX_HEADS = 8
IDX_DH = 64
K_MAX = 256
Q_BLOCK = 128
ROPE_THETA = 10000.0
MIX_W = DN_VAL + SA_W
N_GROUPS = 4
EXP_PER_GROUP = 8
N_EXPERTS = N_GROUPS * EXP_PER_GROUP
TOP_K_IN_GROUP = 2
D_EXPERT = 256
DEEPNORM_ALPHA = (2.0 * DEPTH) ** 0.25
DEEPNORM_BETA = (8.0 * DEPTH) ** -0.25

SPLIT_SIZES = (DN_KEY, DN_KEY, DN_VAL, DN_VAL, DN_HEADS, DN_HEADS,
               SA_W, SA_W, SA_W, IDX_HEADS * IDX_DH, IDX_DH, IDX_HEADS)
SPLIT_POINTS = tuple(int(s) for s in np.cumsum(SPLIT_SIZES)[:-1])
D_IN_PROJ = int(sum(SPLIT_SIZES))
VALUE_COLS = (2, 8)


F32 = jnp.float32

def layer_norm(x, g, b, eps=1e-5):
    xf = x.astype(F32)
    mu = jnp.mean(xf, -1, keepdims=True)
    var = jnp.mean(jnp.square(xf - mu), -1, keepdims=True)
    return ((xf - mu) * lax.rsqrt(var + eps) * g + b).astype(x.dtype)

def rope_tables(n_pos, dim):
    inv = 1.0 / (ROPE_THETA ** (jnp.arange(0, dim, 2, dtype=F32) / dim))
    ang = jnp.arange(n_pos, dtype=F32)[:, None] * inv[None, :]
    ang = jnp.concatenate([ang, ang], -1)
    return jnp.cos(ang), jnp.sin(ang)

def apply_rope(x, cos, sin):
    half = x.shape[-1] // 2
    rot = jnp.concatenate([-x[..., half:], x[..., :half]], -1)
    shape = (1, cos.shape[0]) + (1,) * (x.ndim - 3) + (cos.shape[-1],)
    return (x * cos.reshape(shape) + rot * sin.reshape(shape)).astype(x.dtype)

def causal_dwconv(x, w):
    c = x.shape[-1]
    return lax.conv_general_dilated(x, w[:, None, :].astype(x.dtype), window_strides=(1,),
                                    padding=[(CONV_W - 1, 0)],
                                    dimension_numbers=('NWC', 'WIO', 'NWC'),
                                    feature_group_count=c)

def l2norm(x, eps=1e-6):
    return x * lax.rsqrt(jnp.sum(x * x, -1, keepdims=True) + eps)

def chunk_gated_delta_rule(q, k, v, g, beta):
    bsz, seq, h, dk = q.shape
    dv = v.shape[-1]
    n = seq // CHUNK

    def chunks(t):
        t = t.reshape((bsz, n, CHUNK, h) + t.shape[3:])
        return jnp.moveaxis(t, 3, 2)

    q, k, v, g, beta = (chunks(t) for t in (q, k, v, g, beta))
    q = q * dk ** -0.5
    gc = jnp.cumsum(g, axis=-1)
    pos = jnp.arange(CHUNK)
    tril = pos[:, None] >= pos[None, :]
    strict = pos[:, None] > pos[None, :]
    decay = jnp.exp(jnp.where(tril, gc[..., :, None] - gc[..., None, :], -jnp.inf))
    kb = k * beta[..., None]
    lower = jnp.where(strict, jnp.einsum('bnhid,bnhjd->bnhij', kb, k) * decay, 0.0)
    eye = jnp.eye(CHUNK, dtype=q.dtype)
    tmat = lax.linalg.triangular_solve(eye + lower, jnp.broadcast_to(eye, lower.shape),
                                       left_side=True, lower=True, unit_diagonal=True)
    u = tmat @ (v * beta[..., None])
    w = tmat @ (kb * jnp.exp(gc)[..., None])
    q_dec = q * jnp.exp(gc)[..., None]
    a_qk = jnp.where(tril, jnp.einsum('bnhid,bnhjd->bnhij', q, k) * decay, 0.0)
    g_last = gc[..., -1]
    k_dec = k * jnp.exp(g_last[..., None] - gc)[..., None]

    def step(state, inp):
        u_n, w_n, qd_n, a_n, kd_n, gl_n = inp
        v_new = u_n - jnp.einsum('bhck,bhkv->bhcv', w_n, state)
        o_n = jnp.einsum('bhck,bhkv->bhcv', qd_n, state) + jnp.einsum('bhij,bhjv->bhiv', a_n, v_new)
        state = state * jnp.exp(gl_n)[..., None, None] + jnp.einsum('bhck,bhcv->bhkv', kd_n, v_new)
        return state, o_n

    xs = tuple(jnp.moveaxis(t, 1, 0) for t in (u, w, q_dec, a_qk, k_dec, g_last))
    s0 = jnp.zeros((bsz, h, dk, dv), q.dtype)
    _, o = lax.scan(step, s0, xs)
    o = jnp.moveaxis(o, 0, 1)
    return jnp.moveaxis(o, 3, 2).reshape(bsz, seq, h, dv)

def deltanet_group(q, k, v, z, b_logit, a_logit, conv_w, a_log, dt_bias, norm_g):
    bsz, seq, _ = q.shape
    qkv = jax.nn.silu(causal_dwconv(jnp.concatenate([q, k, v], -1), conv_w)).astype(F32)
    q, k, v = jnp.split(qkv, [DN_KEY, 2 * DN_KEY], axis=-1)
    q = l2norm(q.reshape(bsz, seq, DN_HEADS, DN_DK))
    k = l2norm(k.reshape(bsz, seq, DN_HEADS, DN_DK))
    v = v.reshape(bsz, seq, DN_HEADS, DN_DV)
    beta = jax.nn.sigmoid(b_logit.astype(F32))
    g = -jnp.exp(a_log.astype(F32)) * jax.nn.softplus(a_logit.astype(F32) + dt_bias.astype(F32))
    pad = (-N_META) % CHUNK
    padf = lambda t: jnp.pad(t, ((0, 0), (pad, 0)) + ((0, 0),) * (t.ndim - 2))
    o = chunk_gated_delta_rule(padf(q), padf(k), padf(v), padf(g), padf(beta))[:, pad:]
    o = o * lax.rsqrt(jnp.mean(o * o, -1, keepdims=True) + 1e-6) * norm_g
    o = o.reshape(bsz, seq, DN_VAL) * jax.nn.silu(z.astype(F32))
    return o.astype(z.dtype)

def dsa_group(q, k, v, qi, ki, wi, cos, sin, cos_i, sin_i, k_top):
    bsz, seq, _ = q.shape
    q = apply_rope(q.reshape(bsz, seq, SA_HEADS, SA_DH), cos, sin)
    k = apply_rope(k.reshape(bsz, seq, SA_HEADS, SA_DH), cos, sin)
    v = v.reshape(bsz, seq, SA_HEADS, SA_DH)
    qi = apply_rope(qi.reshape(bsz, seq, IDX_HEADS, IDX_DH), cos_i, sin_i)
    ki = apply_rope(ki, cos_i, sin_i)
    wi = wi.astype(F32) * IDX_HEADS ** -0.5
    n_blk = -(-seq // Q_BLOCK)
    lq = n_blk * Q_BLOCK

    def blocks(t):
        t = jnp.pad(t, ((0, 0), (0, lq - seq)) + ((0, 0),) * (t.ndim - 2))
        return jnp.moveaxis(t.reshape((bsz, n_blk, Q_BLOCK) + t.shape[2:]), 1, 0)

    key_pos = jnp.arange(seq)
    q_pos = jnp.arange(lq).reshape(n_blk, Q_BLOCK)
    gather = jax.vmap(lambda arr, idx: arr[idx])

    def attend(args):
        qb, qib, wib, pos = args
        causal = key_pos[None, :] <= pos[:, None]
        rel = jax.nn.relu(jnp.einsum('bqhd,bsd->bqhs', qib, ki, preferred_element_type=F32) * IDX_DH ** -0.5)
        score = jnp.einsum('bqhs,bqh->bqs', rel, wib)
        score = jnp.where(causal[None], score, -jnp.inf)
        _, sel = lax.top_k(score, k_top)
        k_sel = gather(k, sel)
        v_sel = gather(v, sel)
        valid = sel <= pos[None, :, None]
        logits = jnp.einsum('bqhd,bqkhd->bhqk', qb, k_sel, preferred_element_type=F32) * SA_DH ** -0.5
        logits = jnp.where(valid[:, None], logits, -jnp.inf)
        p = jax.nn.softmax(logits, axis=-1)
        return jnp.einsum('bhqk,bqkhd->bqhd', p.astype(v.dtype), v_sel)

    out = lax.map(attend, (blocks(q), blocks(qi), blocks(wi), q_pos))
    return jnp.moveaxis(out, 0, 1).reshape(bsz, lq, SA_W)[:, :seq]

def hier_moe(h, w_grp, b_grp, w_rtr, b_rtr, w1, w3, w2):
    bsz, seq, d = h.shape
    t = h.reshape(-1, d)
    grp_prob = jax.nn.softmax((t @ w_grp).astype(F32) + b_grp, axis=-1)
    g_prob, g_sel = lax.top_k(grp_prob, 1)
    exp_logits = ((t @ w_rtr).astype(F32) + b_rtr).reshape(-1, N_GROUPS, EXP_PER_GROUP)
    in_grp = jnp.take_along_axis(exp_logits, g_sel[:, :, None], axis=1)[:, 0]
    e_prob, e_sel = lax.top_k(jax.nn.softmax(in_grp, axis=-1), TOP_K_IN_GROUP)
    gate = g_prob * e_prob / jnp.sum(e_prob, -1, keepdims=True)
    expert_id = g_sel * EXP_PER_GROUP + e_sel
    combine = jnp.sum(jax.nn.one_hot(expert_id, N_EXPERTS, dtype=F32) * gate[..., None], axis=1)
    hid = jax.nn.silu(jnp.einsum('td,edf->tef', t, w1)) * jnp.einsum('td,edf->tef', t, w3)
    y = jnp.einsum('tef,efd->td', hid * combine[..., None].astype(hid.dtype), w2)
    return y.reshape(bsz, seq, d)

def first_inputs(seed: int = 0) -> dict:
    key = jax.random.key(seed)
    ks = jax.random.split(key, 20)
    nrm = lambda k, shape, s: jax.random.normal(k, shape, F32) * s
    d_sc = D_MODEL ** -0.5
    col_scale = np.concatenate([np.full((s,), DEEPNORM_BETA if i in VALUE_COLS else 1.0, np.float32)
                                for i, s in enumerate(SPLIT_SIZES)])
    dt = jnp.exp(jax.random.uniform(ks[5], (DEPTH, DN_HEADS), F32, math.log(1e-3), math.log(1e-1)))
    return {
        'x': nrm(ks[0], (BATCH, SEQ, D_MODEL), 1.0),
        'meta_tokens': nrm(ks[1], (N_META, D_MODEL), 1.0),
        'w_in': nrm(ks[2], (DEPTH, D_MODEL, D_IN_PROJ), d_sc) * jnp.asarray(col_scale),
        'conv_w': nrm(ks[3], (DEPTH, CONV_W, 2 * DN_KEY + DN_VAL), CONV_W ** -0.5),
        'a_log': jnp.log(jax.random.uniform(ks[4], (DEPTH, DN_HEADS), F32, 1.0, 16.0)),
        'dt_bias': dt + jnp.log(-jnp.expm1(-dt)),
        'dn_norm_g': 1.0 + nrm(ks[6], (DEPTH, DN_DV), 0.02),
        'w_out': nrm(ks[7], (DEPTH, MIX_W, D_MODEL), MIX_W ** -0.5 * DEEPNORM_BETA),
        'ln1_g': 1.0 + nrm(ks[8], (DEPTH, D_MODEL), 0.02),
        'ln1_b': nrm(ks[9], (DEPTH, D_MODEL), 0.02),
        'w_grp': nrm(ks[10], (DEPTH, D_MODEL, N_GROUPS), d_sc),
        'b_grp': nrm(ks[11], (DEPTH, N_GROUPS), 0.01),
        'w_rtr': nrm(ks[12], (DEPTH, D_MODEL, N_EXPERTS), d_sc),
        'b_rtr': nrm(ks[13], (DEPTH, N_EXPERTS), 0.01),
        'w1': nrm(ks[14], (DEPTH, N_EXPERTS, D_MODEL, D_EXPERT), d_sc),
        'w3': nrm(ks[15], (DEPTH, N_EXPERTS, D_MODEL, D_EXPERT), d_sc),
        'w2': nrm(ks[16], (DEPTH, N_EXPERTS, D_EXPERT, D_MODEL), D_EXPERT ** -0.5 * DEEPNORM_BETA),
        'ln2_g': 1.0 + nrm(ks[17], (DEPTH, D_MODEL), 0.02),
        'ln2_b': nrm(ks[18], (DEPTH, D_MODEL), 0.02),
    }

def first_block(x, meta_tokens, w_in, conv_w, a_log, dt_bias, dn_norm_g, w_out, ln1_g, ln1_b,
              w_grp, b_grp, w_rtr, b_rtr, w1, w3, w2, ln2_g, ln2_b):
    bsz, seq, _ = x.shape
    total = seq + N_META
    k_top = min(K_MAX, seq // 4)
    meta = jnp.broadcast_to(meta_tokens[None].astype(x.dtype), (bsz, N_META, D_MODEL))
    h = jnp.concatenate([meta, x], axis=1)
    cos, sin = rope_tables(total, SA_DH)
    cos_i, sin_i = rope_tables(total, IDX_DH)
    for l in range(DEPTH):
        proj = h @ w_in[l]
        dq, dk, dv, dz, db, da, sq, sk, sv, iq, ik, iw = jnp.split(proj, SPLIT_POINTS, axis=-1)
        o_dn = deltanet_group(dq, dk, dv, dz, db, da, conv_w[l], a_log[l], dt_bias[l], dn_norm_g[l])
        o_sa = dsa_group(sq, sk, sv, iq, ik, iw, cos, sin, cos_i, sin_i, k_top)
        mix = jnp.concatenate([o_dn, o_sa.astype(o_dn.dtype)], axis=-1) @ w_out[l]
        h = layer_norm(DEEPNORM_ALPHA * h + mix, ln1_g[l], ln1_b[l])
        ffn = hier_moe(h, w_grp[l], b_grp[l], w_rtr[l], b_rtr[l], w1[l], w3[l], w2[l])
        h = layer_norm(DEEPNORM_ALPHA * h + ffn, ln2_g[l], ln2_b[l])
    return h[:, N_META:]


MEM_LEN = 256

NSA_HEADS = 8
NSA_GROUPS = 2
NSA_HEAD_DIM = 64
CMP_BLOCK = 32
CMP_STRIDE = 16
CMP_HIDDEN = 4 * NSA_HEAD_DIM
SEL_BLOCK = 64
N_SEL = 16
WINDOW = 512
NSA_QBLOCK = 64
FORCE_SCORE = 1e4

GLA_HEADS = 4
GLA_HEAD_DK = 64
GLA_HEAD_DV = 128
GLA_RANK = 16
GLA_TAU = 16.0
GLA_CHUNK = 64

MEM_HEADS = 4
MEM_HEAD_DIM = 128

N_BRANCH = 3
BRANCH_WIDTH = NSA_HEADS * NSA_HEAD_DIM
MLP_HIDDEN = 4 * D_MODEL
ROPE_THETA_2 = 500000.0
ROPE_FRACTION = 4
NORM_EPS = 1e-6

IN_SIZES = (
    NSA_HEADS * NSA_HEAD_DIM,
    NSA_GROUPS * NSA_HEAD_DIM,
    NSA_GROUPS * NSA_HEAD_DIM,
    NSA_GROUPS * NSA_HEAD_DIM,
    NSA_GROUPS * NSA_HEAD_DIM,
    NSA_GROUPS * NSA_HEAD_DIM,
    NSA_GROUPS * NSA_HEAD_DIM,
    NSA_HEADS * 3,
    GLA_HEADS * GLA_HEAD_DK,
    GLA_HEADS * GLA_HEAD_DK,
    GLA_HEADS * GLA_HEAD_DV,
    GLA_HEADS * GLA_HEAD_DV,
    GLA_RANK,
    MEM_HEADS * MEM_HEAD_DIM,
    N_BRANCH * D_MODEL,
)
D_IN = sum(IN_SIZES)


def rms_norm(x, g):
    xf = x.astype(jnp.float32)
    y = xf * lax.rsqrt(jnp.mean(xf * xf, axis=-1, keepdims=True) + NORM_EPS)
    return (y * g.astype(jnp.float32)).astype(x.dtype)

def split_heads(t, n):
    B, S, _ = t.shape
    return t.reshape(B, S, n, -1).transpose(0, 2, 1, 3)

def partial_rope(x, pos):
    rot = x.shape[-1] // ROPE_FRACTION
    half = rot // 2
    inv_freq = jnp.power(ROPE_THETA_2, -jnp.arange(half, dtype=jnp.float32) / half)
    ang = pos.astype(jnp.float32)[:, None, :, None] * inv_freq
    cos, sin = jnp.cos(ang), jnp.sin(ang)
    xf = x.astype(jnp.float32)
    x1, x2, rest = xf[..., :half], xf[..., half:rot], xf[..., rot:]
    out = jnp.concatenate([x1 * cos - x2 * sin, x2 * cos + x1 * sin, rest], axis=-1)
    return out.astype(x.dtype)

def masked_softmax(s, mask):
    s = jnp.where(mask, s.astype(jnp.float32), -jnp.inf)
    m = jnp.max(s, axis=-1, keepdims=True)
    m = jnp.where(jnp.isfinite(m), m, 0.0)
    p = jnp.exp(s - m)
    d = jnp.sum(p, axis=-1, keepdims=True)
    return p / jnp.where(d > 0, d, 1.0)

def nsa_attention(q, k_c, v_c, k_s, v_s, k_w, v_w, gate_logits, positions,
                  q_norm, k_norm, cmp_pe, cmp_w1, cmp_w2):
    B, S, _ = q.shape
    H, G, dh, QB = NSA_HEADS, NSA_GROUPS, NSA_HEAD_DIM, NSA_QBLOCK
    R = H // G
    q = partial_rope(rms_norm(split_heads(q, H), q_norm), positions) * (dh ** -0.5)
    k_s = partial_rope(rms_norm(split_heads(k_s, G), k_norm[1]), positions)
    k_w = partial_rope(rms_norm(split_heads(k_w, G), k_norm[2]), positions)
    v_s = split_heads(v_s, G)
    v_w = split_heads(v_w, G)

    n_cmp = (S - CMP_BLOCK) // CMP_STRIDE + 1
    cmp_idx = np.arange(n_cmp)[:, None] * CMP_STRIDE + np.arange(CMP_BLOCK)[None, :]
    cmp_end_np = cmp_idx[:, -1]
    raw = jnp.stack([split_heads(k_c, G), split_heads(v_c, G)])[:, :, :, cmp_idx]
    raw = (raw + cmp_pe[:, None, None, None]).reshape(2, B, G, n_cmp, CMP_BLOCK * dh)
    hid = jax.nn.gelu(jnp.einsum('kbgnf,kfe->kbgne', raw, cmp_w1))
    comp = jnp.einsum('kbgne,ked->kbgnd', hid, cmp_w2)
    k_cmp = partial_rope(rms_norm(comp[0], k_norm[0]), positions[:, cmp_end_np])
    v_cmp = comp[1]
    cmp_end = jnp.asarray(cmp_end_np, jnp.int32)

    n_blk = S // SEL_BLOCK
    c_start = np.arange(n_cmp) * CMP_STRIDE
    b_start = np.arange(n_blk) * SEL_BLOCK
    overlap = jnp.asarray(((c_start[:, None] < b_start[None, :] + SEL_BLOCK)
                           & (b_start[None, :] < c_start[:, None] + CMP_BLOCK)).astype(np.float32))
    n_sel = min(N_SEL, n_blk)
    ks_blk = k_s.reshape(B, G, n_blk, SEL_BLOCK, dh)
    vs_blk = v_s.reshape(B, G, n_blk, SEL_BLOCK, dh)
    kw_pad = jnp.pad(k_w, ((0, 0), (0, 0), (WINDOW, 0), (0, 0)))
    vw_pad = jnp.pad(v_w, ((0, 0), (0, 0), (WINDOW, 0), (0, 0)))

    n_qb = S // QB
    q_blocks = q.reshape(B, H, n_qb, QB, dh).transpose(2, 0, 1, 3, 4).reshape(n_qb, B, G, R, QB, dh)
    gates = jax.nn.sigmoid(gate_logits.astype(jnp.float32)).astype(q.dtype)
    g_blocks = (gates.reshape(B, S, H, 3).transpose(0, 2, 1, 3)
                .reshape(B, H, n_qb, QB, 3).transpose(2, 0, 1, 3, 4).reshape(n_qb, B, G, R, QB, 3))
    gather_blocks = jax.vmap(jax.vmap(lambda blk, ix: blk[ix]))
    blk_ids = jnp.arange(n_blk)

    def query_block(args):
        qi, qb, gb = args
        t = qi * QB + jnp.arange(QB)
        s_c = jnp.einsum('bgrqd,bgnd->bgrqn', qb, k_cmp)
        p_c = masked_softmax(s_c, cmp_end[None, :] <= t[:, None])
        o_c = jnp.einsum('bgrqn,bgnd->bgrqd', p_c.astype(v_cmp.dtype), v_cmp)
        imp = jnp.einsum('bgqn,nj->bgqj', jnp.sum(p_c, axis=2), overlap)
        causal = (blk_ids * SEL_BLOCK)[None, :] <= t[:, None]
        cur = (t // SEL_BLOCK)[:, None]
        forced = causal & ((blk_ids[None, :] == 0) | (blk_ids[None, :] == cur)
                           | (blk_ids[None, :] == cur - 1))
        score = jnp.where(forced, FORCE_SCORE, jnp.where(causal, imp, -FORCE_SCORE))
        _, idx = lax.top_k(score, n_sel)
        k_g = gather_blocks(ks_blk, idx)
        v_g = gather_blocks(vs_blk, idx)
        kpos = idx[..., None] * SEL_BLOCK + jnp.arange(SEL_BLOCK)
        mask_s = (kpos <= t[:, None, None])[:, :, None].reshape(B, G, 1, QB, n_sel * SEL_BLOCK)
        s_s = jnp.einsum('bgrqd,bgqnld->bgrqnl', qb, k_g).reshape(B, G, R, QB, n_sel * SEL_BLOCK)
        p_s = masked_softmax(s_s, mask_s).reshape(B, G, R, QB, n_sel, SEL_BLOCK)
        o_s = jnp.einsum('bgrqnl,bgqnld->bgrqd', p_s.astype(v_g.dtype), v_g)
        kwb = lax.dynamic_slice_in_dim(kw_pad, qi * QB, WINDOW + QB, axis=2)
        vwb = lax.dynamic_slice_in_dim(vw_pad, qi * QB, WINDOW + QB, axis=2)
        kp = qi * QB - WINDOW + jnp.arange(WINDOW + QB)
        mask_w = ((kp[None, :] <= t[:, None]) & (kp[None, :] > t[:, None] - WINDOW)
                  & (kp[None, :] >= 0))
        p_w = masked_softmax(jnp.einsum('bgrqd,bgkd->bgrqk', qb, kwb), mask_w)
        o_w = jnp.einsum('bgrqk,bgkd->bgrqd', p_w.astype(vwb.dtype), vwb)
        return gb[..., 0:1] * o_c + gb[..., 1:2] * o_s + gb[..., 2:3] * o_w

    out = lax.map(query_block, (jnp.arange(n_qb), q_blocks, g_blocks))
    return out.reshape(n_qb, B, H, QB, dh).transpose(1, 0, 3, 2, 4).reshape(B, S, H * dh)

def gated_linear_attention(q, k, v, r, g_low, w_gate, b_gate, norm_g):
    B, S, _ = q.shape
    H, C = GLA_HEADS, GLA_CHUNK
    n_c = S // C
    log_a = jax.nn.log_sigmoid((g_low @ w_gate + b_gate).astype(jnp.float32)) / GLA_TAU

    def chunks(t):
        return t.astype(jnp.float32).reshape(B, n_c, C, H, -1).transpose(1, 0, 3, 2, 4)

    qc = chunks(q) * (GLA_HEAD_DK ** -0.5)
    kc, vc, ac = chunks(k), chunks(v), chunks(log_a)
    tril = jnp.tril(jnp.ones((C, C), dtype=bool))

    def step(state, xs):
        qb, kb, vb, ab = xs
        b = jnp.cumsum(ab, axis=2)
        decay = jnp.exp(jnp.where(tril[:, :, None], b[:, :, :, None, :] - b[:, :, None, :, :], -jnp.inf))
        attn = jnp.einsum('bhid,bhjd,bhijd->bhij', qb, kb, decay)
        o = attn @ vb + jnp.einsum('bhid,bhdv->bhiv', qb * jnp.exp(b), state)
        b_last = b[:, :, -1:, :]
        state = (jnp.exp(b_last)[:, :, 0, :, None] * state
                 + jnp.einsum('bhjd,bhjv->bhdv', kb * jnp.exp(b_last - b), vb))
        return state, o

    state0 = jnp.zeros((B, H, GLA_HEAD_DK, GLA_HEAD_DV), jnp.float32)
    _, o = lax.scan(step, state0, (qc, kc, vc, ac))
    o = o.transpose(1, 0, 3, 2, 4).reshape(B, S, H, GLA_HEAD_DV)
    o = rms_norm(o, norm_g).reshape(B, S, H * GLA_HEAD_DV)
    return (o * jax.nn.silu(r.astype(jnp.float32))).astype(q.dtype)

def memory_attention(q, mem, mem_norm, w_kv, q_norm, k_norm):
    B, S, _ = q.shape
    H, dh = MEM_HEADS, MEM_HEAD_DIM
    k, v = jnp.split(rms_norm(mem, mem_norm) @ w_kv, 2, axis=-1)
    q = rms_norm(split_heads(q, H), q_norm) * (dh ** -0.5)
    k = rms_norm(split_heads(k, H), k_norm)
    v = split_heads(v, H)
    p = jax.nn.softmax(jnp.einsum('bhsd,bhmd->bhsm', q, k).astype(jnp.float32), axis=-1)
    o = jnp.einsum('bhsm,bhmd->bhsd', p.astype(v.dtype), v)
    return o.transpose(0, 2, 1, 3).reshape(B, S, H * dh)

def hybrid_layer(x, mem, positions, ln_mix, w_in, b_merge, nsa_q_norm, nsa_k_norm,
                 cmp_pe, cmp_w1, cmp_w2, gla_w_gate, gla_b_gate, gla_norm,
                 mem_norm, mem_w_kv, mem_q_norm, mem_k_norm, w_branch, w_out,
                 ln_mlp, w_up, w_down):
    B, S, D = x.shape
    h = rms_norm(x, ln_mix)
    z = h @ w_in
    offsets = np.cumsum(IN_SIZES)[:-1].tolist()
    (n_q, n_kc, n_vc, n_ks, n_vs, n_kw, n_vw, n_g,
     g_q, g_k, g_v, g_r, g_low, m_q, merge) = jnp.split(z, offsets, axis=-1)
    o_nsa = nsa_attention(n_q, n_kc, n_vc, n_ks, n_vs, n_kw, n_vw, n_g, positions,
                          nsa_q_norm, nsa_k_norm, cmp_pe, cmp_w1, cmp_w2)
    o_gla = gated_linear_attention(g_q, g_k, g_v, g_r, g_low, gla_w_gate, gla_b_gate, gla_norm)
    o_mem = memory_attention(m_q, mem, mem_norm, mem_w_kv, mem_q_norm, mem_k_norm)
    gates = jax.nn.sigmoid((merge.reshape(B, S, N_BRANCH, D) + b_merge).astype(jnp.float32)).astype(x.dtype)
    merged = (gates[:, :, 0] * (o_nsa @ w_branch[0])
              + gates[:, :, 1] * (o_gla @ w_branch[1])
              + gates[:, :, 2] * (o_mem @ w_branch[2]))
    x = x + merged @ w_out
    h = rms_norm(x, ln_mlp)
    return x + jnp.square(jax.nn.relu(h @ w_up)) @ w_down

def second_inputs(seed: int = 0) -> dict:
    key = jax.random.key(seed)
    ks = jax.random.split(key, 24)
    f32 = jnp.float32
    dh = NSA_HEAD_DIM
    resid = (2 * DEPTH) ** -0.5

    def nrm(k, shape, scale):
        return jax.random.normal(k, shape, f32) * scale

    def gain(k, shape):
        return 1.0 + 0.02 * jax.random.normal(k, shape, f32)

    positions = (jnp.arange(SEQ, dtype=jnp.int32)[None, :]
                 + jax.random.randint(ks[2], (BATCH, 1), 0, SEQ, dtype=jnp.int32))
    return {
        'x': nrm(ks[0], (BATCH, SEQ, D_MODEL), 1.0),
        'mem': nrm(ks[1], (BATCH, MEM_LEN, D_MODEL), 1.0),
        'positions': positions,
        'ln_mix': gain(ks[3], (DEPTH, D_MODEL)),
        'w_in': nrm(ks[4], (DEPTH, D_MODEL, D_IN), D_MODEL ** -0.5),
        'b_merge': nrm(ks[5], (DEPTH, N_BRANCH, D_MODEL), 0.02),
        'nsa_q_norm': gain(ks[6], (DEPTH, dh)),
        'nsa_k_norm': gain(ks[7], (DEPTH, 3, dh)),
        'cmp_pe': nrm(ks[8], (DEPTH, 2, CMP_BLOCK, dh), 0.02),
        'cmp_w1': nrm(ks[9], (DEPTH, 2, CMP_BLOCK * dh, CMP_HIDDEN), (CMP_BLOCK * dh) ** -0.5),
        'cmp_w2': nrm(ks[10], (DEPTH, 2, CMP_HIDDEN, dh), CMP_HIDDEN ** -0.5),
        'gla_w_gate': nrm(ks[11], (DEPTH, GLA_RANK, GLA_HEADS * GLA_HEAD_DK), GLA_RANK ** -0.5),
        'gla_b_gate': nrm(ks[12], (DEPTH, GLA_HEADS * GLA_HEAD_DK), 0.02),
        'gla_norm': gain(ks[13], (DEPTH, GLA_HEAD_DV)),
        'mem_norm': gain(ks[14], (DEPTH, D_MODEL)),
        'mem_w_kv': nrm(ks[15], (DEPTH, D_MODEL, 2 * MEM_HEADS * MEM_HEAD_DIM), D_MODEL ** -0.5),
        'mem_q_norm': gain(ks[16], (DEPTH, MEM_HEAD_DIM)),
        'mem_k_norm': gain(ks[17], (DEPTH, MEM_HEAD_DIM)),
        'w_branch': nrm(ks[18], (DEPTH, N_BRANCH, BRANCH_WIDTH, D_MODEL), BRANCH_WIDTH ** -0.5),
        'w_out': nrm(ks[19], (DEPTH, D_MODEL, D_MODEL), D_MODEL ** -0.5 * resid),
        'ln_mlp': gain(ks[20], (DEPTH, D_MODEL)),
        'w_up': nrm(ks[21], (DEPTH, D_MODEL, MLP_HIDDEN), D_MODEL ** -0.5),
        'w_down': nrm(ks[22], (DEPTH, MLP_HIDDEN, D_MODEL), MLP_HIDDEN ** -0.5 * resid),
    }

def second_block(x, mem, positions, ln_mix, w_in, b_merge, nsa_q_norm, nsa_k_norm,
              cmp_pe, cmp_w1, cmp_w2, gla_w_gate, gla_b_gate, gla_norm,
              mem_norm, mem_w_kv, mem_q_norm, mem_k_norm, w_branch, w_out,
              ln_mlp, w_up, w_down):
    for l in range(DEPTH):
        x = hybrid_layer(x, mem, positions, ln_mix[l], w_in[l], b_merge[l],
                         nsa_q_norm[l], nsa_k_norm[l], cmp_pe[l], cmp_w1[l], cmp_w2[l],
                         gla_w_gate[l], gla_b_gate[l], gla_norm[l],
                         mem_norm[l], mem_w_kv[l], mem_q_norm[l], mem_k_norm[l],
                         w_branch[l], w_out[l], ln_mlp[l], w_up[l], w_down[l])
    return x


def setup_inputs(seed=0):
    out = dict(first_inputs(seed))
    for name, value in second_inputs(seed + 1).items():
        if name != "x":
            out[name + "_2"] = value
    return out


def reference(
    x, meta_tokens, w_in, conv_w, a_log, dt_bias, dn_norm_g, w_out, ln1_g, ln1_b, w_grp, b_grp,
    w_rtr, b_rtr, w1, w3, w2, ln2_g, ln2_b, mem_2, positions_2, ln_mix_2, w_in_2, b_merge_2,
    nsa_q_norm_2, nsa_k_norm_2, cmp_pe_2, cmp_w1_2, cmp_w2_2, gla_w_gate_2, gla_b_gate_2,
    gla_norm_2, mem_norm_2, mem_w_kv_2, mem_q_norm_2, mem_k_norm_2, w_branch_2, w_out_2,
    ln_mlp_2, w_up_2, w_down_2,
):
    x = first_block(
        x, meta_tokens, w_in, conv_w, a_log, dt_bias, dn_norm_g, w_out, ln1_g, ln1_b, w_grp,
        b_grp, w_rtr, b_rtr, w1, w3, w2, ln2_g, ln2_b,
    )
    return second_block(
        x, mem_2, positions_2, ln_mix_2, w_in_2, b_merge_2, nsa_q_norm_2, nsa_k_norm_2,
        cmp_pe_2, cmp_w1_2, cmp_w2_2, gla_w_gate_2, gla_b_gate_2, gla_norm_2, mem_norm_2,
        mem_w_kv_2, mem_q_norm_2, mem_k_norm_2, w_branch_2, w_out_2, ln_mlp_2, w_up_2, w_down_2,
    )


_drawn_inputs = setup_inputs


def setup_inputs(seed=0):
    import zlib

    import numpy as np

    out = dict(_drawn_inputs(seed))
    spreads = {}
    factors = {'dn_norm_g': 5.228,
     'b_grp': 5.007,
     'b_rtr': 4.242,
     'ln_mix_2': 5.64,
     'b_merge_2': 8.0,
     'nsa_q_norm_2': 8.0,
     'nsa_k_norm_2': 8.0,
     'cmp_pe_2': 29.596,
     'gla_b_gate_2': 8.0,
     'gla_norm_2': 8.0,
     'mem_norm_2': 8.0,
     'mem_q_norm_2': 8.0,
     'mem_k_norm_2': 8.0,
     'ln_mlp_2': 3.414}
    for name, (base, spread) in spreads.items():
        noise = np.random.default_rng([zlib.crc32(name.encode()), seed]).standard_normal(out[name].shape)
        drawn = base * np.exp(spread * noise) if base else spread * noise
        out[name] = jnp.asarray(drawn.astype(out[name].dtype))
    for name, factor in factors.items():
        out[name] = (out[name] * factor).astype(out[name].dtype)
    return out
```

```python
from contextlib import ExitStack

import numpy as np

import concourse.bass as bass
from concourse import mybir

F32 = mybir.dt.float32
I32 = mybir.dt.int32
ALU = mybir.AluOpType
ACT = mybir.ActivationFunctionType
AX = mybir.AxisListType

P = 128
D = 1024
KT = D // P
DEPTH = 2
N_META = 16
SEQ = 256
T = SEQ + N_META
TILES = [(0, 128), (128, 128), (256, 16)]
TOP_K = SEQ // 4
EXPERTS, GROUPS, PER_GROUP, DE = 32, 4, 8, 256
ALPHA = (2.0 * DEPTH) ** 0.25
BIG = 1e30
SLOTS = 4
SLOT = KT * 512


class WeightRing:

    def __init__(self, loaded, used):
        self.loaded, self.used = loaded, used
        self.in_slot = [0] * SLOTS
        self.last_in_slot = [None] * SLOTS
        self.chunks = {}
        self.n = 0

    def add(self, name, slot, dmas=1):
        before = self.last_in_slot[slot]
        self.in_slot[slot] += 16 * dmas
        self.chunks[name] = (slot, self.in_slot[slot], None if before is None else before + 1)
        self.last_in_slot[slot] = self.n
        self.n += 1

    def arrived(self, name):
        slot, value, _ = self.chunks[name]
        return self.loaded[slot], value

    def freed(self, name):
        before = self.chunks[name][2]
        return None if before is None else (self.used, before)


def constants():
    i = np.arange(P)
    c = {}
    c["ident"] = np.eye(P)
    c["ones"] = np.ones((P, P))
    c["mean_w"] = np.full((P, P), 1.0 / D)
    c["cum"] = i[:, None] <= i[None, :]
    c["strict"] = i[:, None] > i[None, :]
    c["incl"] = i[:, None] >= i[None, :]
    lv = [((i[:, None] >> l) == (i[None, :] >> l) + 1) & ((i[:, None] >> l) % 2 == 1) for l in range(7)]
    c["level0"] = lv[0]
    c["levelsT"] = np.stack([m.T for m in lv], 1)
    t = np.arange(T)
    c["causal"] = np.stack([(t[None, :] <= (t0 + i)[:, None]) for t0, _ in TILES], 1)
    rot = np.zeros((P, P))
    for h in (0, 64):
        for d in range(32):
            rot[h + d + 32, h + d] = -1.0
            rot[h + d, h + d + 32] = 1.0
    c["rot"] = rot
    inv = (1.0 / (np.float32(10000.0) ** (np.arange(0, 64, 2, dtype=np.float32) / np.float32(64)))).astype(np.float32)
    ang = (t.astype(np.float32)[None, :] * inv[i % 32][:, None]).astype(np.float32)
    c["cos"] = np.cos(ang.astype(np.float64))
    c["sin"] = np.sin(ang.astype(np.float64))
    c["rank4"] = np.broadcast_to(4.0 - np.arange(4), (P, 4))
    c["rank8"] = np.broadcast_to(8.0 - np.arange(8), (P, 8))
    return {k: np.ascontiguousarray(v, np.float32) for k, v in c.items()}


class Buffers:
    pass


def load_constants(nc, ctx, arrays, tag=""):
    buffers = {}
    done = ctx.enter_context(nc.semaphore("constants_loaded" + tag))
    for name, a in arrays.items():
        src = nc.inline_tensor(a, name="c_" + name + tag).ap()
        dst = ctx.enter_context(nc.sbuf_tensor("k_" + name + tag, list(a.shape), F32))
        full = tuple(slice(None) for _ in a.shape)
        nc.sync.dma_start(dst[full], src[full]).then_inc(done, 16)
        buffers[name] = dst
    nc.sync.wait_ge(done, 16 * len(arrays))
    return buffers


def projections(nc, m, l, A, S):
    w_in = A["w_in"].rearrange("l (k p) n -> l p k n", p=P)
    W, ring, ps = m.W, m.ring, m.ps
    plan = [("conv", f"in{c}", 128 * j, 4 * c + j) for c in range(3) for j in range(4)]
    plan += [("z", "in3", 128 * j, j) for j in range(4)]
    plan += [("rope", "in4", 128 * j, j) for j in range(4)]
    plan += [("rope", "in5", 128 * j, 4 + j) for j in range(4)]
    plan += [("sv", "in6", 0, j) for j in range(3)]
    plan += [("rope", "in7", 128 * j, 8 + j) for j in range(4)]
    plan += [("rope", "in8", 16, 12)]
    plan += [("bai", "in8", 0, j) for j in range(3)]
    taker = {"conv": "act", "z": "act", "rope": "dve", "sv": "act", "bai": "dve"}
    rope_dst = [m.sqT[:, j, :] for j in range(4)] + [m.skT[:, j, :] for j in range(4)] + \
               [m.iqT[:, j, :] for j in range(4)] + [m.ikT[:, :]]

    def taken(n):
        who = taker[plan[n][0]]
        return (S["proj_by_act"] if who == "act" else S["proj_by_dve"]), sum(taker[p[0]] == who for p in plan[:n + 1])

    with nc.Block() as block:
        @block.sync
        def _(sp):
            pr = m.prm
            src = [(0, 48, A["conv_w"].rearrange("l j (t f) -> l (j t) f", f=P)[l]),
                   (48, 1, A["dn_norm_g"].rearrange("l (a n) -> l a n", a=1)[l]),
                   (49, 8, A["ln1_g"].rearrange("l (t f) -> l t f", f=P)[l]),
                   (57, 8, A["ln1_b"].rearrange("l (t f) -> l t f", f=P)[l]),
                   (65, 8, A["ln2_g"].rearrange("l (t f) -> l t f", f=P)[l]),
                   (73, 8, A["ln2_b"].rearrange("l (t f) -> l t f", f=P)[l])]
            for r0, n, ap in src:
                sp.dma_start(pr[r0:r0 + n, :], ap).then_inc(S["params_loaded"], 16)
            bc = m.rows
            sp.dma_start(bc[:, 0:4], A["a_log"].rearrange("l (a n) -> l a n", a=1)[l].to_broadcast([P, 4])).then_inc(S["rows_loaded"], 16)
            sp.dma_start(bc[:, 4:8], A["dt_bias"].rearrange("l (a n) -> l a n", a=1)[l].to_broadcast([P, 4])).then_inc(S["rows_loaded"], 16)
            sp.dma_start(bc[:, 8:12], A["b_grp"].rearrange("l (a n) -> l a n", a=1)[l].to_broadcast([P, 4])).then_inc(S["rows_loaded"], 16)
            sp.dma_start(bc[:, 12:44], A["b_rtr"].rearrange("l (a n) -> l a n", a=1)[l].to_broadcast([P, 32])).then_inc(S["rows_loaded"], 16)
            for name, c0, n in (("w_grp", 0, 4), ("w_rtr", 4, 32)):
                sp.dma_start(m.w_route[:, :, c0:c0 + n],
                               A[name].rearrange("l (k p) n -> l p k n", p=P)[l]).then_inc(S["rows_loaded"], 16)
            for c in range(9):
                name = f"in{c}"
                free = ring.freed(name)
                if free:
                    sp.wait_ge(*free)
                slot = ring.chunks[name][0]
                done = ring.loaded[slot]
                w = W[:, slot, :].rearrange("p (k n) -> p k n", k=KT)
                if c < 8:
                    c0 = 512 * c + (8 if c >= 4 else 0)
                    sp.dma_start(w[:, :, :], w_in[l, :, :, c0:c0 + 512]).then_inc(done, 16)
                else:
                    sp.dma_start(w[:, :, 0:8], w_in[l, :, :, 2048:2056]).then_inc(done, 16)
                    sp.dma_start(w[:, :, 8:16], w_in[l, :, :, 4168:4176]).then_inc(done, 16)
                    sp.dma_start(w[:, :, 16:80], w_in[l, :, :, 4104:4168]).then_inc(done, 16)
                    sp.dma_start(w[:, :, 80:144], w_in[l, :, :, 4104:4168]).then_inc(done, 16)

        @block.tensor
        def _(pe):
            pe.wait_ge(S["params_loaded"], 16 * 6)
            nc.tensor.transpose(ps[7][:, 0:81], m.prm[0:81, :], m.ident[0:81, 0:81]).then_inc(S["params_turned"], 1)

            def rope_mm(r):
                pe.wait_ge(S["rope_in"], r + 1)
                if r >= 2:
                    pe.wait_ge(S["rope_out"], r - 1)
                o = ps[4 + r % 2][:, 0:T]
                nc.tensor.matmul(o, m.rot[:, :], m.rope_tmp[:, r % 2, 0, :], start=True, stop=False)
                nc.tensor.matmul(o, m.ident[:, :], m.rope_tmp[:, r % 2, 1, :], start=False, stop=True).then_inc(S["rope_mm"], 1)

            last_chunk, ropes = None, []
            for n, (kind, chunk, c0, idx) in enumerate(plan):
                slot = ring.chunks[chunk][0]
                w = W[:, slot, :].rearrange("p (k n) -> p k n", k=KT)
                if chunk != last_chunk:
                    pe.wait_ge(*ring.arrived(chunk))
                    last_chunk = chunk
                if n >= 4:
                    pe.wait_ge(*taken(n - 4))
                bank = ps[n % 4]
                for k in range(KT):
                    st = dict(start=(k == 0), stop=(k == KT - 1))
                    if kind == "sv":
                        t0, nt = TILES[idx]
                        mm = nc.tensor.matmul(bank[0:nt, 0:512], m.hT[:, k, t0:t0 + nt], w[:, k, :], **st)
                    elif kind == "bai":
                        t0, nt = TILES[idx]
                        mm = nc.tensor.matmul(bank[0:nt, 0:16], m.hT[:, k, t0:t0 + nt], w[:, k, 0:16], **st)
                    else:
                        mm = nc.tensor.matmul(bank[:, 0:T], w[:, k, c0:c0 + P], m.hT[:, k, :], **st)
                mm.then_inc(S["proj"], 1)
                if n + 1 == len(plan) or plan[n + 1][1] != chunk:
                    nc.tensor.drain().then_inc(ring.used, 1)
                if ropes:
                    rope_mm(ropes.pop())
                if kind == "rope":
                    ropes.append(idx)

        @block.scalar
        def _(act):
            convs, ropes, seen = [], [], 0

            def silu(i):
                act.wait_ge(S["conv"], i + 1)
                nc.scalar.activation(m.qkvT[:, i, :], m.conv_out[:, i % 2, :], ACT.Silu).then_inc(S["conv_silu"], 1)

            def rope_evac(r):
                act.wait_ge(S["rope_mm"], r + 1)
                nc.scalar.activation(rope_dst[r], ps[4 + r % 2][:, 0:T], ACT.Copy).then_inc(S["rope_out"], 1)

            for n, (kind, chunk, c0, idx) in enumerate(plan):
                if kind in ("conv", "z", "sv"):
                    act.wait_ge(S["proj"], n + 1)
                    src = ps[n % 4]
                    if kind == "conv":
                        if idx >= 3:
                            act.wait_ge(S["conv"], idx - 2)
                        nc.scalar.activation(m.xpad[:, idx % 3, 3:3 + T], src[:, 0:T], ACT.Copy).then_inc(S["proj_by_act"], 1)
                        convs.append(idx)
                    elif kind == "z":
                        nc.scalar.activation(m.zT[:, idx, :], src[:, 0:T], ACT.Silu).then_inc(S["proj_by_act"], 1)
                    else:
                        nt = TILES[idx][1]
                        nc.scalar.activation(m.sv[0:nt, idx, :], src[0:nt, 0:512], ACT.Copy).then_inc(S["proj_by_act"], 1)
                if len(convs) > 1 or (convs and kind != "conv"):
                    silu(convs.pop(0))
                if ropes:
                    rope_evac(ropes.pop())
                if kind == "rope":
                    ropes.append(idx)
            assert not convs and not ropes

        @block.vector
        def _(dve):
            dve.wait_ge(S["params_turned"], 1)
            nc.vector.tensor_copy(m.prmT[:, 0:81], ps[7][:, 0:81])
            dve.drain()
            for n, (kind, chunk, c0, idx) in enumerate(plan):
                if kind == "conv":
                    dve.wait_ge(S["proj_by_act"], idx + 1)
                    if idx >= 2:
                        dve.wait_ge(S["conv_silu"], idx - 1)
                    y = m.conv_out[:, idx % 2, :]
                    for j in range(4):
                        x = m.xpad[:, idx % 3, j:j + T]
                        wj = m.prmT[:, 12 * j + idx:12 * j + idx + 1]
                        if j == 0:
                            i = nc.vector.tensor_scalar(y, x, wj, None, ALU.mult)
                        else:
                            i = nc.vector.scalar_tensor_tensor(y, x, wj, y, ALU.mult, ALU.add)
                        if j < 3:
                            dve.drain()
                    i.then_inc(S["conv"], 1)
                elif kind == "rope":
                    dve.wait_ge(S["proj"], n + 1)
                    if idx >= 2:
                        dve.wait_ge(S["rope_mm"], idx - 1)
                    src = ps[n % 4][:, 0:T]
                    nc.vector.tensor_tensor(m.rope_tmp[:, idx % 2, 0, :], src, m.sin[:, :], ALU.mult)
                    i = nc.vector.tensor_tensor(m.rope_tmp[:, idx % 2, 1, :], src, m.cos[:, :], ALU.mult)
                    i.then_inc(S["rope_in"], 1)
                    dve.drain().then_inc(S["proj_by_dve"], 1)
                elif kind == "bai":
                    dve.wait_ge(S["proj"], n + 1)
                    nt = TILES[idx][1]
                    nc.vector.tensor_copy(m.bai[0:nt, idx, :], ps[n % 4][0:nt, 0:16]).then_inc(S["proj_by_dve"], 1)


def delta_rule(nc, m, l, A, S):
    ps = m.ps
    H = 4
    q4, k4, v4 = m.qkvT[:, 0:4, :], m.qkvT[:, 4:8, :], m.qkvT[:, 8:12, :]
    with ExitStack() as ctx:
        def sb(name, shape):
            return ctx.enter_context(nc.sbuf_tensor(name, shape, F32))

        sq = sb("d_sq", [P, 8, T])
        beta = sb("d_beta", [P, 3, H])
        gate = sb("d_gate", [P, 3, H])
        gt = sb("d_gt", [P, 5, 3, H])
        gc = sb("d_gc", [P, H])
        gcum = sb("d_gcum", [P, H, P])
        dif = sb("d_dif", [P, H, P])
        egc = sb("d_egc", [P, 4, H])
        eGB = sb("d_eGB", [P, H, P])
        kbg = sb("d_kbg", [P, H, P])
        vb = sb("d_vb", [P, H, P])
        kdec = sb("d_kdec", [P, H, P])
        qd = sb("d_qd", [P, H, P])
        Lm = sb("d_L", [P, H, P])
        Am = sb("d_A", [P, H, P])
        AT = sb("d_AT", [P, H, P])
        LT = sb("d_LT", [P, H, P])
        LM = sb("d_LM", [P, 2, H, P])
        X = sb("d_X", [P, H, P])
        Y = sb("d_Y", [P, H, P])
        Pm = sb("d_P", [P, H, P])
        wT = sb("d_wT", [P, H, P])
        u = sb("d_u", [P, H, P])
        vn = sb("d_vn", [P, H, P])
        St = sb("d_S", [P, H, P])
        oT = sb("d_oT", [P, H, T])

        def b4(ps_, n, w=P):
            return ps_[0:n, 0:H * P].rearrange("p (h c) -> p h c", h=H)[:, :, 0:w]

        def over_cols(ap, n, w):
            return ap.unsqueeze(2).to_broadcast([n, H, w])

        def over_heads(ap, n, w):
            return ap.unsqueeze(1).to_broadcast([n, H, w])

        def levels(nt):
            return nt.bit_length() - 1

        lev_base = [0]
        for _, nt in TILES:
            lev_base.append(lev_base[-1] + levels(nt) - 1)

        with nc.Block() as block:
            @block.tensor
            def _(pe):
                for j in range(8):
                    pe.wait_ge(S["d_squares"], j + 1)
                    if j >= 4:
                        pe.wait_ge(S["d_ln"], j - 3)
                    nc.tensor.matmul(ps[j % 4][:, 0:T], m.ones[:, :], sq[:, j, :], start=True, stop=True).then_inc(S["d_norms"], 1)
                for c, (t0, n) in enumerate(TILES):
                    pe.wait_ge(S["d_gcum"], c + 1)
                    nc.tensor.matmul(ps[4][0:n, 0:H], m.cum[0:n, 0:n], gate[0:n, c, :], start=True, stop=True)
                    nc.tensor.matmul(ps[5][:, :], m.ones[0:n, :], gcum[0:n, :, :], start=True, stop=True).then_inc(S["d_gc"], 1)
                    pe.wait_ge(S["d_normed"], 1)
                    for h in range(H):
                        nc.tensor.transpose(ps[0][0:n, h * P:(h + 1) * P], k4[:, h, t0:t0 + n], m.ident[:, :])
                    for h in range(H):
                        mm = nc.tensor.transpose(ps[1][0:n, h * P:(h + 1) * P], v4[:, h, t0:t0 + n], m.ident[:, :])
                    mm.then_inc(S["d_kv"], 1)
                    for h in range(H):
                        nc.tensor.matmul(ps[2][0:n, h * P:h * P + n], k4[:, h, t0:t0 + n], k4[:, h, t0:t0 + n], start=True, stop=True)
                    for h in range(H):
                        mm = nc.tensor.matmul(ps[3][0:n, h * P:h * P + n], q4[:, h, t0:t0 + n], k4[:, h, t0:t0 + n], start=True, stop=True)
                    mm.then_inc(S["d_kk"], 1)
                    pe.wait_ge(S["d_LA"], c + 1)
                    for h in range(H):
                        nc.tensor.transpose(ps[4][0:n, h * P:h * P + n], Lm[0:n, h, 0:n], m.ident[0:n, 0:n])
                    for h in range(H):
                        mm = nc.tensor.transpose(ps[5][0:n, h * P:h * P + n], Am[0:n, h, 0:n], m.ident[0:n, 0:n])
                    mm.then_inc(S["d_LAT"], 1)
                    for v in range(1, levels(n)):
                        q = lev_base[c] + v - 1
                        last = v == levels(n) - 1
                        pe.wait_ge(S["d_XY"], q + 1 + c)
                        for h in range(H):
                            mm = nc.tensor.matmul(ps[2][0:n, h * P:h * P + n], LM[0:n, v % 2, h, 0:n], X[0:n, h, 0:n], start=True, stop=True)
                        mm.then_inc(S["d_LX"], 1)
                        pe.wait_ge(S["d_P"], q + 1)
                        for h in range(H):
                            mm = nc.tensor.matmul(ps[4][0:n, h * P:h * P + n], Pm[0:n, h, 0:n], Y[0:n, h, 0:n], start=True, stop=True)
                        mm.then_inc(S["d_PY"], 1)
                        if not last:
                            for h in range(H):
                                mm = nc.tensor.matmul(ps[3][0:n, h * P:h * P + n], Y[0:n, h, 0:n], Pm[0:n, h, 0:n], start=True, stop=True)
                            mm.then_inc(S["d_YP"], 1)
                    pe.wait_ge(S["d_XY"], lev_base[c + 1] + c + 1)
                    for h in range(H):
                        nc.tensor.matmul(ps[6][:, h * P:h * P + n], kbg[0:n, h, :], Y[0:n, h, 0:n], start=True, stop=True)
                    for h in range(H):
                        mm = nc.tensor.matmul(ps[7][0:n, h * P:(h + 1) * P], Y[0:n, h, 0:n], vb[0:n, h, :], start=True, stop=True)
                    mm.then_inc(S["d_wu"], 1)
                    pe.wait_ge(S["d_wu_sb"], c + 1)
                    for h in range(H):
                        mm = nc.tensor.matmul(ps[2][0:n, h * P:(h + 1) * P], wT[:, h, 0:n], St[:, h, :], start=True, stop=True)
                    mm.then_inc(S["d_wS"], 1)
                    pe.wait_ge(S["d_vnew"], c + 1)
                    for h in range(H):
                        nc.tensor.matmul(ps[3][:, h * P:h * P + n], St[:, h, :], qd[:, h, 0:n], start=True, stop=False)
                        nc.tensor.matmul(ps[3][:, h * P:h * P + n], vn[0:n, h, :], AT[0:n, h, 0:n], start=False, stop=True)
                    for h in range(H):
                        mm = nc.tensor.matmul(ps[4][:, h * P:(h + 1) * P], kdec[0:n, h, :], vn[0:n, h, :], start=True, stop=True)
                    mm.then_inc(S["d_oS"], 1)
                    pe.wait_ge(S["d_state"], c + 1)
                for h in range(H):
                    pe.wait_ge(S["d_osq"], h + 1)
                    nc.tensor.matmul(ps[h][:, 0:T], m.ones[:, :], sq[:, h, :], start=True, stop=True).then_inc(S["d_onorm"], 1)

            @block.scalar
            def _(act):
                for j in range(8):
                    nc.scalar.activation(sq[:, j, :], m.qkvT[:, j, :], ACT.Square).then_inc(S["d_squares"], 1)
                act.wait_ge(S["d_gin"], 1)
                nc.scalar.activation(gt[:, 0, :, :], m.bai[:, :, 0:4], ACT.Exp, scale=-1.0)
                nc.scalar.activation(gt[:, 1, 0, :], m.rows[:, 0:4], ACT.Exp)
                nc.scalar.activation(gt[:, 3, :, :], gt[:, 3, :, :], ACT.Exp, scale=-1.0)
                act.drain()
                nc.scalar.activation(gt[:, 3, :, :], gt[:, 3, :, :], ACT.Ln, bias=1.0).then_inc(S["d_gexp"], 1)
                for j in range(8):
                    act.wait_ge(S["d_norms"], j + 1)
                    nc.scalar.activation(sq[:, j, :], ps[j % 4][:, 0:T], ACT.Ln, bias=m.eps6[:, 0:1]).then_inc(S["d_ln"], 1)
                act.drain()
                nc.scalar.activation(sq[:, :, :], sq[:, :, :], ACT.Exp, scale=-0.5).then_inc(S["d_rnorm"], 1)
                for c, (t0, n) in enumerate(TILES):
                    act.wait_ge(S["d_dif"], c + 1)
                    nc.scalar.activation(dif[0:n, :, 0:n], dif[0:n, :, 0:n], ACT.Exp)
                    nc.scalar.activation(eGB[:, :, :], ps[5][:, :].rearrange("p (h c) -> p h c", h=H), ACT.Exp)
                    nc.scalar.activation(egc[0:n, 0, :], gc[0:n, :], ACT.Exp)
                    nc.scalar.activation(egc[0:n, 1, :], egc[0:n, 3, :], ACT.Exp)
                    act.drain().then_inc(S["d_decay"], 1)
                    act.wait_ge(S["d_wu"], c + 1)
                    nc.scalar.activation(wT[:, :, 0:n], b4(ps[6], P, n), ACT.Copy)
                    act.drain().then_inc(S["d_wT_sb"], 1)
                act.wait_ge(S["d_o"], 1)
                for h in range(H):
                    nc.scalar.activation(sq[:, h, :], oT[:, h, :], ACT.Square).then_inc(S["d_osq"], 1)
                for h in range(H):
                    act.wait_ge(S["d_onorm"], h + 1)
                    nc.scalar.activation(sq[:, 4 + h, :], ps[h][:, 0:T], ACT.Ln, bias=m.eps6[:, 0:1], scale=1.0 / P)
                act.drain()
                nc.scalar.activation(sq[:, 4:8, :], sq[:, 4:8, :], ACT.Exp, scale=-0.5).then_inc(S["d_ornorm"], 1)

            @block.vector
            def _(dve):
                dve.wait_ge(S["rows_loaded"], 16 * 6)
                a = m.bai[:, :, 4:8]
                nc.vector.tensor_tensor(gt[:, 2, :, :], a, m.rows[:, 4:8].unsqueeze(1).to_broadcast([P, 3, H]), ALU.add)
                nc.vector.memset(St[:, :, :], 0.0)
                nc.vector.tensor_scalar(m.bai[:, :, 0:4], m.bai[:, :, 0:4], -80.0, None, ALU.max)
                dve.drain()
                nc.vector.tensor_scalar(gt[:, 4, :, :], gt[:, 2, :, :], -1.0, None, ALU.mult)
                dve.drain()
                nc.vector.tensor_tensor(gt[:, 3, :, :], gt[:, 2, :, :], gt[:, 4, :, :], ALU.max)
                dve.drain().then_inc(S["d_gin"], 1)
                dve.wait_ge(S["d_gexp"], 1)
                nc.vector.tensor_scalar(gt[:, 0, :, :], gt[:, 0, :, :], 1.0, None, ALU.add)
                nc.vector.scalar_tensor_tensor(gt[:, 2, :, :], gt[:, 2, :, :], 0.0, gt[:, 3, :, :], ALU.max, ALU.add)
                dve.drain()
                nc.vector.reciprocal(beta[:, :, :], gt[:, 0, :, :])
                nc.vector.scalar_tensor_tensor(gate[:, :, :], gt[:, 2, :, :], -1.0,
                                               gt[:, 1, 0:1, :].to_broadcast([P, 3, H]), ALU.mult, ALU.mult)
                dve.drain()
                dve.wait_ge(S["d_rnorm"], 1)
                nc.vector.scalar_tensor_tensor(q4, q4, float(P) ** -0.5, sq[:, 0:4, :], ALU.mult, ALU.mult)
                nc.vector.tensor_tensor(k4, k4, sq[:, 4:8, :], ALU.mult)
                dve.drain().then_inc(S["d_normed"], 1)
                for c, (t0, n) in enumerate(TILES):
                    nc.vector.tensor_tensor(gcum[0:n, :, :], over_heads(m.cum[0:n, :], n, P), over_cols(gate[0:n, c, :], n, P), ALU.mult)
                    dve.drain().then_inc(S["d_gcum"], 1)
                    dve.wait_ge(S["d_gc"], c + 1)
                    GB = ps[5][:, :].rearrange("p (h c) -> p h c", h=H)
                    nc.vector.tensor_copy(gc[0:n, :], ps[4][0:n, 0:H])
                    dve.drain()
                    nc.vector.tensor_tensor(dif[0:n, :, 0:n], over_cols(gc[0:n, :], n, n), GB[0:n, :, 0:n], ALU.subtract)
                    nc.vector.tensor_tensor(egc[0:n, 3, :].unsqueeze(2), GB[0:n, :, n - 1:n], gc[0:n, :].unsqueeze(2), ALU.subtract)
                    dve.drain()
                    nc.vector.tensor_scalar(dif[0:n, :, 0:n], dif[0:n, :, 0:n], 0.0, None, ALU.min)
                    dve.drain().then_inc(S["d_dif"], 1)
                    dve.wait_ge(S["d_decay"], c + 1)
                    nc.vector.tensor_tensor(egc[0:n, 2, :], egc[0:n, 0, :], beta[0:n, c, :], ALU.mult)
                    nc.vector.tensor_tensor(qd[:, :, 0:n], q4[:, :, t0:t0 + n], eGB[:, :, 0:n], ALU.mult)
                    dve.drain()
                    dve.wait_ge(S["d_kv"], c + 1)
                    nc.vector.tensor_tensor(kbg[0:n, :, :], b4(ps[0], n), over_cols(egc[0:n, 2, :], n, P), ALU.mult)
                    nc.vector.tensor_tensor(kdec[0:n, :, :], b4(ps[0], n), over_cols(egc[0:n, 1, :], n, P), ALU.mult)
                    nc.vector.tensor_tensor(vb[0:n, :, :], b4(ps[1], n), over_cols(beta[0:n, c, :], n, P), ALU.mult)
                    dve.wait_ge(S["d_kk"], c + 1)
                    nc.vector.tensor_tensor(Lm[0:n, :, 0:n], b4(ps[2], n, n), dif[0:n, :, 0:n], ALU.mult)
                    nc.vector.tensor_tensor(Am[0:n, :, 0:n], b4(ps[3], n, n), dif[0:n, :, 0:n], ALU.mult)
                    dve.drain()
                    nc.vector.tensor_tensor(Lm[0:n, :, 0:n], Lm[0:n, :, 0:n], over_heads(m.strict[0:n, 0:n], n, n), ALU.mult)
                    nc.vector.tensor_tensor(Am[0:n, :, 0:n], Am[0:n, :, 0:n], over_heads(m.incl[0:n, 0:n], n, n), ALU.mult)
                    dve.drain()
                    nc.vector.tensor_tensor(Lm[0:n, :, 0:n], Lm[0:n, :, 0:n], over_cols(beta[0:n, c, :], n, n), ALU.mult)
                    dve.drain().then_inc(S["d_LA"], 1)
                    idn = over_heads(m.ident[0:n, 0:n], n, n)
                    nc.vector.tensor_tensor(X[0:n, :, 0:n], Lm[0:n, :, 0:n], over_heads(m.level0[0:n, 0:n], n, n), ALU.mult)
                    dve.drain()
                    nc.vector.tensor_tensor(X[0:n, :, 0:n], idn, X[0:n, :, 0:n], ALU.subtract)
                    dve.wait_ge(S["d_LAT"], c + 1)
                    nc.vector.tensor_copy(LT[0:n, :, 0:n], b4(ps[4], n, n))
                    nc.vector.tensor_copy(AT[0:n, :, 0:n], b4(ps[5], n, n))
                    dve.drain()
                    nc.vector.tensor_tensor(Y[0:n, :, 0:n], LT[0:n, :, 0:n], over_heads(m.levelsT[0:n, 0, 0:n], n, n), ALU.mult)
                    nc.vector.tensor_tensor(LM[0:n, 1, :, 0:n], LT[0:n, :, 0:n], over_heads(m.levelsT[0:n, 1, 0:n], n, n), ALU.mult)
                    dve.drain()
                    nc.vector.tensor_tensor(Y[0:n, :, 0:n], idn, Y[0:n, :, 0:n], ALU.subtract)
                    dve.drain().then_inc(S["d_XY"], 1)
                    for v in range(1, levels(n)):
                        q = lev_base[c] + v - 1
                        last = v == levels(n) - 1
                        dve.wait_ge(S["d_LX"], q + 1)
                        nc.vector.tensor_copy(Pm[0:n, :, 0:n], b4(ps[2], n, n))
                        dve.drain().then_inc(S["d_P"], 1)
                        if not last:
                            nc.vector.tensor_tensor(LM[0:n, (v + 1) % 2, :, 0:n], LT[0:n, :, 0:n], over_heads(m.levelsT[0:n, v + 1, 0:n], n, n), ALU.mult)
                        dve.wait_ge(S["d_PY"], q + 1)
                        if not last:
                            dve.wait_ge(S["d_YP"], q - c + 1)
                            nc.vector.tensor_tensor(X[0:n, :, 0:n], X[0:n, :, 0:n], b4(ps[3], n, n), ALU.subtract)
                        nc.vector.tensor_tensor(Y[0:n, :, 0:n], Y[0:n, :, 0:n], b4(ps[4], n, n), ALU.subtract)
                        dve.drain().then_inc(S["d_XY"], 1)
                    dve.wait_ge(S["d_wu"], c + 1)
                    nc.vector.tensor_copy(u[0:n, :, :], b4(ps[7], n))
                    dve.drain()
                    dve.wait_ge(S["d_wT_sb"], c + 1)
                    dve.drain().then_inc(S["d_wu_sb"], 1)
                    dve.wait_ge(S["d_wS"], c + 1)
                    nc.vector.tensor_tensor(vn[0:n, :, :], u[0:n, :, :], b4(ps[2], n), ALU.subtract)
                    dve.drain().then_inc(S["d_vnew"], 1)
                    dve.wait_ge(S["d_oS"], c + 1)
                    nc.vector.tensor_copy(oT[:, :, t0:t0 + n], b4(ps[3], P, n))
                    nc.vector.tensor_tensor(St[:, :, :], St[:, :, :], eGB[:, :, n - 1:n].to_broadcast([P, H, P]), ALU.mult)
                    dve.drain()
                    nc.vector.tensor_tensor(St[:, :, :], St[:, :, :], b4(ps[4], P), ALU.add)
                    dve.drain().then_inc(S["d_state"], 1)
                nc.vector.tensor_scalar(m.zT[:, :, :], m.zT[:, :, :], m.prmT[:, 48:49], None, ALU.mult)
                dve.drain().then_inc(S["d_o"], 1)
                dve.wait_ge(S["d_ornorm"], 1)
                nc.vector.tensor_tensor(oT[:, :, :], oT[:, :, :], sq[:, 4:8, :], ALU.mult)
                dve.drain()
                nc.vector.tensor_tensor(m.mixT[:, 0:4, :], oT[:, :, :], m.zT[:, :, :], ALU.mult)


def sparse_attention(nc, m, l, A, S):
    ps = m.ps
    NH = 8
    with ExitStack() as ctx:
        def sb(name, shape):
            return ctx.enter_context(nc.sbuf_tensor(name, shape, F32))

        rel = sb("s_rel", [P, 2, T])
        score = sb("s_score", [P, T])
        work = sb("s_work", [P, T])
        top = sb("s_top", [P, 8])
        keep = sb("s_keep", [P, T])
        bias = sb("s_bias", [P, T])
        lg = sb("s_lg", [P, NH, T])
        mx = sb("s_mx", [P, NH])
        den = sb("s_den", [P, NH])
        pT = sb("s_pT", [P, 2, 3, P])

        def half(h):
            return slice(64 * (h % 2), 64 * (h % 2) + 64)

        with nc.Block() as block:
            @block.tensor
            def _(pe):
                for c, (t0, n) in enumerate(TILES):
                    ns = t0 + n
                    for h in range(NH):
                        q = c * NH + h
                        if q >= 2:
                            pe.wait_ge(S["s_rel"], q - 1)
                        nc.tensor.matmul(ps[h % 2][0:n, 0:ns], m.iqT[half(h), h // 2, t0:t0 + n], m.ikT[half(h), 0:ns],
                                         start=True, stop=True).then_inc(S["s_idx"], 1)
                    for h in range(NH):
                        q = c * NH + h
                        if q >= 2:
                            pe.wait_ge(S["s_logit_sb"], q - 1)
                        nc.tensor.matmul(ps[2 + h % 2][0:n, 0:ns], m.sqT[half(h), h // 2, t0:t0 + n], m.skT[half(h), h // 2, 0:ns],
                                         start=True, stop=True).then_inc(S["s_logit"], 1)
                    pe.wait_ge(S["s_prob"], c + 1)
                    for h in range(NH):
                        q = c * NH + h
                        if q >= 2:
                            pe.wait_ge(S["s_pT_sb"], q - 1)
                        for j in range(c + 1):
                            s0, w = TILES[j]
                            mm = nc.tensor.transpose(ps[4 + h % 2][0:w, j * P:j * P + n], lg[0:n, h, s0:s0 + w], m.ident[0:n, 0:n])
                        mm.then_inc(S["s_pT"], 1)
                        pe.wait_ge(S["s_pT_sb"], q + 1)
                        if h % 2 == 0 and q >= 4:
                            pe.wait_ge(S["s_out"], q // 2 - 1)
                        for j in range(c + 1):
                            s0, w = TILES[j]
                            mm = nc.tensor.matmul(ps[6 + h // 2 % 2][half(h), 0:n], m.sv[0:w, j, h * 64:(h + 1) * 64],
                                                  pT[0:w, h % 2, j, 0:n], start=(j == 0), stop=(j == c))
                        mm.then_inc(S["s_pv"], 1)

            @block.scalar
            def _(act):
                for c, (t0, n) in enumerate(TILES):
                    ns = t0 + n
                    for h in range(NH):
                        q = c * NH + h
                        act.wait_ge(S["s_idx"], q + 1)
                        if q >= 2:
                            act.wait_ge(S["s_acc"], q - 1)
                        nc.scalar.activation(rel[0:n, h % 2, 0:ns], ps[h % 2][0:n, 0:ns], ACT.Relu, scale=0.125).then_inc(S["s_rel"], 1)
                    act.wait_ge(S["s_max"], c + 1)
                    for h in range(NH):
                        nc.scalar.activation(lg[0:n, h, 0:ns], lg[0:n, h, 0:ns], ACT.Exp, bias=mx[0:n, h:h + 1],
                                             accum_out=den[0:n, h:h + 1])
                    act.drain().then_inc(S["s_exp"], 1)
                    for h in range(1, NH, 2):
                        q = c * NH + h
                        act.wait_ge(S["s_pv"], q + 1)
                        nc.scalar.activation(m.mixT[:, 4 + h // 2, t0:t0 + n], ps[6 + h // 2 % 2][:, 0:n], ACT.Copy).then_inc(S["s_out"], 1)

            @block.vector
            def _(dve):
                for c, (t0, n) in enumerate(TILES):
                    ns = t0 + n
                    caus = m.causal[0:n, c, 0:ns]
                    for h in range(NH):
                        q = c * NH + h
                        dve.wait_ge(S["s_rel"], q + 1)
                        wi = m.bai[0:n, c, 8 + h:9 + h]
                        if h == 0:
                            nc.vector.tensor_scalar(score[0:n, 0:ns], rel[0:n, 0, 0:ns], wi, None, ALU.mult)
                        else:
                            nc.vector.scalar_tensor_tensor(score[0:n, 0:ns], rel[0:n, h % 2, 0:ns], wi, score[0:n, 0:ns], ALU.mult, ALU.add)
                        dve.drain().then_inc(S["s_acc"], 1)
                    nc.vector.tensor_scalar(bias[0:n, 0:ns], caus, -1.0, BIG, ALU.add, ALU.mult)
                    nc.vector.tensor_tensor(score[0:n, 0:ns], score[0:n, 0:ns], caus, ALU.mult)
                    dve.drain()
                    nc.vector.tensor_tensor(work[0:n, 0:ns], score[0:n, 0:ns], bias[0:n, 0:ns], ALU.add)
                    dve.drain()
                    for r in range(TOP_K // 8):
                        nc.vector.max(top[0:n, :], work[0:n, 0:ns])
                        dve.drain()
                        nc.vector.match_replace(work[0:n, 0:ns], top[0:n, :], work[0:n, 0:ns], -3 * BIG)
                        dve.drain()
                    nc.vector.scalar_tensor_tensor(keep[0:n, 0:ns], work[0:n, 0:ns], -2 * BIG, caus, ALU.is_lt, ALU.mult)
                    dve.drain()
                    nc.vector.tensor_scalar(bias[0:n, 0:ns], keep[0:n, 0:ns], -1.0, BIG, ALU.add, ALU.mult)
                    dve.drain()
                    if c:
                        dve.wait_ge(S["s_pT"], c * NH)
                    for h in range(NH):
                        q = c * NH + h
                        dve.wait_ge(S["s_logit"], q + 1)
                        nc.vector.scalar_tensor_tensor(lg[0:n, h, 0:ns], ps[2 + h % 2][0:n, 0:ns], 0.125, bias[0:n, 0:ns], ALU.mult, ALU.add).then_inc(S["s_logit_sb"], 1)
                    dve.drain()
                    nc.vector.tensor_reduce(mx[0:n, :], lg[0:n, :, 0:ns], AX.X, ALU.max)
                    dve.drain()
                    nc.vector.tensor_scalar(mx[0:n, :], mx[0:n, :], -1.0, None, ALU.mult)
                    dve.drain().then_inc(S["s_max"], 1)
                    dve.wait_ge(S["s_exp"], c + 1)
                    nc.vector.reciprocal(den[0:n, :], den[0:n, :])
                    dve.drain()
                    nc.vector.tensor_tensor(lg[0:n, :, 0:ns], lg[0:n, :, 0:ns], den[0:n, :].unsqueeze(2).to_broadcast([n, NH, ns]), ALU.mult)
                    dve.drain().then_inc(S["s_prob"], 1)
                    for h in range(NH):
                        q = c * NH + h
                        dve.wait_ge(S["s_pT"], q + 1)
                        if q >= 2:
                            dve.wait_ge(S["s_pv"], q - 1)
                        for j in range(c + 1):
                            w = TILES[j][1]
                            i = nc.vector.tensor_copy(pT[0:w, h % 2, j, 0:n], ps[4 + h % 2][0:w, j * P:j * P + n])
                        i.then_inc(S["s_pT_sb"], 1)


def layer_norm_steps(nc, m, signals, g0, b0):
    ready, mean, squares, var, rstd = signals
    centred, scratch = m.ln_x, m.ln_sq

    def on_tensor(pe):
        pe.wait_ge(ready, 1)
        for k in range(KT):
            mm = nc.tensor.matmul(m.ps[0][:, 0:T], m.mean_w[:, :], m.hT[:, k, :], start=(k == 0), stop=(k == KT - 1))
        mm.then_inc(mean, 1)
        for k in range(KT):
            pe.wait_ge(squares, k + 1)
            mm = nc.tensor.matmul(m.ps[1][:, 0:T], m.mean_w[:, :], scratch[:, k, :], start=(k == 0), stop=(k == KT - 1))
        mm.then_inc(var, 1)

    def on_scalar(act, centred_ready):
        for k in range(KT):
            act.wait_ge(centred_ready, k + 1)
            nc.scalar.activation(scratch[:, k, :], centred[:, k, :], ACT.Square).then_inc(squares, 1)
        act.wait_ge(var, 1)
        nc.scalar.activation(m.rstd[:, :], m.ps[1][:, 0:T], ACT.Ln, bias=m.eps5[:, 0:1])
        act.drain()
        nc.scalar.activation(m.rstd[:, :], m.rstd[:, :], ACT.Exp, scale=-0.5).then_inc(rstd, 1)

    def on_vector(dve, centred_ready):
        dve.wait_ge(mean, 1)
        for k in range(KT):
            nc.vector.tensor_tensor(centred[:, k, :], m.hT[:, k, :], m.ps[0][:, 0:T], ALU.subtract).then_inc(centred_ready, 1)
        dve.wait_ge(rstd, 1)
        for k in range(KT):
            nc.vector.scalar_tensor_tensor(centred[:, k, :], centred[:, k, :], m.prmT[:, g0 + k:g0 + k + 1], m.rstd[:, :], ALU.mult, ALU.mult)
        dve.drain()
        for k in range(KT):
            nc.vector.tensor_scalar(m.hT[:, k, :], centred[:, k, :], m.prmT[:, b0 + k:b0 + k + 1], None, ALU.add)

    return on_tensor, on_scalar, on_vector


def mix_and_route(nc, m, l, A, S):
    W, ring, ps = m.W, m.ring, m.ps
    w_out = A["w_out"].rearrange("l (k p) n -> l p k n", p=P)
    w1 = A["w1"].rearrange("l e (k p) f -> l e p k f", p=P)
    w3 = A["w3"].rearrange("l e (k p) f -> l e p k f", p=P)
    w2 = A["w2"].rearrange("l e (k p) d -> l e p k d", p=P)
    with ExitStack() as ctx:
        def sb(name, shape):
            return ctx.enter_context(nc.sbuf_tensor(name, shape, F32))

        m.ln_x = sb("ln_x", [P, KT, T])
        m.ln_sq = sb("ln_sq", [P, KT, T])
        m.rstd = sb("ln_rstd", [P, T])
        r = sb("r_tmp", [P, 12, 32])
        comb = sb("r_comb", [P, 3, 32])
        on_pe, on_act, on_dve = layer_norm_steps(nc, m, (S["n1_ready"], S["n1_mean"], S["n1_squares"], S["n1_var"], S["n1_rstd"]), 49, 57)

        with nc.Block() as block:
            @block.sync
            def _(sp):
                for c in range(2):
                    name = f"out{c}"
                    sp.wait_ge(*ring.freed(name))
                    slot = ring.chunks[name][0]
                    w = W[:, slot, :].rearrange("p (k n) -> p k n", k=KT)
                    sp.dma_start(w, w_out[l, :, :, 512 * c:512 * c + 512]).then_inc(ring.loaded[slot], 16)
                for e in range(2):
                    load_expert(nc, sp, m, l, e, e, w1, w3, w2, wait=True)

            @block.tensor
            def _(pe):
                for n in range(KT):
                    c = n // 4
                    if n % 4 == 0:
                        pe.wait_ge(*ring.arrived(f"out{c}"))
                    if n >= 4:
                        pe.wait_ge(S["o_added"], n - 3)
                    w = W[:, ring.chunks[f"out{c}"][0], :].rearrange("p (k n) -> p k n", k=KT)
                    for k in range(KT):
                        mm = nc.tensor.matmul(ps[n % 4][:, 0:T], w[:, k, n % 4 * P:n % 4 * P + P], m.mixT[:, k, :], start=(k == 0), stop=(k == KT - 1))
                    mm.then_inc(S["o_mm"], 1)
                    if n % 4 == 3:
                        nc.tensor.drain().then_inc(ring.used, 1)
                on_pe(pe)
                pe.wait_ge(S["n1_done"], 1)
                for c, (t0, n) in enumerate(TILES):
                    for k in range(KT):
                        mm = nc.tensor.matmul(ps[2 + c][0:n, 0:36], m.hT[:, k, t0:t0 + n], m.w_route[:, k, :], start=(k == 0), stop=(k == KT - 1))
                    mm.then_inc(S["r_logit"], 1)
                pe.wait_ge(S["r_comb"], 1)
                for c, (t0, n) in enumerate(TILES):
                    mm = nc.tensor.transpose(ps[5][0:32, t0:t0 + n], comb[0:n, c, :], m.ident[0:n, 0:n])
                mm.then_inc(S["r_combT"], 1)

            @block.scalar
            def _(act):
                on_act(act, S["n1_centred"])
                for c, (t0, n) in enumerate(TILES):
                    act.wait_ge(S["r_exp_in"], c + 1)
                    nc.scalar.activation(r[0:n, 3, 0:4], r[0:n, 0, 0:4], ACT.Exp, bias=r[0:n, 2, 0:1], accum_out=r[0:n, 2, 1:2])
                    nc.scalar.activation(r[0:n, 2, 4:5], r[0:n, 2, 3:4], ACT.Exp)
                    act.drain().then_inc(S["r_exp"], 1)

            @block.vector
            def _(dve):
                for n in range(KT):
                    dve.wait_ge(S["o_mm"], n + 1)
                    nc.vector.scalar_tensor_tensor(m.hT[:, n, :], m.hT[:, n, :], ALPHA, ps[n % 4][:, 0:T], ALU.mult, ALU.add).then_inc(S["o_added"], 1)
                dve.drain().then_inc(S["n1_ready"], 1)
                on_dve(dve, S["n1_centred"])
                dve.drain().then_inc(S["n1_done"], 1)
                nc.vector.tensor_scalar(m.yT[:, :, :], m.hT[:, :, :], ALPHA, None, ALU.mult)
                for c, (t0, n) in enumerate(TILES):
                    dve.wait_ge(S["r_logit"], c + 1)
                    lg, col = r[0:n, 0, :], r[0:n, 2, :]
                    el = r[0:n, 1, :]
                    nc.vector.tensor_tensor(lg[:, 0:4], ps[2 + c][0:n, 0:4], m.rows[0:n, 8:12], ALU.add)
                    nc.vector.tensor_tensor(el, ps[2 + c][0:n, 4:36], m.rows[0:n, 12:44], ALU.add)
                    dve.drain()
                    nc.vector.tensor_reduce(col[:, 8:9], lg[:, 0:4], AX.X, ALU.max)
                    dve.drain()
                    nc.vector.scalar_tensor_tensor(r[0:n, 4, 0:4], lg[:, 0:4], col[:, 8:9], m.rank4[0:n, :], ALU.is_equal, ALU.mult)
                    nc.vector.tensor_scalar(col[:, 0:1], col[:, 8:9], -1.0, None, ALU.mult)
                    dve.drain()
                    nc.vector.tensor_reduce(col[:, 9:10], r[0:n, 4, 0:4], AX.X, ALU.max)
                    dve.drain()
                    nc.vector.tensor_scalar(r[0:n, 5, 0:4], r[0:n, 4, 0:4], col[:, 9:10], None, ALU.is_equal)
                    dve.drain()
                    e48 = el.rearrange("p (g e) -> p g e", g=4)
                    g48 = r[0:n, 5, 0:4].unsqueeze(2).to_broadcast([n, 4, 8])
                    nc.vector.tensor_tensor(r[0:n, 6, :].rearrange("p (g e) -> p g e", g=4), e48, g48, ALU.mult)
                    dve.drain()
                    nc.vector.tensor_reduce(r[0:n, 7, 0:8], r[0:n, 6, :].rearrange("p (g e) -> p e g", g=4), AX.X, ALU.add)
                    dve.drain()
                    for s in range(2):
                        x = r[0:n, 7, 8 * s:8 * s + 8]
                        nc.vector.tensor_reduce(col[:, 10 + s:11 + s], x, AX.X, ALU.max)
                        dve.drain()
                        nc.vector.scalar_tensor_tensor(r[0:n, 8, 0:8], x, col[:, 10 + s:11 + s], m.rank8[0:n, :], ALU.is_equal, ALU.mult)
                        dve.drain()
                        nc.vector.tensor_reduce(col[:, 12:13], r[0:n, 8, 0:8], AX.X, ALU.max)
                        dve.drain()
                        nc.vector.tensor_scalar(r[0:n, 9, 8 * s:8 * s + 8], r[0:n, 8, 0:8], col[:, 12:13], None, ALU.is_equal)
                        dve.drain()
                        if s == 0:
                            nc.vector.scalar_tensor_tensor(r[0:n, 7, 8:16], r[0:n, 9, 0:8], -BIG, x, ALU.mult, ALU.add)
                            dve.drain()
                    nc.vector.tensor_tensor(col[:, 3:4], col[:, 11:12], col[:, 10:11], ALU.subtract)
                    dve.drain().then_inc(S["r_exp_in"], 1)
                    dve.wait_ge(S["r_exp"], c + 1)
                    nc.vector.scalar_tensor_tensor(col[:, 13:14], col[:, 4:5], 1.0, col[:, 1:2], ALU.add, ALU.mult)
                    dve.drain()
                    nc.vector.reciprocal(col[:, 14:15], col[:, 13:14])
                    dve.drain()
                    nc.vector.tensor_tensor(col[:, 15:16], col[:, 14:15], col[:, 4:5], ALU.mult)
                    nc.vector.tensor_scalar(r[0:n, 10, 0:8], r[0:n, 9, 0:8], col[:, 14:15], None, ALU.mult)
                    dve.drain()
                    nc.vector.scalar_tensor_tensor(r[0:n, 10, 0:8], r[0:n, 9, 8:16], col[:, 15:16], r[0:n, 10, 0:8], ALU.mult, ALU.add)
                    dve.drain()
                    nc.vector.tensor_tensor(comb[0:n, c, :].rearrange("p (g e) -> p g e", g=4),
                                            r[0:n, 10, 0:8].unsqueeze(1).to_broadcast([n, 4, 8]), g48, ALU.mult)
                    dve.drain()
                dve.drain().then_inc(S["r_comb"], 1)
                dve.wait_ge(S["r_combT"], 1)
                nc.vector.tensor_copy(m.combT[:, :], ps[5][0:32, 0:T])


def load_expert(nc, sp, m, l, e, half, w1, w3, w2, wait=False):
    a, b = 2 * half, 2 * half + 1
    W, ring = m.W, m.ring
    wa = W[:, a, :].rearrange("p (x k f) -> p x k f", x=2, k=KT)
    wb = W[:, b, 0:2 * D].rearrange("p (k d) -> p k d", k=2)
    if wait:
        sp.wait_ge(*ring.freed(f"up{half}"))
    sp.dma_start(wa[:, 0, :, :], w1[l, e, :, :, :]).then_inc(ring.loaded[a], 16)
    sp.dma_start(wa[:, 1, :, :], w3[l, e, :, :, :]).then_inc(ring.loaded[a], 16)
    if wait:
        sp.wait_ge(*ring.freed(f"down{half}"))
    sp.dma_start(wb[:, :, :], w2[l, e, :, :, :]).then_inc(ring.loaded[b], 16)


def experts(nc, m, l, A, S):
    W, ring, ps = m.W, m.ring, m.ps
    w1 = A["w1"].rearrange("l e (k p) f -> l e p k f", p=P)
    w3 = A["w3"].rearrange("l e (k p) f -> l e p k f", p=P)
    w2 = A["w2"].rearrange("l e (k p) d -> l e p k d", p=P)
    PAIRS = EXPERTS // 2
    first_up = [ring.arrived(f"up{h}") for h in range(2)]
    first_down = [ring.arrived(f"down{h}") for h in range(2)]
    used0 = m.used_before_experts
    with ExitStack() as ctx:
        def sb(name, shape):
            return ctx.enter_context(nc.sbuf_tensor(name, shape, F32))

        hid = sb("e_hid", [P, 2, 2, T])
        sil = sb("e_sil", [P, 2, T])
        gm = sb("e_gm", [32, 2, T])
        m.ln_x = sb("ln2_x", [P, KT, T])
        m.ln_sq = sb("ln2_sq", [P, KT, T])
        m.rstd = sb("ln2_rstd", [P, T])
        on_pe, on_act, on_dve = layer_norm_steps(nc, m, (S["n2_ready"], S["n2_mean"], S["n2_squares"], S["n2_var"], S["n2_rstd"]), 65, 73)

        with nc.Block() as block:
            @block.sync
            def _(sp):
                with sp.Fori(0, PAIRS - 1) as it:
                    for h in range(2):
                        sp.wait_ge(ring.used, it * 4 + (used0 + 2 * h + 2))
                        load_expert(nc, sp, m, l, it * 2 + (2 + h), h, w1, w3, w2)

            @block.tensor
            def _(pe):
                def up(it, x, f):
                    wa = W[:, 2 * x, :].rearrange("p (y k f) -> p y k f", y=2, k=KT)
                    pe.wait_ge(S["e_hid_free"], it * 4 + (2 * x + f + 1))
                    for y in range(2):
                        for k in range(KT):
                            mm = nc.tensor.matmul(ps[2 * f + y][:, 0:T], wa[:, y, k, f * P:(f + 1) * P], m.hT[:, k, :], start=(k == 0), stop=(k == KT - 1))
                    mm.then_inc(S["e_up"], 1)

                def down(it, x):
                    pe.wait_ge(S["e_hid"], it * 4 + (2 * x + 2))
                    pe.wait_ge(ring.loaded[2 * x + 1], it * 16 + first_down[x][1])
                    wb = W[:, 2 * x + 1, 0:2 * D].rearrange("p (k d) -> p k d", k=2)
                    for d in range(KT):
                        pe.wait_ge(S["e_y_free"], it * 16 + (8 * x + d + 1))
                        for k in range(2):
                            mm = nc.tensor.matmul(ps[4 + (8 * x + d) % 2][:, 0:T], wb[:, k, d * P:(d + 1) * P], hid[:, x, k, :], start=(k == 0), stop=(k == 1))
                        mm.then_inc(S["e_y"], 1)
                    nc.tensor.drain().then_inc(ring.used, 1)

                def gates(it, x):
                    pe.wait_ge(S["e_gm"], it * 2 + (x + 1))
                    nc.tensor.matmul(ps[6 + x][:, 0:T], m.ones[0:32, :], gm[:, x, :], start=True, stop=True).then_inc(S["e_gate"], 1)

                with pe.Fori(0, PAIRS) as it:
                    for x in range(2):
                        gates(it, x)
                        pe.wait_ge(ring.loaded[2 * x], it * 32 + first_up[x][1])
                        up(it, x, 0)
                        if x == 1:
                            down(it, 0)
                        up(it, x, 1)
                        nc.tensor.drain().then_inc(ring.used, 1)
                    down(it, 1)
                on_pe(pe)

            @block.scalar
            def _(act):
                with act.Fori(0, PAIRS) as it:
                    for x in range(2):
                        for f in range(2):
                            act.wait_ge(S["e_up"], it * 4 + (2 * x + f + 1))
                            act.wait_ge(S["e_sil_free"], it * 4 + (2 * x + f + 1))
                            nc.scalar.activation(sil[:, f, :], ps[2 * f][:, 0:T], ACT.Silu).then_inc(S["e_sil"], 1)
                on_act(act, S["n2_centred"])

            @block.vector
            def _(dve):
                dve.drain().then_inc(S["e_hid_free"], 2)
                dve.drain().then_inc(S["e_sil_free"], 2)
                dve.drain().then_inc(S["e_y_free"], 2)

                def gate_row(it, x):
                    nc.vector.tensor_scalar(gm[:, x, :], m.combT[:, :], m.ident[0:32, bass.ds(it * 2 + x, 1)], None, ALU.mult)
                    dve.drain().then_inc(S["e_gm"], 1)

                def hidden(it, x, f):
                    dve.wait_ge(S["e_sil"], it * 4 + (2 * x + f + 1))
                    nc.vector.tensor_tensor(hid[:, x, f, :], sil[:, f, :], ps[2 * f + 1][:, 0:T], ALU.mult)
                    dve.drain().then_inc(S["e_sil_free"], 1)
                    dve.drain().then_inc(S["e_hid_free"], 1)
                    if f == 0:
                        dve.wait_ge(S["e_gate"], it * 2 + (x + 1))
                    nc.vector.tensor_tensor(hid[:, x, f, :], hid[:, x, f, :], ps[6 + x][:, 0:T], ALU.mult)
                    dve.drain().then_inc(S["e_hid"], 1)

                def add_y(it, x):
                    for d in range(KT):
                        dve.wait_ge(S["e_y"], it * 16 + (8 * x + d + 1))
                        nc.vector.tensor_tensor(m.yT[:, d, :], m.yT[:, d, :], ps[4 + (8 * x + d) % 2][:, 0:T], ALU.add).then_inc(S["e_y_free"], 1)

                with dve.Fori(0, PAIRS) as it:
                    gate_row(it, 0)
                    gate_row(it, 1)
                    hidden(it, 0, 0)
                    hidden(it, 0, 1)
                    hidden(it, 1, 0)
                    add_y(it, 0)
                    hidden(it, 1, 1)
                    add_y(it, 1)
                    dve.drain()
                nc.vector.tensor_copy(m.hT[:, :, :], m.yT[:, :, :])
                dve.drain().then_inc(S["n2_ready"], 1)
                on_dve(dve, S["n2_centred"])


SEMS1 = """params_loaded params_turned rows_loaded proj proj_by_act proj_by_dve rope_in rope_mm rope_out conv conv_silu
d_squares d_norms d_ln d_rnorm d_normed d_gin d_gexp d_gcum d_gc d_dif d_decay d_kv d_kk d_LA d_LAT d_XY d_LX d_P d_PY d_YP
d_wu d_wT_sb d_wu_sb d_wS d_vnew d_oS d_state d_o d_osq d_onorm d_ornorm
s_idx s_rel s_acc s_logit s_logit_sb s_max s_exp s_prob s_pT s_pT_sb s_pv s_out
o_mm o_added n1_ready n1_centred n1_mean n1_squares n1_var n1_rstd n1_done r_logit r_exp_in r_exp r_comb r_combT
e_up e_sil e_sil_free e_hid e_hid_free e_gm e_gate e_y e_y_free n2_ready n2_centred n2_mean n2_squares n2_var n2_rstd""".split()


def clear(nc, signals, ring):
    for s in signals + list(ring.loaded) + [ring.used]:
        nc.sync.sem_clear(s)
    nc.all_engine_barrier()


def first_block(nc, ps, xT, A, x, meta):
    with ExitStack() as ctx:
        def sb(name, shape):
            return ctx.enter_context(nc.sbuf_tensor(name, shape, F32))

        def sem(name):
            return ctx.enter_context(nc.semaphore(name))

        C = constants()
        start = sem("start")
        m = Buffers()
        m.ps, m.xT = ps, xT
        K = load_constants(nc, ctx, C)
        m.ident, m.ones, m.mean_w, m.cum = K["ident"], K["ones"], K["mean_w"], K["cum"]
        m.strict, m.incl, m.level0, m.levelsT = K["strict"], K["incl"], K["level0"], K["levelsT"]
        m.causal, m.rot, m.cos, m.sin = K["causal"], K["rot"], K["cos"], K["sin"]
        m.rank4, m.rank8 = K["rank4"], K["rank8"]
        m.W = sb("W", [P, SLOTS, SLOT])
        m.prm = sb("prm", [P, P])
        m.prmT = sb("prmT", [P, 96])
        m.rows = sb("rows", [P, 44])
        m.eps5 = sb("eps5", [P, 1])
        m.eps6 = sb("eps6", [P, 1])
        m.hT = sb("hT", [P, KT, T])
        m.yT = sb("yT", [P, KT, T])
        m.w_route = sb("w_route", [P, KT, 36])
        m.combT = sb("combT", [32, T])

        turned, copied = sem("turned"), sem("copied")
        with nc.sbuf_tensor("x_tok", [P, 3, D], F32) as xt, nc.Block() as block:
            @block.sync
            def _(sp):
                sp.dma_start(xt[0:16, 0, :], meta[:, :]).then_inc(start, 16)
                sp.dma_start(xt[16:128, 0, :], x[0, 0:112, :]).then_inc(start, 16)
                sp.dma_start(xt[:, 1, :], x[0, 112:240, :]).then_inc(start, 16)
                sp.dma_start(xt[0:16, 2, :], x[0, 240:256, :]).then_inc(start, 16)

            @block.tensor
            def _(pe):
                pe.wait_ge(start, 64)
                for k in range(KT):
                    if k >= 4:
                        pe.wait_ge(copied, k - 3)
                    for c, (t0, n) in enumerate(TILES):
                        mm = nc.tensor.transpose(m.ps[k % 4][:, t0:t0 + n], xt[0:n, c, k * P:(k + 1) * P], m.ident[0:n, 0:n])
                    mm.then_inc(turned, 1)

            @block.vector
            def _(dve):
                nc.vector.memset(m.eps5[:, :], 1e-5)
                nc.vector.memset(m.eps6[:, :], 1e-6)
                for k in range(KT):
                    dve.wait_ge(turned, k + 1)
                    nc.vector.tensor_copy(m.hT[:, k, :], m.ps[k % 4][:, 0:T]).then_inc(copied, 1)

        ring = m.ring = WeightRing([sem(f"loaded{i}") for i in range(SLOTS)], sem("used"))
        for c in range(8):
            ring.add(f"in{c}", c % 4)
        ring.add("in8", 0, dmas=4)
        ring.add("out0", 1)
        ring.add("out1", 2)
        m.used_before_experts = ring.n
        ring.add("up0", 0, dmas=2)
        ring.add("up1", 2, dmas=2)
        ring.add("down0", 1)
        ring.add("down1", 3)
        signals = {name: sem(name) for name in SEMS1}
        S = signals
        with nc.Fori(0, DEPTH) as l:
            with ExitStack() as lay:
                def lsb(name, shape):
                    return lay.enter_context(nc.sbuf_tensor(name, shape, F32))

                m.qkvT = lsb("qkvT", [P, 12, T])
                m.zT = lsb("zT", [P, 4, T])
                m.bai = lsb("bai", [P, 3, 16])
                m.sqT = lsb("sqT", [P, 4, T])
                m.skT = lsb("skT", [P, 4, T])
                m.iqT = lsb("iqT", [P, 4, T])
                m.ikT = lsb("ikT", [P, T])
                m.sv = lsb("sv", [P, 3, 512])
                m.mixT = lsb("mixT", [P, 8, T])
                with nc.sbuf_tensor("xpad", [P, 3, 3 + T], F32) as m.xpad, nc.sbuf_tensor("conv_out", [P, 2, T], F32) as m.conv_out, \
                        nc.sbuf_tensor("rope_tmp", [P, 2, 2, T], F32) as m.rope_tmp:
                    nc.vector.memset(m.xpad[:, :, 0:3], 0.0)
                    nc.vector.memset(m.bai[:, :, :], 0.0)
                    nc.vector.drain()
                    projections(nc, m, l, A, S)
                delta_rule(nc, m, l, A, S)
                sparse_attention(nc, m, l, A, S)
                mix_and_route(nc, m, l, A, S)
            experts(nc, m, l, A, S)
            clear(nc, list(signals.values()), ring)
        nc.vector.tensor_copy(m.xT[:, :, :], m.hT[:, :, N_META:T])
        nc.all_engine_barrier()


NAMES1 = "w_in conv_w a_log dt_bias dn_norm_g w_out ln1_g ln1_b w_grp b_grp w_rtr b_rtr w1 w3 w2 ln2_g ln2_b".split()





S2 = SEQ
N_CMP = (SEQ - 32) // 16 + 1
HIDDEN = 4 * D
IN2 = dict(q=0, kc=512, vc=640, ks=768, vs=896, kw=1024, vw=1152, g=1280, gq=1304, gk=1560, gv=1816, gr=2328,
           glow=2840, mq=2856, merge=3368)


def constants2():
    i = np.arange(P)
    c = {"ident": np.eye(P), "mean_w": np.full((P, P), 1.0 / D), "mean128": np.full((P, P), 1.0 / P)}
    c["mean64"] = (i[:, None] // 64 == i[None, :] // 64) / 64.0
    rot = np.zeros((P, P))
    for h in (0, 64):
        for d in range(8):
            rot[h + d + 8, h + d] = -1.0
            rot[h + d, h + d + 8] = 1.0
    c["rot"] = rot
    t = np.arange(S2)
    qpos = np.stack([i, i + P], 1)
    c["causal_bias"] = np.where(t[None, None, :] <= qpos[:, :, None], 0.0, -BIG)
    ends = np.arange(N_CMP) * 16 + 31
    c["cmp_mask"] = ends[None, None, :] <= qpos[:, :, None]
    c["cmp_bias"] = np.where(c["cmp_mask"], 0.0, -BIG)
    inv = np.power(np.float32(500000.0), -np.arange(8, dtype=np.float32) / np.float32(8)).astype(np.float32)
    c["inv_freq"] = np.where(i % 64 < 16, inv[i % 8], 0.0)[:, None]
    sums = np.zeros((P, 9, P))
    for lv in range(7):
        mid = ((i >> (lv + 1)) << (lv + 1)) + (1 << lv)
        up = i >= mid
        u = i[:, None]
        sums[:, lv, :] = np.where(up[None, :], (u >= mid[None, :]) & (u <= i[None, :]), (u > i[None, :]) & (u < mid[None, :]))
    sums[:, 7, :] = i[:, None] > i[None, :]
    sums[:, 8, :] = i[:, None] <= i[None, :]
    c["sums"] = sums
    pairs = np.zeros((P, 8, P))
    for lv in range(7):
        pairs[:, lv, :] = ((i[None, :] >> lv) == (i[:, None] >> lv) + 1) & ((i[None, :] >> lv) % 2 == 1)
    pairs[:, 7, :] = np.eye(P)
    c["pairs"] = pairs * 64 ** -0.5
    return {k: np.ascontiguousarray(v, np.float32) for k, v in c.items()}


def rms_steps(nc, m, signals, g0):
    sq, ms, rstd, done = signals

    def on_scalar(act):
        for k in range(KT):
            nc.scalar.activation(m.hT[:, k, :], m.xT[:, k, :], ACT.Square).then_inc(sq, 1)
        act.wait_ge(ms, 1)
        nc.scalar.activation(m.rstd[:, :], m.ps[7][:, 0:S2], ACT.Ln, bias=m.eps6[:, 0:1])
        act.drain()
        nc.scalar.activation(m.rstd[:, :], m.rstd[:, :], ACT.Exp, scale=-0.5)
        act.drain().then_inc(rstd, 1)

    def on_tensor(pe):
        for k in range(KT):
            pe.wait_ge(sq, k + 1)
            mm = nc.tensor.matmul(m.ps[7][:, 0:S2], m.mean_w[:, :], m.hT[:, k, :], start=(k == 0), stop=(k == KT - 1))
        mm.then_inc(ms, 1)

    def on_vector(dve):
        dve.wait_ge(rstd, 1)
        for k in range(KT):
            i = nc.vector.scalar_tensor_tensor(m.hT[:, k, :], m.xT[:, k, :], m.prmT[:, g0 + k:g0 + k + 1], m.rstd[:, :], ALU.mult, ALU.mult)
            i.then_inc(done, 1)

    return on_scalar, on_tensor, on_vector


class Loads:

    def __init__(self, ring, items):
        self.ring, self.items, self.at = ring, items, 0

    def upto(self, sp, name):
        while True:
            n, dmas = self.items[self.at]
            free = self.ring.freed(n)
            if free:
                sp.wait_ge(*free)
            slot = self.ring.chunks[n][0]
            for dst, src in dmas:
                sp.dma_start(dst, src).then_inc(self.ring.loaded[slot], 16)
            self.at += 1
            if n == name:
                return


def weights2(nc, m, l, A, ring):
    W = m.W
    w_in = A["w_in_2"].rearrange("l (k p) n -> l p k n", p=P)
    w_kv = A["mem_w_kv_2"].rearrange("l (k p) n -> l p k n", p=P)
    w_out = A["w_out_2"].rearrange("l (k p) n -> l p k n", p=P)
    w_up = A["w_up_2"].rearrange("l (k p) n -> l p k n", p=P)
    w_down = A["w_down_2"].rearrange("l (c k p) n -> l c p k n", p=P, k=4)
    cmp1 = A["cmp_w1_2"].rearrange("l x (k p) e -> l x p k e", p=P)
    br0 = A["w_branch_2"].rearrange("l b (a t d) n -> l b a d t n", a=2, t=4)
    br = A["w_branch_2"].rearrange("l b (k p) n -> l b p k n", p=P)
    used, loads, slot_of = [], {}, {}

    def view(slot, k):
        return W[:, slot, :].rearrange("p (k n) -> p k n", k=k)

    def add(name, slot, dmas):
        ring.add(name, slot, dmas=len(dmas))
        loads[name] = dmas

    s = 0

    def plain(name, c0, n=512, extra=()):
        nonlocal s
        w = view(s % 4, KT)
        dmas = [(w[:, :, 0:n], w_in[l, :, :, c0:c0 + n])]
        dmas += [(w[:, :, a:a + k], w_in[l, :, :, b:b + k]) for a, b, k in extra]
        add(name, s % 4, dmas)
        s += 1

    wq = W[:, 0, :].rearrange("p (k t a d) -> p k t a d", k=KT, t=4, a=2)
    src = A["w_in_2"].rearrange("l (k p) n -> l p k n", p=P)[l, :, :, 0:512].rearrange("p k (a t d) -> p k t a d", a=2, t=4)
    add("q", 0, [(wq[:, :, t, a, :], src[:, :, t, a, :]) for t in range(4) for a in range(2)])
    s += 1
    plain("nkv", 512)
    plain("nkw", 1024, 280, [(280, IN2["glow"], 16)])
    plain("gqk", IN2["gq"])
    plain("gv", IN2["gv"])
    plain("gr", IN2["gr"])
    plain("mq", IN2["mq"])
    for x in range(2):
        add(f"cmp{x}", s % 4, [(view(s % 4, 16), cmp1[l, x, :, :, :])])
        s += 1
    for x in range(2):
        add(f"kv{x}", s % 4, [(view(s % 4, KT), w_kv[l, :, :, 512 * x:512 * x + 512])])
        s += 1
    order = list(loads)
    for b in range(3):
        plain(f"mg{2 * b}", IN2["merge"] + 1024 * b)
        plain(f"mg{2 * b + 1}", IN2["merge"] + 1024 * b + 512)
        w = view(s % 4, 4)
        if b == 0:
            add("br0", s % 4, [(w[0:64, :, :], br0[l, 0, 0, :, :, :]), (w[64:128, :, :], br0[l, 0, 1, :, :, :])])
        else:
            add(f"br{b}", s % 4, [(w, br[l, b, :, :, :])])
        s += 1
        order += [f"mg{2 * b}", f"br{b}", f"mg{2 * b + 1}"]
    for c in range(2):
        add(f"wo{c}", s % 4, [(view(s % 4, KT), w_out[l, :, :, 512 * c:512 * c + 512])])
        order.append(f"wo{c}")
        s += 1
    m.used_before_mlp = ring.n
    m.mlp_slots = []
    for c in range(2):
        m.mlp_slots.append((s % 4, (s + 1) % 4))
        add(f"mu{c}", s % 4, [(view(s % 4, KT), w_up[l, :, :, 512 * c:512 * c + 512])])
        add(f"md{c}", (s + 1) % 4, [(view((s + 1) % 4, 4), w_down[l, c, :, :, :])])
        order += [f"mu{c}", f"md{c}"]
        s += 2
    return Loads(ring, [(n, loads[n]) for n in order])


def project2(nc, m, l, A, S, loads):
    ring, ps, W = m.ring, m.ps, m.W
    plan = [("q", True, ("pair", j), m.raw[:, j, :]) for j in range(4)]
    plan += [("nkv", True, (0, P), m.kcv[:, 0, :]), ("nkv", True, (P, P), m.kcv[:, 1, :]), ("nkv", True, (2 * P, P), m.raw[:, 4, :])]
    plan += [("nkv", False, (3 * P, P), m.vs[:, j, :]) for j in range(2)]
    plan += [("nkw", True, (0, P), m.raw[:, 5, :])]
    plan += [("nkw", False, (P, P), m.vw[:, j, :]) for j in range(2)]
    plan += [("nkw", False, (256, 24), m.ngate[:, j, :]) for j in range(2)]
    plan += [("nkw", True, (280, 16), m.glow[:, :])]
    plan += [("gqk", True, (P * j, P), m.gqk[:, j, :]) for j in range(4)]
    plan += [("gv", False, (0, 512), m.gv[:, j, :]) for j in range(2)]
    plan += [("gr", True, (P * j, P), m.gr[:, j, :]) for j in range(4)]
    plan += [("mq", True, (P * j, P), m.raw[:, 6 + j, :]) for j in range(4)]
    tok = {i: sum(1 for p in plan[:i] if p[0] == plan[i][0] and not p[1] and p[2] == plan[i][2]) for i in range(len(plan)) if not plan[i][1]}
    on_act, on_pe, on_dve = rms_steps(nc, m, (S["p_sq"], S["p_ms"], S["p_rstd"], S["p_done"]), 0)

    def shape(i):
        _, fm, (a, w), _ = plan[i]
        w = P if a == "pair" else w
        return (w, S2) if fm else (P, w)

    with nc.Block() as block:
        @block.sync
        def _(sp):
            pr = m.prm

            def v(name, c=P):
                return A[name].rearrange("l (t f) -> l t f", f=c)[l]

            kn = A["nsa_k_norm_2"]
            for r0, n, ap in [(0, 8, v("ln_mix_2")), (8, 24, A["b_merge_2"].rearrange("l b (t f) -> l (b t) f", f=P)[l]),
                              (32, 8, v("mem_norm_2")), (40, 8, v("ln_mlp_2")), (48, 1, v("gla_norm_2")),
                              (49, 1, v("mem_q_norm_2")), (50, 1, v("mem_k_norm_2")),
                              (55, 32, A["cmp_pe_2"].rearrange("l x (k a) d -> l (x k) (a d)", a=2)[l])]:
                sp.dma_start(pr[r0:r0 + n, :], ap).then_inc(S["params_loaded"], 16)
            for a in (0, 64):
                sp.dma_start(pr[51:52, a:a + 64], v("nsa_q_norm_2", 64)).then_inc(S["params_loaded"], 16)
                sp.dma_start(pr[52:55, a:a + 64], kn[l, :, :]).then_inc(S["params_loaded"], 16)
            sp.dma_start(m.w_gate[:, :], A["gla_w_gate_2"][l, :, :]).then_inc(S["small_loaded"], 16)
            sp.dma_start(m.b_gate[:, :], A["gla_b_gate_2"].rearrange("l (a n) -> l a n", a=1)[l]).then_inc(S["small_loaded"], 16)
            sp.dma_start(m.w_cmp2[:, :, :, :], A["cmp_w2_2"].rearrange("l x (k p) d -> l p x k d", p=P)[l]).then_inc(S["small_loaded"], 16)
            loads.upto(sp, "kv1")

        @block.tensor
        def _(pe):
            pe.wait_ge(S["params_loaded"], 16 * 12)
            nc.tensor.transpose(ps[6][:, 0:87], m.prm[0:87, :], m.ident[0:87, 0:87]).then_inc(S["params_turned"], 1)
            on_pe(pe)
            pe.wait_ge(S["p_done"], KT)
            for i, (chunk, fm, (a, w), _) in enumerate(plan):
                wv = W[:, ring.chunks[chunk][0], :].rearrange("p (k n) -> p k n", k=KT)
                if i == 0 or plan[i - 1][0] != chunk:
                    pe.wait_ge(*ring.arrived(chunk))
                if i >= 6:
                    pe.wait_ge(S["p_dve"] if i % 2 == 0 else S["p_act"], (i - 6) // 2 + 1)
                rows, cols = shape(i)
                o = ps[i % 6][0:rows, 0:cols]
                for k in range(KT):
                    st = dict(start=(k == 0), stop=(k == KT - 1))
                    if a == "pair":
                        mm = nc.tensor.matmul(o, wv[:, k, w * P:(w + 1) * P], m.hT[:, k, :], **st)
                    elif fm:
                        mm = nc.tensor.matmul(o, wv[:, k, a:a + w], m.hT[:, k, :], **st)
                    else:
                        t0 = P * tok[i]
                        mm = nc.tensor.matmul(o, m.hT[:, k, t0:t0 + P], wv[:, k, a:a + w], **st)
                mm.then_inc(S["p_mm"], 1)
                if i + 1 == len(plan) or plan[i + 1][0] != chunk:
                    nc.tensor.drain().then_inc(ring.used, 1)

        @block.scalar
        def _(act):
            on_act(act)
            for i in range(1, len(plan), 2):
                act.wait_ge(S["p_mm"], i + 1)
                rows, cols = shape(i)
                nc.scalar.activation(plan[i][3], ps[i % 6][0:rows, 0:cols], ACT.Copy).then_inc(S["p_act"], 1)

        @block.vector
        def _(dve):
            dve.wait_ge(S["params_turned"], 1)
            nc.vector.tensor_copy(m.prmT[:, 0:87], ps[6][:, 0:87])
            dve.drain()
            on_dve(dve)
            for i in range(0, len(plan), 2):
                dve.wait_ge(S["p_mm"], i + 1)
                rows, cols = shape(i)
                nc.vector.tensor_copy(plan[i][3], ps[i % 6][0:rows, 0:cols]).then_inc(S["p_dve"], 1)


def heads2(nc, m, l, A, S, loads):
    ring, ps, W = m.ring, m.ps, m.W
    with ExitStack() as ctx:
        def sb(name, shape):
            return ctx.enter_context(nc.sbuf_tensor(name, shape, F32))

        rs = sb("h_rs", [P, 10, S2])
        xs = sb("h_xs", [P, 2, 6, S2])
        kk = sb("h_kk", [P, 2, 2, S2])
        win = sb("h_win", [P, 2, 16, 2 * N_CMP])
        hid = sb("h_hid", [2 * N_CMP, 2, 256])
        gl = sb("h_gl", [2 * N_CMP, 2, 256])
        hidT = sb("h_hidT", [P, 2, 2, 2 * N_CMP])
        kq = sb("h_kq", [P, 5, N_CMP])
        NC2 = 2 * N_CMP

        def cols(ap):
            return ap[:, 31:S2:16]

        with nc.Block() as block:
            @block.sync
            def _(sp):
                for lp in range(2):
                    for g in range(2):
                        sp.dma_start(kk[64 * lp:64 * lp + 64, :, g, 0:S2 - 1], m.kcv[64 * g:64 * g + 64, :, lp:lp + S2 - 1]).then_inc(S["h_kk"], 16)

            @block.tensor
            def _(pe):
                for j in range(5):
                    pe.wait_ge(S["h_sq"], 1)
                    mm = nc.tensor.matmul(ps[j][:, :], (m.mean64 if j < 3 else m.mean128)[:, :], rs[:, 2 * j:2 * j + 2, :], start=True, stop=True)
                mm.then_inc(S["h_ms"], 1)
                for x in range(2):
                    pe.wait_ge(*ring.arrived(f"cmp{x}"))
                    pe.wait_ge(S["h_win"], x + 1)
                    w = W[:, ring.chunks[f"cmp{x}"][0], :].rearrange("p (k n) -> p k n", k=16)
                    for k in range(16):
                        mm = nc.tensor.matmul(ps[5 + x][0:NC2, 0:256], win[:, x, k, :], w[:, k, :], start=(k == 0), stop=(k == 15))
                    mm.then_inc(S["h_hid"], 1)
                    nc.tensor.drain().then_inc(ring.used, 1)
                pe.wait_ge(S["h_xs"], 1)
                for j in range(3):
                    nc.tensor.matmul(ps[j][:, :], m.rot[:, :], xs[:, 0, 2 * j:2 * j + 2, :], start=True, stop=False)
                    mm = nc.tensor.matmul(ps[j][:, :], m.ident[:, :], xs[:, 1, 2 * j:2 * j + 2, :], start=False, stop=True)
                mm.then_inc(S["h_rope"], 1)
                pe.wait_ge(S["h_gelu"], 1)
                for x in range(2):
                    for e in range(2):
                        c0 = (2 * x + e) * 32
                        mm = nc.tensor.transpose(ps[7][:, c0:c0 + NC2], gl[:, x, e * P:(e + 1) * P], m.ident[0:NC2, 0:NC2])
                mm.then_inc(S["h_turn"], 1)
                pe.wait_ge(S["small_loaded"], 48)
                pe.wait_ge(S["h_hidT"], 1)
                for g in range(2):
                    for e in range(2):
                        nc.tensor.matmul(ps[3][64 * g:64 * g + 64, 0:N_CMP], m.w_cmp2[:, 0, e, :], hidT[:, 0, e, g * N_CMP:(g + 1) * N_CMP],
                                         start=(e == 0), stop=(e == 1))
                for g in range(2):
                    for e in range(2):
                        mm = nc.tensor.matmul(ps[4][0:N_CMP, 64 * g:64 * g + 64], hidT[:, 1, e, g * N_CMP:(g + 1) * N_CMP], m.w_cmp2[:, 1, e, :],
                                              start=(e == 0), stop=(e == 1))
                mm.then_inc(S["h_comp"], 1)
                pe.wait_ge(S["h_ksq"], 1)
                nc.tensor.matmul(ps[5][:, 0:N_CMP], m.mean64[:, :], kq[:, 1, :], start=True, stop=True).then_inc(S["h_kms"], 1)
                pe.wait_ge(S["h_kxs"], 1)
                nc.tensor.matmul(ps[6][:, 0:N_CMP], m.rot[:, :], kq[:, 3, :], start=True, stop=False)
                nc.tensor.matmul(ps[6][:, 0:N_CMP], m.ident[:, :], kq[:, 4, :], start=False, stop=True).then_inc(S["h_krope"], 1)

            @block.scalar
            def _(act):
                nc.scalar.activation(rs[:, :, :], m.raw[:, :, :], ACT.Square)
                act.drain().then_inc(S["h_sq"], 1)
                act.wait_ge(S["h_ms"], 1)
                for j in range(5):
                    nc.scalar.activation(rs[:, 2 * j:2 * j + 2, :], ps[j][:, :].rearrange("p (a t) -> p a t", a=2), ACT.Ln, bias=m.eps6[:, 0:1])
                act.drain()
                nc.scalar.activation(rs[:, :, :], rs[:, :, :], ACT.Exp, scale=-0.5)
                act.drain().then_inc(S["h_rs"], 1)
                act.wait_ge(S["h_gin"], 1)
                nc.scalar.activation(gl[:, :, :], gl[:, :, :], ACT.Exp, scale=-1.5957691216057308)
                act.drain().then_inc(S["h_gexp"], 1)
                act.wait_ge(S["h_rope"], 1)
                for j in range(3):
                    nc.scalar.activation(m.qk[:, 2 * j:2 * j + 2, :], ps[j][:, :].rearrange("p (a t) -> p a t", a=2), ACT.Copy)
                act.wait_ge(S["h_comp"], 1)
                nc.scalar.activation(kq[:, 0, :], ps[3][:, 0:N_CMP], ACT.Copy)
                nc.scalar.activation(kq[:, 1, :], ps[3][:, 0:N_CMP], ACT.Square)
                act.drain().then_inc(S["h_ksq"], 1)
                act.wait_ge(S["h_kms"], 1)
                nc.scalar.activation(kq[:, 2, :], ps[5][:, 0:N_CMP], ACT.Ln, bias=m.eps6[:, 0:1])
                act.drain()
                nc.scalar.activation(kq[:, 2, :], kq[:, 2, :], ACT.Exp, scale=-0.5)
                act.drain().then_inc(S["h_krs"], 1)
                act.wait_ge(S["h_krope"], 1)
                nc.scalar.activation(m.kcmp[:, :], ps[6][:, 0:N_CMP], ACT.Copy)

            @block.vector
            def _(dve):
                dve.wait_ge(S["h_kk"], 64)
                for x in range(2):
                    for g in range(2):
                        base = kk[:, x, g, 0:S2]
                        src = bass.AP(base.tensor, base.offset, [list(base.ap[0]), [2, 16], [16, N_CMP]])
                        pe_ = m.prmT[:, 55 + 16 * x:71 + 16 * x].unsqueeze(2).to_broadcast([P, 16, N_CMP])
                        nc.vector.tensor_tensor(win[:, x, :, g * N_CMP:(g + 1) * N_CMP], src, pe_, ALU.add)
                    dve.drain().then_inc(S["h_win"], 1)
                dve.wait_ge(S["h_rs"], 1)
                for j in range(10):
                    g = 51 if j < 4 else 49 if j >= 6 else 53 + j - 4
                    dst = m.raw[:, j, :]
                    nc.vector.scalar_tensor_tensor(dst, m.raw[:, j, :], m.prmT[:, g:g + 1], rs[:, j, :], ALU.mult, ALU.mult)
                dve.drain()
                for y, tab in ((0, m.sin), (1, m.cos)):
                    nc.vector.tensor_tensor(xs[:, y, :, :], m.raw[:, 0:6, :], tab[:, :].unsqueeze(1).to_broadcast([P, 6, S2]), ALU.mult)
                dve.drain().then_inc(S["h_xs"], 1)
                for x in range(2):
                    dve.wait_ge(S["h_hid"], x + 1)
                    nc.vector.tensor_copy(hid[:, x, :], ps[5 + x][0:NC2, 0:256])
                dve.drain()
                nc.vector.tensor_tensor(gl[:, :, :], hid[:, :, :], hid[:, :, :], ALU.mult)
                dve.drain()
                nc.vector.tensor_scalar(gl[:, :, :], gl[:, :, :], 0.044715, 1.0, ALU.mult, ALU.add)
                dve.drain()
                nc.vector.tensor_tensor(gl[:, :, :], gl[:, :, :], hid[:, :, :], ALU.mult)
                dve.drain()
                nc.vector.tensor_scalar(gl[:, :, :], gl[:, :, :], -50.0, None, ALU.max)
                dve.drain().then_inc(S["h_gin"], 1)
                dve.wait_ge(S["h_gexp"], 1)
                nc.vector.tensor_scalar(gl[:, :, :], gl[:, :, :], 1.0, None, ALU.add)
                dve.drain()
                nc.vector.reciprocal(gl[:, :, :], gl[:, :, :])
                dve.drain()
                nc.vector.tensor_tensor(gl[:, :, :], gl[:, :, :], hid[:, :, :], ALU.mult)
                dve.drain().then_inc(S["h_gelu"], 1)
                dve.wait_ge(S["h_turn"], 1)
                nc.vector.tensor_copy(hidT[:, :, :, :], ps[7][:, 0:128].rearrange("p (x e n) -> p x e n", x=2, e=2)[:, :, :, 0:NC2])
                dve.drain().then_inc(S["h_hidT"], 1)
                dve.wait_ge(S["h_comp"], 1)
                nc.vector.tensor_copy(m.vcmp[:, :], ps[4][0:N_CMP, 0:P])
                dve.wait_ge(S["h_krs"], 1)
                nc.vector.scalar_tensor_tensor(kq[:, 0, :], kq[:, 0, :], m.prmT[:, 52:53], kq[:, 2, :], ALU.mult, ALU.mult)
                dve.drain()
                nc.vector.tensor_tensor(kq[:, 3, :], kq[:, 0, :], cols(m.sin), ALU.mult)
                nc.vector.tensor_tensor(kq[:, 4, :], kq[:, 0, :], cols(m.cos), ALU.mult)
                dve.drain().then_inc(S["h_kxs"], 1)


def native_sparse(nc, m, l, A, S, loads):
    ps = m.ps
    with ExitStack() as ctx:
        def sb(name, shape):
            return ctx.enter_context(nc.sbuf_tensor(name, shape, F32))

        p = sb("n_p", [P, 4, 2, S2])
        pc = sb("n_pc", [P, 4, N_CMP])
        mx = sb("n_mx", [P, 4, 3])
        den = sb("n_den", [P, 4, 3])
        gt = sb("n_gt", [P, 2, 24])
        pT = sb("n_pT", [P, 2, 4, P])
        pcT = sb("n_pcT", [N_CMP, 4 * P])
        GROUP = [(c, g) for c in range(2) for g in range(2)]

        with nc.Block() as block:
            @block.tensor
            def _(pe):
                for u, (c, g) in enumerate(GROUP):
                    hs = slice(64 * g, 64 * g + 64)
                    ns = P * (c + 1)
                    if u:
                        pe.wait_ge(S["n_pT_sb"], 4 * u)
                    for r in range(4):
                        qh = m.qk[hs, r, c * P:(c + 1) * P]
                        nc.tensor.matmul(ps[r][:, 0:ns], qh, m.qk[hs, 4, 0:ns], start=True, stop=True)
                        nc.tensor.matmul(ps[r][:, S2:S2 + ns], qh, m.qk[hs, 5, 0:ns], start=True, stop=True)
                    for r in range(4):
                        mm = nc.tensor.matmul(ps[4][:, 16 * r:16 * r + N_CMP], m.qk[hs, r, c * P:(c + 1) * P], m.kcmp[hs, :], start=True, stop=True)
                    mm.then_inc(S["n_logit"], 1)
                    pe.wait_ge(S["n_prob"], u + 1)
                    for r in range(4):
                        mm = nc.tensor.transpose(ps[6][0:N_CMP, r * P:(r + 1) * P], pc[:, r, :], m.ident[:, :])
                    mm.then_inc(S["n_pcT"], 1)
                    for r in range(4):
                        q = 4 * u + r
                        if r >= 2:
                            pe.wait_ge(S["n_pT_sb"], q - 1)
                        for y in range(2):
                            for j in range(c + 1):
                                mm = nc.tensor.transpose(ps[4 + r % 2][:, (2 * y + j) * P:(2 * y + j + 1) * P], p[:, r, y, j * P:(j + 1) * P], m.ident[:, :])
                        mm.then_inc(S["n_pT"], 1)
                        pe.wait_ge(S["n_pT_sb"], q + 1)
                        if r == 0:
                            pe.wait_ge(S["n_pcT_sb"], u + 1)
                            if u:
                                pe.wait_ge(S["n_out"], u)
                        o = ps[7][hs, r * P:(r + 1) * P]
                        for y, v in ((0, m.vs), (1, m.vw)):
                            for j in range(c + 1):
                                nc.tensor.matmul(o, v[:, j, hs], pT[:, r % 2, 2 * y + j, :], start=(y == 0 and j == 0), stop=False)
                        nc.tensor.matmul(o, m.vcmp[:, hs], pcT[:, r * P:(r + 1) * P], start=False, stop=True).then_inc(S["n_pv"], 1)

            @block.scalar
            def _(act):
                act.wait_ge(S["n_gin"], 1)
                nc.scalar.activation(gt[:, :, :], m.ngate[:, :, :], ACT.Exp, scale=-1.0)
                act.drain().then_inc(S["n_gexp"], 1)
                for u, (c, g) in enumerate(GROUP):
                    ns = P * (c + 1)
                    act.wait_ge(S["n_max"], u + 1)
                    for r in range(4):
                        for y in range(2):
                            nc.scalar.activation(p[:, r, y, 0:ns], p[:, r, y, 0:ns], ACT.Exp, bias=mx[:, r, y:y + 1], scale=0.125,
                                                 accum_out=den[:, r, y:y + 1])
                        nc.scalar.activation(pc[:, r, :], pc[:, r, :], ACT.Exp, bias=mx[:, r, 2:3], scale=0.125)
                    act.drain().then_inc(S["n_exp"], 1)
                    act.wait_ge(S["n_pv"], 4 * u + 4)
                    hs = slice(64 * g, 64 * g + 64)
                    nc.scalar.activation(m.o_nsa[hs, :, c * P:(c + 1) * P], ps[7][hs, :].rearrange("p (r q) -> p r q", r=4), ACT.Copy).then_inc(S["n_out"], 1)

            @block.vector
            def _(dve):
                nc.vector.tensor_scalar(m.ngate[:, :, :], m.ngate[:, :, :], -80.0, None, ALU.max)
                dve.drain().then_inc(S["n_gin"], 1)
                dve.wait_ge(S["n_gexp"], 1)
                nc.vector.tensor_scalar(gt[:, :, :], gt[:, :, :], 1.0, None, ALU.add)
                dve.drain()
                nc.vector.reciprocal(gt[:, :, :], gt[:, :, :])
                dve.drain()
                for u, (c, g) in enumerate(GROUP):
                    ns = P * (c + 1)
                    dve.wait_ge(S["n_logit"], u + 1)
                    for r in range(4):
                        nc.vector.tensor_tensor(p[:, r, :, 0:ns], ps[r][:, :].rearrange("p (y s) -> p y s", y=2)[:, :, 0:ns],
                                                m.causal_bias[:, c, 0:ns].unsqueeze(1).to_broadcast([P, 2, ns]), ALU.add)
                    nc.vector.tensor_tensor(pc[:, :, :], ps[4][:, 0:64].rearrange("p (r n) -> p r n", r=4)[:, :, 0:N_CMP],
                                            m.cmp_mask[:, c, :].unsqueeze(1).to_broadcast([P, 4, N_CMP]), ALU.mult)
                    dve.drain()
                    nc.vector.tensor_tensor(pc[:, :, :], pc[:, :, :], m.cmp_bias[:, c, :].unsqueeze(1).to_broadcast([P, 4, N_CMP]), ALU.add)
                    nc.vector.tensor_reduce(mx[:, :, 0:2], p[:, :, :, 0:ns], AX.X, ALU.max)
                    dve.drain()
                    nc.vector.tensor_reduce(mx[:, :, 2:3], pc[:, :, :], AX.X, ALU.max)
                    dve.drain()
                    nc.vector.tensor_scalar(mx[:, :, :], mx[:, :, :], -0.125, None, ALU.mult)
                    dve.drain().then_inc(S["n_max"], 1)
                    dve.wait_ge(S["n_exp"], u + 1)
                    nc.vector.tensor_tensor(pc[:, :, :], pc[:, :, :], m.cmp_mask[:, c, :].unsqueeze(1).to_broadcast([P, 4, N_CMP]), ALU.mult)
                    dve.drain()
                    nc.vector.tensor_reduce(den[:, :, 2:3], pc[:, :, :], AX.X, ALU.add)
                    dve.drain()
                    nc.vector.tensor_scalar(den[:, :, 2:3], den[:, :, 2:3], 1e-30, None, ALU.max)
                    dve.drain()
                    nc.vector.reciprocal(den[:, :, :], den[:, :, :])
                    dve.drain()
                    gh = gt[:, c, 12 * g:12 * g + 12].rearrange("p (r b) -> p r b", b=3)
                    nc.vector.tensor_tensor(den[:, :, 0:2], den[:, :, 0:2], gh[:, :, 1:3], ALU.mult)
                    nc.vector.tensor_tensor(den[:, :, 2:3], den[:, :, 2:3], gh[:, :, 0:1], ALU.mult)
                    dve.drain()
                    nc.vector.tensor_tensor(pc[:, :, :], pc[:, :, :], den[:, :, 2:3].to_broadcast([P, 4, N_CMP]), ALU.mult)
                    for r in range(4):
                        nc.vector.tensor_tensor(p[:, r, :, 0:ns], p[:, r, :, 0:ns], den[:, r, 0:2].unsqueeze(2).to_broadcast([P, 2, ns]), ALU.mult)
                    dve.drain().then_inc(S["n_prob"], 1)
                    dve.wait_ge(S["n_pcT"], u + 1)
                    nc.vector.tensor_copy(pcT[:, :], ps[6][0:N_CMP, :])
                    dve.drain().then_inc(S["n_pcT_sb"], 1)
                    for r in range(4):
                        q = 4 * u + r
                        dve.wait_ge(S["n_pT"], q + 1)
                        if q >= 2:
                            dve.wait_ge(S["n_pv"], q - 1)
                        for y in range(2):
                            i = nc.vector.tensor_copy(pT[:, r % 2, 2 * y:2 * y + c + 1, :], ps[4 + r % 2][:, 2 * y * P:(2 * y + c + 1) * P].rearrange("p (j q) -> p j q", q=P))
                        i.then_inc(S["n_pT_sb"], 1)


def memory2(nc, m, l, A, S, loads):
    ring, ps, W = m.ring, m.ps, m.W
    with ExitStack() as ctx:
        def sb(name, shape):
            return ctx.enter_context(nc.sbuf_tensor(name, shape, F32))

        memn = sb("m_memn", [P, KT, S2])
        kT = sb("m_kT", [P, 4, S2])
        rs = sb("m_rs", [P, 4, S2])
        v = sb("m_v", [P, 2, 512])
        p = sb("m_p", [P, 4, S2])
        mx = sb("m_mx", [P, 4])
        den = sb("m_den", [P, 4])
        pT = sb("m_pT", [P, 2, 2, P])
        SC = float(P) ** -0.5

        with nc.Block() as block:
            @block.sync
            def _(sp):
                loads.upto(sp, "mg1")

            @block.tensor
            def _(pe):
                pe.wait_ge(S["m_memn"], 1)
                for x in range(2):
                    pe.wait_ge(*ring.arrived(f"kv{x}"))
                    w = W[:, ring.chunks[f"kv{x}"][0], :].rearrange("p (k n) -> p k n", k=KT)
                    if x == 0:
                        for j in range(4):
                            for k in range(KT):
                                mm = nc.tensor.matmul(ps[j][:, 0:S2], w[:, k, j * P:(j + 1) * P], memn[:, k, :], start=(k == 0), stop=(k == KT - 1))
                            mm.then_inc(S["m_kv"], 1)
                    else:
                        for c in range(2):
                            for k in range(KT):
                                mm = nc.tensor.matmul(ps[4 + c][:, :], memn[:, k, c * P:(c + 1) * P], w[:, k, :], start=(k == 0), stop=(k == KT - 1))
                            mm.then_inc(S["m_kv"], 1)
                    nc.tensor.drain().then_inc(ring.used, 1)
                pe.wait_ge(S["m_ksq"], 1)
                for j in range(2):
                    mm = nc.tensor.matmul(ps[6 + j][:, :], m.mean128[:, :], rs[:, 2 * j:2 * j + 2, :], start=True, stop=True)
                mm.then_inc(S["m_kms"], 1)
                pe.wait_ge(S["m_k"], 1)
                for c in range(2):
                    if c:
                        pe.wait_ge(S["m_exp"], c)
                    for h in range(4):
                        mm = nc.tensor.matmul(ps[h // 2][:, 256 * (h % 2):256 * (h % 2) + 256], m.raw[:, 6 + h, c * P:(c + 1) * P], kT[:, h, :], start=True, stop=True)
                    mm.then_inc(S["m_logit"], 1)
                    pe.wait_ge(S["m_prob"], c + 1)
                    for h in range(4):
                        q = 4 * c + h
                        if q >= 2:
                            pe.wait_ge(S["m_pT_sb"], q - 1)
                        for j in range(2):
                            mm = nc.tensor.transpose(ps[4 + h % 2][:, j * P:(j + 1) * P], p[:, h, j * P:(j + 1) * P], m.ident[:, :])
                        mm.then_inc(S["m_pT"], 1)
                        pe.wait_ge(S["m_pT_sb"], q + 1)
                        if q == 4:
                            pe.wait_ge(S["m_out"], 1)
                        for j in range(2):
                            mm = nc.tensor.matmul(ps[6][:, h * P:(h + 1) * P], v[:, j, h * P:(h + 1) * P], pT[:, h % 2, j, :], start=(j == 0), stop=(j == 1))
                        mm.then_inc(S["m_pv"], 1)

            @block.scalar
            def _(act):
                for j in range(4):
                    act.wait_ge(S["m_kv"], j + 1)
                    nc.scalar.activation(rs[:, j, :], ps[j][:, 0:S2], ACT.Square)
                act.drain().then_inc(S["m_ksq"], 1)
                for c in range(2):
                    act.wait_ge(S["m_kv"], 5 + c)
                    nc.scalar.activation(v[:, c, :], ps[4 + c][:, :], ACT.Copy)
                act.wait_ge(S["m_kms"], 1)
                for j in range(2):
                    nc.scalar.activation(rs[:, 2 * j:2 * j + 2, :], ps[6 + j][:, :].rearrange("p (a t) -> p a t", a=2), ACT.Ln, bias=m.eps6[:, 0:1])
                act.drain()
                nc.scalar.activation(rs[:, :, :], rs[:, :, :], ACT.Exp, scale=-0.5)
                act.drain().then_inc(S["m_krs"], 1)
                for c in range(2):
                    act.wait_ge(S["m_max"], c + 1)
                    for h in range(4):
                        nc.scalar.activation(p[:, h, :], ps[h // 2][:, 256 * (h % 2):256 * (h % 2) + 256], ACT.Exp, bias=mx[:, h:h + 1], scale=SC,
                                             accum_out=den[:, h:h + 1])
                    act.drain().then_inc(S["m_exp"], 1)
                    act.wait_ge(S["m_pv"], 4 * c + 4)
                    nc.scalar.activation(m.o_mem[:, :, c * P:(c + 1) * P], ps[6][:, :].rearrange("p (h q) -> p h q", h=4), ACT.Copy).then_inc(S["m_out"], 1)

            @block.vector
            def _(dve):
                for k in range(KT):
                    nc.vector.scalar_tensor_tensor(memn[:, k, :], m.memT[:, k, :], m.prmT[:, 32 + k:33 + k], m.mem_rstd[:, :], ALU.mult, ALU.mult)
                dve.drain().then_inc(S["m_memn"], 1)
                dve.wait_ge(S["m_krs"], 1)
                for j in range(4):
                    nc.vector.scalar_tensor_tensor(kT[:, j, :], ps[j][:, 0:S2], m.prmT[:, 50:51], rs[:, j, :], ALU.mult, ALU.mult)
                dve.drain().then_inc(S["m_k"], 1)
                for c in range(2):
                    dve.wait_ge(S["m_logit"], c + 1)
                    for x in range(2):
                        nc.vector.tensor_reduce(mx[:, 2 * x:2 * x + 2], ps[x][:, :].rearrange("p (a t) -> p a t", a=2), AX.X, ALU.max)
                    dve.drain()
                    nc.vector.tensor_scalar(mx[:, :], mx[:, :], -SC, None, ALU.mult)
                    dve.drain().then_inc(S["m_max"], 1)
                    dve.wait_ge(S["m_exp"], c + 1)
                    nc.vector.reciprocal(den[:, :], den[:, :])
                    dve.drain()
                    nc.vector.tensor_tensor(p[:, :, :], p[:, :, :], den[:, :].unsqueeze(2).to_broadcast([P, 4, S2]), ALU.mult)
                    dve.drain().then_inc(S["m_prob"], 1)
                    for h in range(4):
                        q = 4 * c + h
                        dve.wait_ge(S["m_pT"], q + 1)
                        if q >= 2:
                            dve.wait_ge(S["m_pv"], q - 1)
                        nc.vector.tensor_copy(pT[:, h % 2, :, :], ps[4 + h % 2][:, 0:256].rearrange("p (j q) -> p j q", j=2)).then_inc(S["m_pT_sb"], 1)


def gated_linear(nc, m, l, A, S, loads):
    ps = m.ps
    with ExitStack() as ctx:
        def sb(name, shape):
            return ctx.enter_context(nc.sbuf_tensor(name, shape, F32))

        la = sb("g_la", [P, 2, 256])
        t1 = sb("g_t1", [P, 2, 256])
        ex = sb("g_ex", [P, 8, P])
        qs = sb("g_qs", [P, 8, P])
        ks = sb("g_ks", [P, 8, P])
        far = sb("g_far", [P, 2, 2, P])
        prod = sb("g_prod", [P, 8, P])
        att = sb("g_att", [P, 4, 3, P])
        oT = sb("g_oT", [P, 4, S2])
        rs = sb("g_rs", [P, 4, S2])
        UNITS = [(f, t) for f in range(2) for t in range(2)]

        with nc.Block() as block:
            @block.tensor
            def _(pe):
                pe.wait_ge(S["small_loaded"], 48)
                for t in range(2):
                    nc.tensor.matmul(ps[0][:, 256 * t:256 * t + 256], m.glow[:, t * P:(t + 1) * P], m.w_gate[:, :], start=True, stop=False)
                    mm = nc.tensor.matmul(ps[0][:, 256 * t:256 * t + 256], m.ones[0:1, :], m.b_gate[:, :], start=False, stop=True)
                mm.then_inc(S["g_gate"], 1)
                pe.wait_ge(S["g_la"], 1)
                for u, (f, t) in enumerate(UNITS):
                    if u:
                        pe.wait_ge(S["g_ex"], u)
                    lhs = la[:, t, f * P:(f + 1) * P]
                    nc.tensor.matmul(ps[1][:, :], lhs, m.sums[:, 0:4, :], start=True, stop=True)
                    nc.tensor.matmul(ps[2][:, 0:384], lhs, m.sums[:, 4:7, :], start=True, stop=True)
                    nc.tensor.matmul(ps[2][:, 384:512], lhs, m.sums[:, 7 + t, :], start=True, stop=True).then_inc(S["g_sums"], 1)
                    pe.wait_ge(S["g_qk"], u + 1)
                    for a in range(2):
                        hs = slice(64 * a, 64 * a + 64)
                        if u or a:
                            pe.wait_ge(S["g_prod"], 2 * u + a)
                        for lv in range(8):
                            mm = nc.tensor.matmul(ps[3 + lv // 4][:, lv % 4 * P:(lv % 4 + 1) * P], ks[hs, lv, :], qs[hs, lv, :], start=True, stop=True)
                        mm.then_inc(S["g_pairs"], 1)
                        if t == 1:
                            mm = nc.tensor.matmul(ps[5 * (1 - a)][:, f * P:(f + 1) * P], far[hs, f, 0, :], far[hs, f, 1, :], start=True, stop=True)
                            mm.then_inc(S["g_far"], 1)
                pe.wait_ge(S["g_att"], 1)
                for h in range(4):
                    o = ps[6 + h % 2]
                    if h >= 2:
                        pe.wait_ge(S["g_o_sb"], h - 1)
                    v0, v1 = m.gv[:, 0, h * P:(h + 1) * P], m.gv[:, 1, h * P:(h + 1) * P]
                    nc.tensor.matmul(o[:, 0:P], v0, att[:, h, 0, :], start=True, stop=True)
                    nc.tensor.matmul(o[:, P:2 * P], v1, att[:, h, 1, :], start=True, stop=False)
                    nc.tensor.matmul(o[:, P:2 * P], v0, att[:, h, 2, :], start=False, stop=True).then_inc(S["g_o"], 1)
                pe.wait_ge(S["g_osq"], 1)
                for j in range(2):
                    mm = nc.tensor.matmul(ps[j][:, :], m.mean128[:, :], rs[:, 2 * j:2 * j + 2, :], start=True, stop=True)
                mm.then_inc(S["g_oms"], 1)

            @block.scalar
            def _(act):
                act.wait_ge(S["g_abs"], 1)
                nc.scalar.activation(t1[:, :, :], t1[:, :, :], ACT.Exp, scale=-1.0)
                act.drain()
                nc.scalar.activation(t1[:, :, :], t1[:, :, :], ACT.Ln, bias=1.0)
                act.drain().then_inc(S["g_ln"], 1)
                for u, (f, t) in enumerate(UNITS):
                    act.wait_ge(S["g_sums"], u + 1)
                    if u:
                        act.wait_ge(S["g_qk"], u)
                    nc.scalar.activation(ex[:, 0:4, :], ps[1][:, :].rearrange("p (l i) -> p l i", l=4), ACT.Exp, scale=1.0 / 16)
                    nc.scalar.activation(ex[:, 4:8, :], ps[2][:, :].rearrange("p (l i) -> p l i", l=4), ACT.Exp, scale=1.0 / 16)
                    act.drain().then_inc(S["g_ex"], 1)
                act.wait_ge(S["g_far"], 4)
                for a in range(2):
                    nc.scalar.activation(att[:, a:4:2, 2, :], ps[5 * (1 - a)][:, 0:2 * P].rearrange("p (f i) -> p f i", f=2), ACT.Copy, scale=0.125)
                act.drain().then_inc(S["g_far_sb"], 1)
                for h in range(4):
                    act.wait_ge(S["g_o"], h + 1)
                    nc.scalar.activation(oT[:, h, :], ps[6 + h % 2][:, 0:S2], ACT.Copy).then_inc(S["g_o_sb"], 1)
                act.drain()
                nc.scalar.activation(rs[:, :, :], oT[:, :, :], ACT.Square)
                act.drain().then_inc(S["g_osq"], 1)
                act.wait_ge(S["g_oms"], 1)
                for j in range(2):
                    nc.scalar.activation(rs[:, 2 * j:2 * j + 2, :], ps[j][:, :].rearrange("p (a t) -> p a t", a=2), ACT.Ln, bias=m.eps6[:, 0:1])
                act.drain()
                nc.scalar.activation(rs[:, :, :], rs[:, :, :], ACT.Exp, scale=-0.5)
                nc.scalar.activation(m.gr[:, :, :], m.gr[:, :, :], ACT.Silu)
                act.drain().then_inc(S["g_ors"], 1)

            @block.vector
            def _(dve):
                dve.wait_ge(S["g_gate"], 1)
                nc.vector.tensor_copy(la[:, :, :], ps[0][:, :].rearrange("p (t n) -> p t n", t=2))
                dve.drain()
                nc.vector.tensor_scalar(t1[:, :, :], la[:, :, :], -1.0, None, ALU.mult)
                dve.drain()
                nc.vector.tensor_tensor(t1[:, :, :], t1[:, :, :], la[:, :, :], ALU.max)
                dve.drain().then_inc(S["g_abs"], 1)
                dve.wait_ge(S["g_ln"], 1)
                nc.vector.scalar_tensor_tensor(la[:, :, :], la[:, :, :], 0.0, t1[:, :, :], ALU.min, ALU.subtract)
                dve.drain().then_inc(S["g_la"], 1)
                for u, (f, t) in enumerate(UNITS):
                    dve.wait_ge(S["g_ex"], u + 1)
                    if u:
                        dve.wait_ge(S["g_pairs"], 2 * u)
                    q, k = m.gqk[:, f, t * P:(t + 1) * P], m.gqk[:, 2 + f, t * P:(t + 1) * P]
                    nc.vector.tensor_tensor(qs[:, 0:7, :], ex[:, 0:7, :], q.unsqueeze(1).to_broadcast([P, 7, P]), ALU.mult)
                    nc.vector.tensor_tensor(ks[:, 0:7, :], ex[:, 0:7, :], k.unsqueeze(1).to_broadcast([P, 7, P]), ALU.mult)
                    nc.vector.tensor_copy(qs[:, 7, :], q)
                    nc.vector.tensor_copy(ks[:, 7, :], k)
                    nc.vector.tensor_tensor(far[:, f, t, :], ex[:, 7, :], q if t else k, ALU.mult)
                    dve.drain().then_inc(S["g_qk"], 1)
                    for a in range(2):
                        dve.wait_ge(S["g_pairs"], 2 * u + a + 1)
                        for b in range(2):
                            nc.vector.tensor_tensor(prod[:, 4 * b:4 * b + 4, :], ps[3 + b][:, :].rearrange("p (l i) -> p l i", l=4), m.pairs[:, 4 * b:4 * b + 4, :], ALU.mult)
                        dve.drain().then_inc(S["g_prod"], 1)
                        nc.vector.tensor_reduce(att[:, 2 * f + a, t, :], prod[:, :, :].rearrange("p l i -> p i l"), AX.X, ALU.add)
                        dve.drain()
                dve.wait_ge(S["g_far_sb"], 1)
                dve.drain().then_inc(S["g_att"], 1)
                dve.wait_ge(S["g_ors"], 1)
                nc.vector.tensor_tensor(oT[:, :, :], oT[:, :, :], rs[:, :, :], ALU.mult)
                dve.drain()
                nc.vector.scalar_tensor_tensor(m.o_gla[:, :, :], oT[:, :, :], m.prmT[:, 48:49], m.gr[:, :, :], ALU.mult, ALU.mult)


def merge2(nc, m, l, A, S, loads):
    ring, ps, W = m.ring, m.ps, m.W
    with ExitStack() as ctx:
        def sb(name, shape):
            return ctx.enter_context(nc.sbuf_tensor(name, shape, F32))

        gate = sb("x_gate", [P, 2, S2])
        term = sb("x_term", [P, 2, S2])
        acc = sb("x_acc", [P, KT, S2])
        branch = [m.o_nsa, m.o_gla, m.o_mem]

        with nc.Block() as block:
            @block.sync
            def _(sp):
                loads.upto(sp, "md1")

            @block.tensor
            def _(pe):
                for b in range(3):
                    wb = W[:, ring.chunks[f"br{b}"][0], :].rearrange("p (k n) -> p k n", k=4)
                    for n in range(KT):
                        q = KT * b + n
                        mg = f"mg{2 * b + n // 4}"
                        if n % 4 == 0:
                            pe.wait_ge(*ring.arrived(mg))
                        wm = W[:, ring.chunks[mg][0], :].rearrange("p (k n) -> p k n", k=KT)
                        if q >= 2:
                            pe.wait_ge(S["x_gate"], q - 1)
                        for k in range(KT):
                            mm = nc.tensor.matmul(ps[q % 2][:, 0:S2], wm[:, k, n % 4 * P:n % 4 * P + P], m.hT[:, k, :], start=(k == 0), stop=(k == KT - 1))
                        mm.then_inc(S["x_merge"], 1)
                        if n == 0:
                            pe.wait_ge(*ring.arrived(f"br{b}"))
                        if q >= 2:
                            pe.wait_ge(S["x_term"], q - 1)
                        for k in range(4):
                            mm = nc.tensor.matmul(ps[2 + q % 2][:, 0:S2], wb[:, k, n * P:(n + 1) * P], branch[b][:, k, :], start=(k == 0), stop=(k == 3))
                        mm.then_inc(S["x_branch"], 1)
                        if n == 3:
                            nc.tensor.drain().then_inc(ring.used, 1)
                    nc.tensor.drain().then_inc(ring.used, 2)
                pe.wait_ge(S["x_acc"], 1)
                for n in range(KT):
                    if n % 4 == 0:
                        pe.wait_ge(*ring.arrived(f"wo{n // 4}"))
                    w = W[:, ring.chunks[f"wo{n // 4}"][0], :].rearrange("p (k n) -> p k n", k=KT)
                    if n >= 4:
                        pe.wait_ge(S["x_res"], n - 3)
                    for k in range(KT):
                        mm = nc.tensor.matmul(ps[4 + n % 4][:, 0:S2], w[:, k, n % 4 * P:n % 4 * P + P], acc[:, k, :], start=(k == 0), stop=(k == KT - 1))
                    mm.then_inc(S["x_out"], 1)
                    if n % 4 == 3:
                        nc.tensor.drain().then_inc(ring.used, 1)

            @block.scalar
            def _(act):
                for q in range(3 * KT):
                    act.wait_ge(S["x_merge"], q + 1)
                    if q >= 2:
                        act.wait_ge(S["x_term"], q - 1)
                    nc.scalar.activation(gate[:, q % 2, :], ps[q % 2][:, 0:S2], ACT.Sigmoid, bias=m.prmT[:, 8 + q:9 + q]).then_inc(S["x_gate"], 1)

            @block.vector
            def _(dve):
                for q in range(3 * KT):
                    n = q % KT
                    dve.wait_ge(S["x_gate"], q + 1)
                    dve.wait_ge(S["x_branch"], q + 1)
                    if q < KT:
                        nc.vector.tensor_tensor(acc[:, n, :], gate[:, q % 2, :], ps[2 + q % 2][:, 0:S2], ALU.mult)
                        dve.drain().then_inc(S["x_term"], 1)
                    else:
                        nc.vector.tensor_tensor(term[:, q % 2, :], gate[:, q % 2, :], ps[2 + q % 2][:, 0:S2], ALU.mult)
                        dve.drain().then_inc(S["x_term"], 1)
                        nc.vector.tensor_tensor(acc[:, n, :], acc[:, n, :], term[:, q % 2, :], ALU.add)
                dve.drain().then_inc(S["x_acc"], 1)
                for n in range(KT):
                    dve.wait_ge(S["x_out"], n + 1)
                    nc.vector.tensor_tensor(m.xT[:, n, :], m.xT[:, n, :], ps[4 + n % 4][:, 0:S2], ALU.add).then_inc(S["x_res"], 1)


def mlp2(nc, m, l, A, S):
    ring, ps, W = m.ring, m.ps, m.W
    w_up = A["w_up_2"].rearrange("l (k p) (c n) -> l c p k n", p=P, n=512)
    w_down = A["w_down_2"].rearrange("l (c k p) n -> l c p k n", p=P, k=4)
    PAIRS = HIDDEN // 1024
    used0 = m.used_before_mlp
    slots = m.mlp_slots
    first = [(ring.arrived(f"mu{x}")[1], ring.arrived(f"md{x}")[1]) for x in range(2)]
    with ExitStack() as ctx:
        def sb(name, shape):
            return ctx.enter_context(nc.sbuf_tensor(name, shape, F32))

        hid = sb("u_hid", [P, 2, 4, S2])
        rel = sb("u_rel", [P, 2, S2])
        on_act, on_pe, on_dve = rms_steps(nc, m, (S["u_sq"], S["u_ms"], S["u_rstd"], S["u_done"]), 40)

        with nc.Block() as block:
            @block.sync
            def _(sp):
                with sp.Fori(0, PAIRS - 1) as it:
                    for x in range(2):
                        a, b = slots[x]
                        sp.wait_ge(ring.used, it * 4 + (used0 + 2 * x + 1))
                        sp.dma_start(W[:, a, :].rearrange("p (k n) -> p k n", k=KT), w_up[l, it * 2 + (2 + x), :, :, :]).then_inc(ring.loaded[a], 16)
                        sp.wait_ge(ring.used, it * 4 + (used0 + 2 * x + 2))
                        sp.dma_start(W[:, b, :].rearrange("p (k n) -> p k n", k=4), w_down[l, it * 2 + (2 + x), :, :, :]).then_inc(ring.loaded[b], 16)

            @block.tensor
            def _(pe):
                on_pe(pe)
                pe.wait_ge(S["u_done"], KT)
                with pe.Fori(0, PAIRS) as it:
                    for x in range(2):
                        wa = W[:, slots[x][0], :].rearrange("p (k n) -> p k n", k=KT)
                        wb = W[:, slots[x][1], :].rearrange("p (k n) -> p k n", k=4)
                        pe.wait_ge(ring.loaded[slots[x][0]], it * 16 + first[x][0])
                        for j in range(4):
                            pe.wait_ge(S["u_h_free"], it * 8 + (4 * x + j + 1))
                            for k in range(KT):
                                mm = nc.tensor.matmul(ps[j % 2][:, 0:S2], wa[:, k, j * P:(j + 1) * P], m.hT[:, k, :], start=(k == 0), stop=(k == KT - 1))
                            mm.then_inc(S["u_h"], 1)
                        nc.tensor.drain().then_inc(ring.used, 1)
                        pe.wait_ge(ring.loaded[slots[x][1]], it * 16 + first[x][1])
                        pe.wait_ge(S["u_hid"], it * 8 + (4 * x + 4))
                        for n in range(KT):
                            pe.wait_ge(S["u_y_free"], it * 16 + (8 * x + n + 1))
                            for k in range(4):
                                mm = nc.tensor.matmul(ps[4 + n % 2][:, 0:S2], wb[:, k, n * P:(n + 1) * P], hid[:, x, k, :], start=(k == 0), stop=(k == 3))
                            mm.then_inc(S["u_y"], 1)
                        nc.tensor.drain().then_inc(ring.used, 1)

            @block.scalar
            def _(act):
                on_act(act)
                with act.Fori(0, PAIRS) as it:
                    for x in range(2):
                        for j in range(4):
                            act.wait_ge(S["u_h"], it * 8 + (4 * x + j + 1))
                            nc.scalar.activation(rel[:, j % 2, :], ps[j % 2][:, 0:S2], ACT.Relu)
                            act.drain().then_inc(S["u_h_free"], 1)
                            nc.scalar.activation(hid[:, x, j, :], rel[:, j % 2, :], ACT.Square)
                            act.drain().then_inc(S["u_hid"], 1)

            @block.vector
            def _(dve):
                dve.drain().then_inc(S["u_h_free"], 2)
                dve.drain().then_inc(S["u_y_free"], 2)
                on_dve(dve)
                with dve.Fori(0, PAIRS) as it:
                    for x in range(2):
                        for n in range(KT):
                            dve.wait_ge(S["u_y"], it * 16 + (8 * x + n + 1))
                            nc.vector.tensor_tensor(m.xT[:, n, :], m.xT[:, n, :], ps[4 + n % 2][:, 0:S2], ALU.add).then_inc(S["u_y_free"], 1)


SEMS2 = """params_loaded params_turned small_loaded p_sq p_ms p_rstd p_done p_mm p_act p_dve
h_kk h_sq h_ms h_win h_hid h_xs h_rope h_gelu h_turn h_hidT h_comp h_ksq h_kms h_kxs h_krope h_rs h_gin h_gexp h_krs
n_pT_sb n_logit n_prob n_pcT n_pT n_pcT_sb n_out n_pv n_gin n_gexp n_max n_exp
m_memn m_kv m_ksq m_kms m_k m_exp m_logit m_prob m_pT_sb m_pT m_out m_pv m_krs m_max
g_gate g_la g_ex g_sums g_qk g_prod g_pairs g_far g_att g_o_sb g_o g_osq g_oms g_abs g_ln g_far_sb g_ors
x_gate x_merge x_term x_branch x_acc x_res x_out
u_sq u_ms u_rstd u_done u_h_free u_h u_hid u_y_free u_y""".split()


def second_block(nc, ps, xT, A, out):
    with ExitStack() as ctx:
        def sb(name, shape, dt=F32):
            return ctx.enter_context(nc.sbuf_tensor(name, shape, dt))

        def sem(name):
            return ctx.enter_context(nc.semaphore(name))

        C = constants2()
        m = Buffers()
        m.ps, m.xT = ps, xT
        K = load_constants(nc, ctx, C, "2")
        m.ident, m.mean_w, m.mean128, m.mean64 = K["ident"], K["mean_w"], K["mean128"], K["mean64"]
        m.rot, m.causal_bias, m.cmp_mask, m.cmp_bias = K["rot"], K["causal_bias"], K["cmp_mask"], K["cmp_bias"]
        m.inv_freq, m.sums, m.pairs = K["inv_freq"], K["sums"], K["pairs"]
        m.ones = sb("ones2", [1, P])
        m.W = sb("W2", [P, SLOTS, SLOT])
        m.prm = sb("prm2", [P, P])
        m.prmT = sb("prmT2", [P, 96])
        m.eps6 = sb("eps6_2", [P, 1])
        m.memT = sb("memT", [P, KT, S2])
        m.mem_rstd = sb("mem_rstd", [P, S2])
        m.rstd = sb("rstd2", [P, S2])
        m.cos = sb("cos2", [P, S2])
        m.sin = sb("sin2", [P, S2])
        m.w_gate = sb("w_gate", [16, 256])
        m.b_gate = sb("b_gate", [1, 256])
        m.w_cmp2 = sb("w_cmp2", [P, 2, 2, 64])
        m.hT = sb("hT2", [P, KT, S2])
        mem_loaded, mem_turned, mem_copied, pos_loaded = sem("mem_loaded"), sem("mem_turned"), sem("mem_copied"), sem("pos_loaded")
        mem_sq, mem_ms, angles = sem("mem_sq"), sem("mem_ms"), sem("angles")
        with nc.sbuf_tensor("mem_tok", [P, 2, D], F32) as mt, nc.sbuf_tensor("pos_i", [P, S2], I32) as pos_i, \
                nc.sbuf_tensor("ang", [P, 4, S2], F32) as ang, nc.sbuf_tensor("turns", [P, S2], I32) as turns, nc.Block() as block:
            @block.sync
            def _(sp):
                sp.dma_start(mt[:, :, :], A["mem_2"].rearrange("a (t p) d -> p (a t) d", p=P)).then_inc(mem_loaded, 16)
                sp.dma_start(pos_i[:, :], A["positions_2"].to_broadcast([P, S2])).then_inc(pos_loaded, 16)

            @block.tensor
            def _(pe):
                pe.wait_ge(mem_loaded, 16)
                for k in range(KT):
                    if k >= 4:
                        pe.wait_ge(mem_copied, k - 3)
                    for t in range(2):
                        mm = nc.tensor.transpose(m.ps[k % 4][:, t * P:(t + 1) * P], mt[:, t, k * P:(k + 1) * P], m.ident[:, :])
                    mm.then_inc(mem_turned, 1)
                for k in range(KT):
                    pe.wait_ge(mem_sq, k + 1)
                    mm = nc.tensor.matmul(m.ps[4][:, 0:S2], m.mean_w[:, :], m.hT[:, k, :], start=(k == 0), stop=(k == KT - 1))
                mm.then_inc(mem_ms, 1)

            @block.scalar
            def _(act):
                for k in range(KT):
                    act.wait_ge(mem_copied, k + 1)
                    nc.scalar.activation(m.hT[:, k, :], m.memT[:, k, :], ACT.Square).then_inc(mem_sq, 1)
                act.wait_ge(mem_ms, 1)
                nc.scalar.activation(m.mem_rstd[:, :], m.ps[4][:, 0:S2], ACT.Ln, bias=m.eps6[:, 0:1])
                act.drain()
                nc.scalar.activation(m.mem_rstd[:, :], m.mem_rstd[:, :], ACT.Exp, scale=-0.5)
                act.wait_ge(angles, 1)
                nc.scalar.activation(m.sin[:, :], ang[:, 2, :], ACT.Sin)
                nc.scalar.activation(m.cos[:, :], ang[:, 3, :], ACT.Sin)

            @block.vector
            def _(dve):
                nc.vector.memset(m.eps6[:, :], 1e-6)
                nc.vector.memset(m.ones[:, :], 1.0)
                dve.drain()
                for k in range(KT):
                    dve.wait_ge(mem_turned, k + 1)
                    nc.vector.tensor_copy(m.memT[:, k, :], m.ps[k % 4][:, 0:S2])
                    dve.drain().then_inc(mem_copied, 1)
                dve.wait_ge(pos_loaded, 16)
                nc.vector.tensor_copy(ang[:, 0, :], pos_i[:, :])
                dve.drain()
                nc.vector.tensor_scalar(ang[:, 0, :], ang[:, 0, :], m.inv_freq[:, 0:1], None, ALU.mult)
                dve.drain()
                for row, quarter in ((2, 0.0), (3, 0.25)):
                    nc.vector.tensor_scalar(ang[:, 1, :], ang[:, 0, :], float(1 / (2 * np.pi)), quarter, ALU.mult, ALU.add)
                    dve.drain()
                    nc.vector.tensor_copy(turns[:, :], ang[:, 1, :])
                    dve.drain()
                    nc.vector.tensor_copy(ang[:, 1, :], turns[:, :])
                    dve.drain()
                    nc.vector.scalar_tensor_tensor(ang[:, row, :], ang[:, 1, :], -TURN[0], ang[:, 0, :], ALU.mult, ALU.add)
                    dve.drain()
                    for part in TURN[1:]:
                        nc.vector.scalar_tensor_tensor(ang[:, row, :], ang[:, 1, :], -part, ang[:, row, :], ALU.mult, ALU.add)
                        dve.drain()
                    if quarter:
                        nc.vector.tensor_scalar(ang[:, row, :], ang[:, row, :], float(np.pi / 2), None, ALU.add)
                        dve.drain()
                    for cmp, sign in ((ALU.is_gt, -1.0), (ALU.is_lt, 1.0)):
                        nc.vector.tensor_scalar(ang[:, 1, :], ang[:, row, :], -sign * PI, sign * 2 * np.pi, cmp, ALU.mult)
                        dve.drain()
                        nc.vector.tensor_tensor(ang[:, row, :], ang[:, row, :], ang[:, 1, :], ALU.add)
                        dve.drain()
                    nc.vector.tensor_scalar(ang[:, row, :], ang[:, row, :], PI, -PI, ALU.min, ALU.max)
                    dve.drain()
                dve.drain().then_inc(angles, 1)

        signals = {name: sem("b_" + name) for name in SEMS2}
        S = signals
        loaded = [sem(f"loaded2_{i}") for i in range(SLOTS)]
        used = sem("used2")
        with nc.Fori(0, DEPTH) as l:
            ring = m.ring = WeightRing(loaded, used)
            loads = weights2(nc, m, l, A, ring)
            with ExitStack() as lay:
                def lsb(name, shape):
                    return lay.enter_context(nc.sbuf_tensor(name, shape, F32))

                m.raw = lsb("b_raw", [P, 10, S2])
                m.vs = lsb("b_vs", [P, 2, P])
                m.vw = lsb("b_vw", [P, 2, P])
                m.ngate = lsb("b_ngate", [P, 2, 24])
                m.glow = lsb("b_glow", [16, S2])
                m.gqk = lsb("b_gqk", [P, 4, S2])
                m.gv = lsb("b_gv", [P, 2, 512])
                m.gr = lsb("b_gr", [P, 4, S2])
                m.kcmp = lsb("b_kcmp", [P, N_CMP])
                m.vcmp = lsb("b_vcmp", [N_CMP, P])
                m.o_nsa = lsb("b_o_nsa", [P, 4, S2])
                m.o_gla = lsb("b_o_gla", [P, 4, S2])
                m.o_mem = lsb("b_o_mem", [P, 4, S2])
                with nc.sbuf_tensor("b_qk", [P, 6, S2], F32) as m.qk:
                    with nc.sbuf_tensor("b_kcv", [P, 2, S2], F32) as m.kcv:
                        project2(nc, m, l, A, S, loads)
                        heads2(nc, m, l, A, S, loads)
                    native_sparse(nc, m, l, A, S, loads)
                memory2(nc, m, l, A, S, loads)
                gated_linear(nc, m, l, A, S, loads)
                merge2(nc, m, l, A, S, loads)
            mlp2(nc, m, l, A, S)
            clear(nc, list(signals.values()), ring)

        turned, copied, stored = sem("out_turned"), sem("out_copied"), sem("stored")
        with nc.sbuf_tensor("out_tok", [P, 2, D], F32) as ot, nc.Block() as block:
            @block.tensor
            def _(pe):
                for i in range(4):
                    t, half = i // 2, i % 2
                    for k in range(4):
                        mm = nc.tensor.transpose(m.ps[i][:, k * P:(k + 1) * P], m.xT[:, 4 * half + k, t * P:(t + 1) * P], m.ident[:, :])
                    mm.then_inc(turned, 1)

            @block.vector
            def _(dve):
                for i in range(4):
                    dve.wait_ge(turned, i + 1)
                    nc.vector.tensor_copy(ot[:, i // 2, 512 * (i % 2):512 * (i % 2) + 512], m.ps[i][:, :]).then_inc(copied, 1)

            @block.sync
            def _(sp):
                for t in range(2):
                    sp.wait_ge(copied, 2 * t + 2)
                    sp.dma_start(out[0, t * P:(t + 1) * P, :], ot[:, t, :]).then_inc(stored, 16)
                sp.wait_ge(stored, 32)


PI = float(np.nextafter(np.float32(np.pi), np.float32(0)))
TURN = [6.28125, 0.0019350051879882812, 3.019916050561733e-07]
NAMES2 = """mem_2 positions_2 ln_mix_2 w_in_2 b_merge_2 nsa_q_norm_2 nsa_k_norm_2 cmp_pe_2 cmp_w1_2 cmp_w2_2 gla_w_gate_2 gla_b_gate_2
gla_norm_2 mem_norm_2 mem_w_kv_2 mem_q_norm_2 mem_k_norm_2 w_branch_2 w_out_2 ln_mlp_2 w_up_2 w_down_2""".split()


def program(nc, A, out):
    with ExitStack() as ctx:
        ps = [ctx.enter_context(nc.psum_tensor(f"bank{i}", [P, 512], F32)) for i in range(8)]
        xT = ctx.enter_context(nc.sbuf_tensor("xT", [P, KT, SEQ], F32))
        first_block(nc, ps, xT, A, A["x"], A["meta_tokens"])
        second_block(nc, ps, xT, A, out)


def kernel(**inputs):
    import numpy as _np
    import concourse.bacc as _bacc
    from concourse import mybir as _mybir
    from concourse.bass_utils import run_bass_kernel_spmd as _run

    nc = _bacc.Bacc("TRN2", target_bir_lowering=False, num_devices=1)
    arrays, A = {}, {}
    for name in ["x", "meta_tokens"] + NAMES1 + NAMES2:
        a = _np.ascontiguousarray(inputs[name])
        arrays["in_" + name] = a
        A[name] = nc.dram_tensor("in_" + name, a.shape, _mybir.dt.from_np(a.dtype), kind="ExternalInput").ap()
    out = nc.dram_tensor("out", (1, SEQ, D), _mybir.dt.float32, kind="ExternalOutput").ap()
    program(nc, A, out)
    return _run(nc, [arrays], core_ids=[0]).results[0]["out"]
```

```python
from contextlib import ExitStack

import numpy as np

import concourse.bass as bass
from concourse import mybir

F32 = mybir.dt.float32
I32 = mybir.dt.int32
ALU = mybir.AluOpType
ACT = mybir.ActivationFunctionType
AX = mybir.AxisListType

P = 128
D = 1024
KT = D // P
DEPTH = 2
N_META = 16
SEQ = 256
T = SEQ + N_META
TILES = [(0, 128), (128, 128), (256, 16)]
TOP_K = SEQ // 4
EXPERTS, GROUPS, PER_GROUP, DE = 32, 4, 8, 256
SLOTS_BLOCK = 32
BLOCKS_GROUP = P // SLOTS_BLOCK
MAX_BLOCKS = EXPERTS + 2 * T // SLOTS_BLOCK
MAX_GROUPS = -(-MAX_BLOCKS // BLOCKS_GROUP)
ALPHA = (2.0 * DEPTH) ** 0.25
BIG = 1e30
SLOTS = 4
SLOT = KT * 512


class WeightRing:

    def __init__(self, loaded, used):
        self.loaded, self.used = loaded, used
        self.in_slot = [0] * SLOTS
        self.last_in_slot = [None] * SLOTS
        self.chunks = {}
        self.n = 0

    def add(self, name, slot, dmas=1):
        before = self.last_in_slot[slot]
        self.in_slot[slot] += 16 * dmas
        self.chunks[name] = (slot, self.in_slot[slot], None if before is None else before + 1)
        self.last_in_slot[slot] = self.n
        self.n += 1

    def arrived(self, name):
        slot, value, _ = self.chunks[name]
        return self.loaded[slot], value

    def freed(self, name):
        before = self.chunks[name][2]
        return None if before is None else (self.used, before)


def constants():
    i = np.arange(P)
    c = {}
    c["ident"] = np.eye(P)
    c["ones"] = np.ones((P, P))
    c["mean_w"] = np.full((P, P), 1.0 / D)
    c["cum"] = i[:, None] <= i[None, :]
    c["strict"] = i[:, None] > i[None, :]
    c["incl"] = i[:, None] >= i[None, :]
    lv = [((i[:, None] >> l) == (i[None, :] >> l) + 1) & ((i[:, None] >> l) % 2 == 1) for l in range(7)]
    c["level0"] = lv[0]
    c["levelsT"] = np.stack([m.T for m in lv], 1)
    t = np.arange(T)
    c["causal"] = np.stack([(t[None, :] <= (t0 + i)[:, None]) for t0, _ in TILES], 1)
    rot = np.zeros((P, P))
    for h in (0, 64):
        for d in range(32):
            rot[h + d + 32, h + d] = -1.0
            rot[h + d, h + d + 32] = 1.0
    c["rot"] = rot
    inv = (1.0 / (np.float32(10000.0) ** (np.arange(0, 64, 2, dtype=np.float32) / np.float32(64)))).astype(np.float32)
    ang = (t.astype(np.float32)[None, :] * inv[i % 32][:, None]).astype(np.float32)
    c["cos"] = np.cos(ang.astype(np.float64))
    c["sin"] = np.sin(ang.astype(np.float64))
    c["before"] = np.arange(EXPERTS)[:, None] < np.arange(EXPERTS)[None, :]
    c["count"] = np.broadcast_to(np.arange(P), (P, P))
    c["slot_id"] = i[:, None]
    c["rank4"] = np.broadcast_to(4.0 - np.arange(4), (P, 4))
    c["rank8"] = np.broadcast_to(8.0 - np.arange(8), (P, 8))
    return {k: np.ascontiguousarray(v, np.float32) for k, v in c.items()}


class Buffers:
    pass


def load_constants(nc, ctx, arrays, tag=""):
    buffers = {}
    done = ctx.enter_context(nc.semaphore("constants_loaded" + tag))
    for name, a in arrays.items():
        src = nc.inline_tensor(a, name="c_" + name + tag).ap()
        dst = ctx.enter_context(nc.sbuf_tensor("k_" + name + tag, list(a.shape), F32))
        full = tuple(slice(None) for _ in a.shape)
        nc.sync.dma_start(dst[full], src[full]).then_inc(done, 16)
        buffers[name] = dst
    nc.sync.wait_ge(done, 16 * len(arrays))
    return buffers


def projections(nc, m, l, A, S):
    w_in = A["w_in"].rearrange("l (k p) n -> l p k n", p=P)
    W, ring, ps = m.W, m.ring, m.ps
    plan = [("conv", f"in{c}", 128 * j, 4 * c + j) for c in range(3) for j in range(4)]
    plan += [("z", "in3", 128 * j, j) for j in range(4)]
    plan += [("rope", "in4", 128 * j, j) for j in range(4)]
    plan += [("rope", "in5", 128 * j, 4 + j) for j in range(4)]
    plan += [("sv", "in6", 0, j) for j in range(3)]
    plan += [("rope", "in7", 128 * j, 8 + j) for j in range(4)]
    plan += [("rope", "in8", 16, 12)]
    plan += [("bai", "in8", 0, j) for j in range(3)]
    taker = {"conv": "act", "z": "act", "rope": "dve", "sv": "act", "bai": "dve"}
    rope_dst = [m.sqT[:, j, :] for j in range(4)] + [m.skT[:, j, :] for j in range(4)] + \
               [m.iqT[:, j, :] for j in range(4)] + [m.ikT[:, :]]

    def taken(n):
        who = taker[plan[n][0]]
        return (S["proj_by_act"] if who == "act" else S["proj_by_dve"]), sum(taker[p[0]] == who for p in plan[:n + 1])

    with nc.Block() as block:
        @block.sync
        def _(sp):
            pr = m.prm
            src = [(0, 48, A["conv_w"].rearrange("l j (t f) -> l (j t) f", f=P)[l]),
                   (48, 1, A["dn_norm_g"].rearrange("l (a n) -> l a n", a=1)[l]),
                   (49, 8, A["ln1_g"].rearrange("l (t f) -> l t f", f=P)[l]),
                   (57, 8, A["ln1_b"].rearrange("l (t f) -> l t f", f=P)[l]),
                   (65, 8, A["ln2_g"].rearrange("l (t f) -> l t f", f=P)[l]),
                   (73, 8, A["ln2_b"].rearrange("l (t f) -> l t f", f=P)[l])]
            for r0, n, ap in src:
                sp.dma_start(pr[r0:r0 + n, :], ap).then_inc(S["params_loaded"], 16)
            bc = m.rows
            sp.dma_start(bc[:, 0:4], A["a_log"].rearrange("l (a n) -> l a n", a=1)[l].to_broadcast([P, 4])).then_inc(S["rows_loaded"], 16)
            sp.dma_start(bc[:, 4:8], A["dt_bias"].rearrange("l (a n) -> l a n", a=1)[l].to_broadcast([P, 4])).then_inc(S["rows_loaded"], 16)
            sp.dma_start(bc[:, 8:12], A["b_grp"].rearrange("l (a n) -> l a n", a=1)[l].to_broadcast([P, 4])).then_inc(S["rows_loaded"], 16)
            sp.dma_start(bc[:, 12:44], A["b_rtr"].rearrange("l (a n) -> l a n", a=1)[l].to_broadcast([P, 32])).then_inc(S["rows_loaded"], 16)
            for name, c0, n in (("w_grp", 0, 4), ("w_rtr", 4, 32)):
                sp.dma_start(m.w_route[:, :, c0:c0 + n],
                               A[name].rearrange("l (k p) n -> l p k n", p=P)[l]).then_inc(S["rows_loaded"], 16)
            for c in range(9):
                name = f"in{c}"
                free = ring.freed(name)
                if free:
                    sp.wait_ge(*free)
                slot = ring.chunks[name][0]
                done = ring.loaded[slot]
                w = W[:, slot, :].rearrange("p (k n) -> p k n", k=KT)
                if c < 8:
                    c0 = 512 * c + (8 if c >= 4 else 0)
                    sp.dma_start(w[:, :, :], w_in[l, :, :, c0:c0 + 512]).then_inc(done, 16)
                else:
                    sp.dma_start(w[:, :, 0:8], w_in[l, :, :, 2048:2056]).then_inc(done, 16)
                    sp.dma_start(w[:, :, 8:16], w_in[l, :, :, 4168:4176]).then_inc(done, 16)
                    sp.dma_start(w[:, :, 16:80], w_in[l, :, :, 4104:4168]).then_inc(done, 16)
                    sp.dma_start(w[:, :, 80:144], w_in[l, :, :, 4104:4168]).then_inc(done, 16)

        @block.tensor
        def _(pe):
            pe.wait_ge(S["params_loaded"], 16 * 6)
            nc.tensor.transpose(ps[7][:, 0:81], m.prm[0:81, :], m.ident[0:81, 0:81]).then_inc(S["params_turned"], 1)

            def rope_mm(r):
                pe.wait_ge(S["rope_in"], r + 1)
                if r >= 2:
                    pe.wait_ge(S["rope_out"], r - 1)
                o = ps[4 + r % 2][:, 0:T]
                nc.tensor.matmul(o, m.rot[:, :], m.rope_tmp[:, r % 2, 0, :], start=True, stop=False)
                nc.tensor.matmul(o, m.ident[:, :], m.rope_tmp[:, r % 2, 1, :], start=False, stop=True).then_inc(S["rope_mm"], 1)

            last_chunk, ropes = None, []
            for n, (kind, chunk, c0, idx) in enumerate(plan):
                slot = ring.chunks[chunk][0]
                w = W[:, slot, :].rearrange("p (k n) -> p k n", k=KT)
                if chunk != last_chunk:
                    pe.wait_ge(*ring.arrived(chunk))
                    last_chunk = chunk
                if n >= 4:
                    pe.wait_ge(*taken(n - 4))
                bank = ps[n % 4]
                for k in range(KT):
                    st = dict(start=(k == 0), stop=(k == KT - 1))
                    if kind == "sv":
                        t0, nt = TILES[idx]
                        mm = nc.tensor.matmul(bank[0:nt, 0:512], m.hT[:, k, t0:t0 + nt], w[:, k, :], **st)
                    elif kind == "bai":
                        t0, nt = TILES[idx]
                        mm = nc.tensor.matmul(bank[0:nt, 0:16], m.hT[:, k, t0:t0 + nt], w[:, k, 0:16], **st)
                    else:
                        mm = nc.tensor.matmul(bank[:, 0:T], w[:, k, c0:c0 + P], m.hT[:, k, :], **st)
                mm.then_inc(S["proj"], 1)
                if n + 1 == len(plan) or plan[n + 1][1] != chunk:
                    nc.tensor.drain().then_inc(ring.used, 1)
                if ropes:
                    rope_mm(ropes.pop())
                if kind == "rope":
                    ropes.append(idx)

        @block.scalar
        def _(act):
            convs, ropes, seen = [], [], 0

            def silu(i):
                act.wait_ge(S["conv"], i + 1)
                nc.scalar.activation(m.qkvT[:, i, :], m.conv_out[:, i % 2, :], ACT.Silu).then_inc(S["conv_silu"], 1)

            def rope_evac(r):
                act.wait_ge(S["rope_mm"], r + 1)
                nc.scalar.activation(rope_dst[r], ps[4 + r % 2][:, 0:T], ACT.Copy).then_inc(S["rope_out"], 1)

            for n, (kind, chunk, c0, idx) in enumerate(plan):
                if kind in ("conv", "z", "sv"):
                    act.wait_ge(S["proj"], n + 1)
                    src = ps[n % 4]
                    if kind == "conv":
                        if idx >= 3:
                            act.wait_ge(S["conv"], idx - 2)
                        nc.scalar.activation(m.xpad[:, idx % 3, 3:3 + T], src[:, 0:T], ACT.Copy).then_inc(S["proj_by_act"], 1)
                        convs.append(idx)
                    elif kind == "z":
                        nc.scalar.activation(m.zT[:, idx, :], src[:, 0:T], ACT.Silu).then_inc(S["proj_by_act"], 1)
                    else:
                        nt = TILES[idx][1]
                        nc.scalar.activation(m.sv[0:nt, idx, :], src[0:nt, 0:512], ACT.Copy).then_inc(S["proj_by_act"], 1)
                if len(convs) > 1 or (convs and kind != "conv"):
                    silu(convs.pop(0))
                if ropes:
                    rope_evac(ropes.pop())
                if kind == "rope":
                    ropes.append(idx)
            assert not convs and not ropes

        @block.vector
        def _(dve):
            dve.wait_ge(S["params_turned"], 1)
            nc.vector.tensor_copy(m.prmT[:, 0:81], ps[7][:, 0:81])
            dve.drain()
            for n, (kind, chunk, c0, idx) in enumerate(plan):
                if kind == "conv":
                    dve.wait_ge(S["proj_by_act"], idx + 1)
                    if idx >= 2:
                        dve.wait_ge(S["conv_silu"], idx - 1)
                    y = m.conv_out[:, idx % 2, :]
                    for j in range(4):
                        x = m.xpad[:, idx % 3, j:j + T]
                        wj = m.prmT[:, 12 * j + idx:12 * j + idx + 1]
                        if j == 0:
                            i = nc.vector.tensor_scalar(y, x, wj, None, ALU.mult)
                        else:
                            i = nc.vector.scalar_tensor_tensor(y, x, wj, y, ALU.mult, ALU.add)
                        if j < 3:
                            dve.drain()
                    i.then_inc(S["conv"], 1)
                elif kind == "rope":
                    dve.wait_ge(S["proj"], n + 1)
                    if idx >= 2:
                        dve.wait_ge(S["rope_mm"], idx - 1)
                    src = ps[n % 4][:, 0:T]
                    nc.vector.tensor_tensor(m.rope_tmp[:, idx % 2, 0, :], src, m.sin[:, :], ALU.mult)
                    i = nc.vector.tensor_tensor(m.rope_tmp[:, idx % 2, 1, :], src, m.cos[:, :], ALU.mult)
                    i.then_inc(S["rope_in"], 1)
                    dve.drain().then_inc(S["proj_by_dve"], 1)
                elif kind == "bai":
                    dve.wait_ge(S["proj"], n + 1)
                    nt = TILES[idx][1]
                    nc.vector.tensor_copy(m.bai[0:nt, idx, :], ps[n % 4][0:nt, 0:16]).then_inc(S["proj_by_dve"], 1)


def delta_rule(nc, m, S, ctx):
    ps = m.ps
    H = 4
    q4, k4, v4 = m.qkvT[:, 0:4, :], m.qkvT[:, 4:8, :], m.qkvT[:, 8:12, :]
    def sb(name, shape):
        return ctx.enter_context(nc.sbuf_tensor(name, shape, F32))

    sq = sb("d_sq", [P, 8, T])
    beta = sb("d_beta", [P, 3, H])
    gate = sb("d_gate", [P, 3, H])
    gt = sb("d_gt", [P, 5, 3, H])
    gc = sb("d_gc", [P, H])
    gcum = sb("d_gcum", [P, H, P])
    dif = sb("d_dif", [P, H, P])
    egc = sb("d_egc", [P, 4, H])
    eGB = sb("d_eGB", [P, H, P])
    kbg = sb("d_kbg", [P, H, P])
    vb = sb("d_vb", [P, H, P])
    kdec = sb("d_kdec", [P, H, P])
    qd = sb("d_qd", [P, H, P])
    Lm = sb("d_L", [P, H, P])
    Am = sb("d_A", [P, H, P])
    AT = sb("d_AT", [P, H, P])
    LT = sb("d_LT", [P, H, P])
    LM = sb("d_LM", [P, 2, H, P])
    X = sb("d_X", [P, H, P])
    Y = sb("d_Y", [P, H, P])
    Pm = sb("d_P", [P, H, P])
    wT = sb("d_wT", [P, H, P])
    u = sb("d_u", [P, H, P])
    vn = sb("d_vn", [P, H, P])
    St = sb("d_S", [P, H, P])
    oT = sb("d_oT", [P, H, T])

    def b4(ps_, n, w=P):
        return ps_[0:n, 0:H * P].rearrange("p (h c) -> p h c", h=H)[:, :, 0:w]

    def over_cols(ap, n, w):
        return ap.unsqueeze(2).to_broadcast([n, H, w])

    def over_heads(ap, n, w):
        return ap.unsqueeze(1).to_broadcast([n, H, w])

    def levels(nt):
        return nt.bit_length() - 1

    base = [4]
    for _, nt in TILES:
        base.append(base[-1] + 5 + levels(nt))
    lev_base = [0]
    for _, nt in TILES:
        lev_base.append(lev_base[-1] + levels(nt) - 1)

    def on_tensor(pe):
        yield 0
        for j in range(8):
            pe.wait_ge(S["d_squares"], j + 1)
            if j >= 4:
                pe.wait_ge(S["d_ln"], j - 3)
            nc.tensor.matmul(ps[j % 4][:, 0:T], m.ones[:, :], sq[:, j, :], start=True, stop=True).then_inc(S["d_norms"], 1)
        for c, (t0, n) in enumerate(TILES):
            yield base[c]
            pe.wait_ge(S["d_gcum"], c + 1)
            nc.tensor.matmul(ps[3][0:n, 0:H], m.cum[0:n, 0:n], gate[0:n, c, :], start=True, stop=True)
            nc.tensor.matmul(ps[4][:, :], m.ones[0:n, :], gcum[0:n, :, :], start=True, stop=True).then_inc(S["d_gc"], 1)
            yield base[c] + 1
            pe.wait_ge(S["d_normed"], 1)
            for h in range(H):
                nc.tensor.transpose(ps[0][0:n, h * P:(h + 1) * P], k4[:, h, t0:t0 + n], m.ident[:, :])
            for h in range(H):
                mm = nc.tensor.transpose(ps[1][0:n, h * P:(h + 1) * P], v4[:, h, t0:t0 + n], m.ident[:, :])
            mm.then_inc(S["d_kv"], 1)
            for h in range(H):
                nc.tensor.matmul(ps[2][0:n, h * P:h * P + n], k4[:, h, t0:t0 + n], k4[:, h, t0:t0 + n], start=True, stop=True)
            pe.wait_ge(S["d_dif"], c + 1)
            for h in range(H):
                mm = nc.tensor.matmul(ps[3][0:n, h * P:h * P + n], q4[:, h, t0:t0 + n], k4[:, h, t0:t0 + n], start=True, stop=True)
            mm.then_inc(S["d_kk"], 1)
            yield base[c] + 2
            pe.wait_ge(S["d_LA"], c + 1)
            for h in range(H):
                nc.tensor.transpose(ps[4][0:n, h * P:h * P + n], Lm[0:n, h, 0:n], m.ident[0:n, 0:n])
            for h in range(H):
                mm = nc.tensor.transpose(ps[0][0:n, h * P:h * P + n], Am[0:n, h, 0:n], m.ident[0:n, 0:n])
            mm.then_inc(S["d_LAT"], 1)
            for v in range(1, levels(n)):
                q = lev_base[c] + v - 1
                last = v == levels(n) - 1
                yield base[c] + 2 + v
                pe.wait_ge(S["d_XY"], q + 1 + c)
                for h in range(H):
                    mm = nc.tensor.matmul(ps[2][0:n, h * P:h * P + n], LM[0:n, v % 2, h, 0:n], X[0:n, h, 0:n], start=True, stop=True)
                mm.then_inc(S["d_LX"], 1)
                yield base[c] + 2.5 + v
                pe.wait_ge(S["d_P"], q + 1)
                for h in range(H):
                    mm = nc.tensor.matmul(ps[4][0:n, h * P:h * P + n], Pm[0:n, h, 0:n], Y[0:n, h, 0:n], start=True, stop=True)
                mm.then_inc(S["d_PY"], 1)
                if not last:
                    for h in range(H):
                        mm = nc.tensor.matmul(ps[3][0:n, h * P:h * P + n], Y[0:n, h, 0:n], Pm[0:n, h, 0:n], start=True, stop=True)
                    mm.then_inc(S["d_YP"], 1)
            yield base[c] + 2 + levels(n)
            pe.wait_ge(S["d_XY"], lev_base[c + 1] + c + 1)
            for h in range(H):
                nc.tensor.matmul(ps[0][:, h * P:h * P + n], kbg[0:n, h, :], Y[0:n, h, 0:n], start=True, stop=True)
            for h in range(H):
                mm = nc.tensor.matmul(ps[1][0:n, h * P:(h + 1) * P], Y[0:n, h, 0:n], vb[0:n, h, :], start=True, stop=True)
            mm.then_inc(S["d_wu"], 1)
            yield base[c] + 2.5 + levels(n)
            pe.wait_ge(S["d_wu_sb"], c + 1)
            for h in range(H):
                mm = nc.tensor.matmul(ps[2][0:n, h * P:(h + 1) * P], wT[:, h, 0:n], St[:, h, :], start=True, stop=True)
            mm.then_inc(S["d_wS"], 1)
            yield base[c] + 3 + levels(n)
            pe.wait_ge(S["d_vnew"], c + 1)
            for h in range(H):
                nc.tensor.matmul(ps[3][:, h * P:h * P + n], St[:, h, :], qd[:, h, 0:n], start=True, stop=False)
                nc.tensor.matmul(ps[3][:, h * P:h * P + n], vn[0:n, h, :], AT[0:n, h, 0:n], start=False, stop=True)
            for h in range(H):
                mm = nc.tensor.matmul(ps[4][:, h * P:(h + 1) * P], kdec[0:n, h, :], vn[0:n, h, :], start=True, stop=True)
            mm.then_inc(S["d_oS"], 1)
            yield base[c] + 4 + levels(n)
            pe.wait_ge(S["d_state"], c + 1)
        yield base[3]
        for h in range(H):
            pe.wait_ge(S["d_osq"], h + 1)
            nc.tensor.matmul(ps[h][:, 0:T], m.ones[:, :], sq[:, h, :], start=True, stop=True).then_inc(S["d_onorm"], 1)

    def on_scalar(act):
        yield 0
        for j in range(8):
            nc.scalar.activation(sq[:, j, :], m.qkvT[:, j, :], ACT.Square).then_inc(S["d_squares"], 1)
        act.wait_ge(S["d_gin"], 1)
        nc.scalar.activation(gt[:, 0, :, :], m.bai[:, :, 0:4], ACT.Exp, scale=-1.0)
        nc.scalar.activation(gt[:, 1, 0, :], m.rows[:, 0:4], ACT.Exp)
        nc.scalar.activation(gt[:, 3, :, :], gt[:, 3, :, :], ACT.Exp, scale=-1.0)
        act.drain()
        nc.scalar.activation(gt[:, 3, :, :], gt[:, 3, :, :], ACT.Ln, bias=1.0).then_inc(S["d_gexp"], 1)
        for j in range(8):
            act.wait_ge(S["d_norms"], j + 1)
            nc.scalar.activation(sq[:, j, :], ps[j % 4][:, 0:T], ACT.Ln, bias=m.eps6[:, 0:1]).then_inc(S["d_ln"], 1)
        act.drain()
        nc.scalar.activation(sq[:, :, :], sq[:, :, :], ACT.Exp, scale=-0.5).then_inc(S["d_rnorm"], 1)
        for c, (t0, n) in enumerate(TILES):
            yield base[c] + 0.4
            act.wait_ge(S["d_dif"], c + 1)
            nc.scalar.activation(dif[0:n, :, 0:n], dif[0:n, :, 0:n], ACT.Exp)
            nc.scalar.activation(eGB[:, :, :], ps[4][:, :].rearrange("p (h c) -> p h c", h=H), ACT.Exp)
            nc.scalar.activation(egc[0:n, 0, :], gc[0:n, :], ACT.Exp)
            nc.scalar.activation(egc[0:n, 1, :], egc[0:n, 3, :], ACT.Exp)
            act.drain().then_inc(S["d_decay"], 1)
            yield base[c] + 2.1 + levels(n)
            act.wait_ge(S["d_wu"], c + 1)
            nc.scalar.activation(wT[:, :, 0:n], b4(ps[0], P, n), ACT.Copy)
            act.drain().then_inc(S["d_wT_sb"], 1)
        yield base[3]
        act.wait_ge(S["d_o"], 1)
        for h in range(H):
            nc.scalar.activation(sq[:, h, :], oT[:, h, :], ACT.Square).then_inc(S["d_osq"], 1)
        for h in range(H):
            act.wait_ge(S["d_onorm"], h + 1)
            nc.scalar.activation(sq[:, 4 + h, :], ps[h][:, 0:T], ACT.Ln, bias=m.eps6[:, 0:1], scale=1.0 / P)
        act.drain()
        nc.scalar.activation(sq[:, 4:8, :], sq[:, 4:8, :], ACT.Exp, scale=-0.5).then_inc(S["d_ornorm"], 1)

    def on_vector(dve):
        yield 0
        dve.wait_ge(S["rows_loaded"], 16 * 6)
        a = m.bai[:, :, 4:8]
        nc.vector.tensor_tensor(gt[:, 2, :, :], a, m.rows[:, 4:8].unsqueeze(1).to_broadcast([P, 3, H]), ALU.add)
        nc.vector.memset(St[:, :, :], 0.0)
        nc.vector.tensor_scalar(m.bai[:, :, 0:4], m.bai[:, :, 0:4], -80.0, None, ALU.max)
        dve.drain()
        nc.vector.tensor_scalar(gt[:, 4, :, :], gt[:, 2, :, :], -1.0, None, ALU.mult)
        dve.drain()
        nc.vector.tensor_tensor(gt[:, 3, :, :], gt[:, 2, :, :], gt[:, 4, :, :], ALU.max)
        dve.drain().then_inc(S["d_gin"], 1)
        dve.wait_ge(S["d_gexp"], 1)
        nc.vector.tensor_scalar(gt[:, 0, :, :], gt[:, 0, :, :], 1.0, None, ALU.add)
        nc.vector.scalar_tensor_tensor(gt[:, 2, :, :], gt[:, 2, :, :], 0.0, gt[:, 3, :, :], ALU.max, ALU.add)
        dve.drain()
        nc.vector.reciprocal(beta[:, :, :], gt[:, 0, :, :])
        nc.vector.scalar_tensor_tensor(gate[:, :, :], gt[:, 2, :, :], -1.0,
                                       gt[:, 1, 0:1, :].to_broadcast([P, 3, H]), ALU.mult, ALU.mult)
        dve.drain()
        dve.wait_ge(S["d_rnorm"], 1)
        nc.vector.scalar_tensor_tensor(q4, q4, float(P) ** -0.5, sq[:, 0:4, :], ALU.mult, ALU.mult)
        nc.vector.tensor_tensor(k4, k4, sq[:, 4:8, :], ALU.mult)
        dve.drain().then_inc(S["d_normed"], 1)
        for c, (t0, n) in enumerate(TILES):
            yield base[c]
            nc.vector.tensor_tensor(gcum[0:n, :, :], over_heads(m.cum[0:n, :], n, P), over_cols(gate[0:n, c, :], n, P), ALU.mult)
            dve.drain().then_inc(S["d_gcum"], 1)
            yield base[c] + 0.2
            dve.wait_ge(S["d_gc"], c + 1)
            GB = ps[4][:, :].rearrange("p (h c) -> p h c", h=H)
            nc.vector.tensor_copy(gc[0:n, :], ps[3][0:n, 0:H])
            dve.drain()
            nc.vector.tensor_tensor(dif[0:n, :, 0:n], over_cols(gc[0:n, :], n, n), GB[0:n, :, 0:n], ALU.subtract)
            nc.vector.tensor_tensor(egc[0:n, 3, :].unsqueeze(2), GB[0:n, :, n - 1:n], gc[0:n, :].unsqueeze(2), ALU.subtract)
            dve.drain()
            nc.vector.tensor_scalar(dif[0:n, :, 0:n], dif[0:n, :, 0:n], 0.0, None, ALU.min)
            dve.drain().then_inc(S["d_dif"], 1)
            yield base[c] + 1
            dve.wait_ge(S["d_decay"], c + 1)
            nc.vector.tensor_tensor(egc[0:n, 2, :], egc[0:n, 0, :], beta[0:n, c, :], ALU.mult)
            nc.vector.tensor_tensor(qd[:, :, 0:n], q4[:, :, t0:t0 + n], eGB[:, :, 0:n], ALU.mult)
            dve.drain()
            dve.wait_ge(S["d_kv"], c + 1)
            nc.vector.tensor_tensor(kbg[0:n, :, :], b4(ps[0], n), over_cols(egc[0:n, 2, :], n, P), ALU.mult)
            nc.vector.tensor_tensor(kdec[0:n, :, :], b4(ps[0], n), over_cols(egc[0:n, 1, :], n, P), ALU.mult)
            nc.vector.tensor_tensor(vb[0:n, :, :], b4(ps[1], n), over_cols(beta[0:n, c, :], n, P), ALU.mult)
            dve.wait_ge(S["d_kk"], c + 1)
            nc.vector.tensor_tensor(Lm[0:n, :, 0:n], b4(ps[2], n, n), dif[0:n, :, 0:n], ALU.mult)
            nc.vector.tensor_tensor(Am[0:n, :, 0:n], b4(ps[3], n, n), dif[0:n, :, 0:n], ALU.mult)
            dve.drain()
            nc.vector.tensor_tensor(Lm[0:n, :, 0:n], Lm[0:n, :, 0:n], over_heads(m.strict[0:n, 0:n], n, n), ALU.mult)
            nc.vector.tensor_tensor(Am[0:n, :, 0:n], Am[0:n, :, 0:n], over_heads(m.incl[0:n, 0:n], n, n), ALU.mult)
            dve.drain()
            nc.vector.tensor_tensor(Lm[0:n, :, 0:n], Lm[0:n, :, 0:n], over_cols(beta[0:n, c, :], n, n), ALU.mult)
            dve.drain().then_inc(S["d_LA"], 1)
            idn = over_heads(m.ident[0:n, 0:n], n, n)
            nc.vector.tensor_tensor(X[0:n, :, 0:n], Lm[0:n, :, 0:n], over_heads(m.level0[0:n, 0:n], n, n), ALU.mult)
            dve.drain()
            nc.vector.tensor_tensor(X[0:n, :, 0:n], idn, X[0:n, :, 0:n], ALU.subtract)
            yield base[c] + 2
            dve.wait_ge(S["d_LAT"], c + 1)
            nc.vector.tensor_copy(LT[0:n, :, 0:n], b4(ps[4], n, n))
            nc.vector.tensor_copy(AT[0:n, :, 0:n], b4(ps[0], n, n))
            dve.drain()
            nc.vector.tensor_tensor(Y[0:n, :, 0:n], LT[0:n, :, 0:n], over_heads(m.levelsT[0:n, 0, 0:n], n, n), ALU.mult)
            nc.vector.tensor_tensor(LM[0:n, 1, :, 0:n], LT[0:n, :, 0:n], over_heads(m.levelsT[0:n, 1, 0:n], n, n), ALU.mult)
            dve.drain()
            nc.vector.tensor_tensor(Y[0:n, :, 0:n], idn, Y[0:n, :, 0:n], ALU.subtract)
            dve.drain().then_inc(S["d_XY"], 1)
            for v in range(1, levels(n)):
                q = lev_base[c] + v - 1
                last = v == levels(n) - 1
                yield base[c] + 2.2 + v
                dve.wait_ge(S["d_LX"], q + 1)
                nc.vector.tensor_copy(Pm[0:n, :, 0:n], b4(ps[2], n, n))
                dve.drain().then_inc(S["d_P"], 1)
                if not last:
                    nc.vector.tensor_tensor(LM[0:n, (v + 1) % 2, :, 0:n], LT[0:n, :, 0:n], over_heads(m.levelsT[0:n, v + 1, 0:n], n, n), ALU.mult)
                yield base[c] + 2.7 + v
                dve.wait_ge(S["d_PY"], q + 1)
                if not last:
                    dve.wait_ge(S["d_YP"], q - c + 1)
                    nc.vector.tensor_tensor(X[0:n, :, 0:n], X[0:n, :, 0:n], b4(ps[3], n, n), ALU.subtract)
                nc.vector.tensor_tensor(Y[0:n, :, 0:n], Y[0:n, :, 0:n], b4(ps[4], n, n), ALU.subtract)
                dve.drain().then_inc(S["d_XY"], 1)
            yield base[c] + 2.2 + levels(n)
            dve.wait_ge(S["d_wu"], c + 1)
            nc.vector.tensor_copy(u[0:n, :, :], b4(ps[1], n))
            dve.drain()
            dve.wait_ge(S["d_wT_sb"], c + 1)
            dve.drain().then_inc(S["d_wu_sb"], 1)
            yield base[c] + 2.7 + levels(n)
            dve.wait_ge(S["d_wS"], c + 1)
            nc.vector.tensor_tensor(vn[0:n, :, :], u[0:n, :, :], b4(ps[2], n), ALU.subtract)
            dve.drain().then_inc(S["d_vnew"], 1)
            yield base[c] + 3.5 + levels(n)
            dve.wait_ge(S["d_oS"], c + 1)
            nc.vector.tensor_copy(oT[:, :, t0:t0 + n], b4(ps[3], P, n))
            nc.vector.tensor_tensor(St[:, :, :], St[:, :, :], eGB[:, :, n - 1:n].to_broadcast([P, H, P]), ALU.mult)
            dve.drain()
            nc.vector.tensor_tensor(St[:, :, :], St[:, :, :], b4(ps[4], P), ALU.add)
            dve.drain().then_inc(S["d_state"], 1)
        yield base[3]
        nc.vector.tensor_scalar(m.zT[:, :, :], m.zT[:, :, :], m.prmT[:, 48:49], None, ALU.mult)
        dve.drain().then_inc(S["d_o"], 1)
        dve.wait_ge(S["d_ornorm"], 1)
        nc.vector.tensor_tensor(oT[:, :, :], oT[:, :, :], sq[:, 4:8, :], ALU.mult)
        dve.drain()
        nc.vector.tensor_tensor(m.mixT[:, 0:4, :], oT[:, :, :], m.zT[:, :, :], ALU.mult)

    return on_tensor, on_scalar, on_vector


def sparse_attention(nc, m, S, ctx):
    ps = m.ps
    NH = 8
    def sb(name, shape):
        return ctx.enter_context(nc.sbuf_tensor(name, shape, F32))

    score = sb("s_score", [P, T])
    work = sb("s_work", [P, T])
    top = sb("s_top", [P, 8])
    keep = sb("s_keep", [P, T])
    bias = sb("s_bias", [P, T])
    mx = sb("s_mx", [P, NH])
    den = sb("s_den", [P, NH])
    room, at = m.W[:, SLOTS - 1, :], NH * T
    lg = room[:, 0:at].rearrange("p (h t) -> p h t", h=NH)
    rel = room[:, at:at + 2 * T].rearrange("p (h t) -> p h t", h=2)
    pT = room[:, at + 2 * T:at + 2 * T + 6 * P].rearrange("p (h j t) -> p h j t", h=2, j=3)

    def order(c, k):
        return 3 + SPARSE_STEP * (35 * c + k)

    def half(h):
        return slice(64 * (h % 2), 64 * (h % 2) + 64)

    def on_tensor(pe):
        for c, (t0, n) in enumerate(TILES):
            ns = t0 + n
            for h in range(NH):
                q = c * NH + h
                yield order(c, h)
                if c and h == 0:
                    pe.wait_ge(S["s_out"], 4 * c)
                if h >= 2:
                    pe.wait_ge(S["s_rel"], q - 1)
                nc.tensor.matmul(ps[6 + h % 2][0:n, 0:ns], m.iqT[half(h), h // 2, t0:t0 + n], m.ikT[half(h), 0:ns],
                                 start=True, stop=True).then_inc(S["s_idx"], 1)
            for h in range(NH):
                q = c * NH + h
                yield order(c, 16 + h)
                pe.wait_ge(S["s_rel"], c * NH + NH)
                if h >= 2:
                    pe.wait_ge(S["s_logit_sb"], q - 1)
                nc.tensor.matmul(ps[6 + h % 2][0:n, 0:ns], m.sqT[half(h), h // 2, t0:t0 + n], m.skT[half(h), h // 2, 0:ns],
                                 start=True, stop=True).then_inc(S["s_logit"], 1)
            yield order(c, 27)
            pe.wait_ge(S["s_prob"], c + 1)
            for h in range(NH):
                q = c * NH + h
                yield order(c, 27 + h)
                if q >= 2:
                    pe.wait_ge(S["s_pT_sb"], q - 1)
                for j in range(c + 1):
                    s0, w = TILES[j]
                    mm = nc.tensor.transpose(ps[6 + h % 2][0:w, j * P:j * P + n], lg[0:n, h, s0:s0 + w], m.ident[0:n, 0:n])
                mm.then_inc(S["s_pT"], 1)
                yield order(c, 27.6 + h)
                pe.wait_ge(S["s_pT_sb"], q + 1)
                if h % 2 == 0 and q >= 2:
                    pe.wait_ge(S["s_out"], q // 2)
                for j in range(c + 1):
                    s0, w = TILES[j]
                    mm = nc.tensor.matmul(ps[5][half(h), 0:n], m.sv[0:w, j, h * 64:(h + 1) * 64],
                                          pT[0:w, h % 2, j, 0:n], start=(j == 0), stop=(j == c))
                mm.then_inc(S["s_pv"], 1)

    def on_scalar(act):
        for c, (t0, n) in enumerate(TILES):
            ns = t0 + n
            for h in range(NH):
                q = c * NH + h
                yield order(c, h + 0.3)
                act.wait_ge(S["s_idx"], q + 1)
                if q >= 2:
                    act.wait_ge(S["s_acc"], q - 1)
                nc.scalar.activation(rel[0:n, h % 2, 0:ns], ps[6 + h % 2][0:n, 0:ns], ACT.Relu, scale=0.125).then_inc(S["s_rel"], 1)
            yield order(c, 25)
            act.wait_ge(S["s_max"], c + 1)
            for h in range(NH):
                nc.scalar.activation(lg[0:n, h, 0:ns], lg[0:n, h, 0:ns], ACT.Exp, bias=mx[0:n, h:h + 1],
                                     accum_out=den[0:n, h:h + 1])
            act.drain().then_inc(S["s_exp"], 1)
            for h in range(1, NH, 2):
                q = c * NH + h
                yield order(c, 27.9 + h)
                act.wait_ge(S["s_pv"], q + 1)
                nc.scalar.activation(m.mixT[:, 4 + h // 2, t0:t0 + n], ps[5][:, 0:n], ACT.Copy).then_inc(S["s_out"], 1)

    def on_vector(dve):
        for c, (t0, n) in enumerate(TILES):
            ns = t0 + n
            caus = m.causal[0:n, c, 0:ns]
            for h in range(NH):
                q = c * NH + h
                yield order(c, h + 0.6)
                dve.wait_ge(S["s_rel"], q + 1)
                wi = m.bai[0:n, c, 8 + h:9 + h]
                if h == 0:
                    nc.vector.tensor_scalar(score[0:n, 0:ns], rel[0:n, 0, 0:ns], wi, None, ALU.mult)
                else:
                    nc.vector.scalar_tensor_tensor(score[0:n, 0:ns], rel[0:n, h % 2, 0:ns], wi, score[0:n, 0:ns], ALU.mult, ALU.add)
                dve.drain().then_inc(S["s_acc"], 1)
            yield order(c, 8)
            nc.vector.tensor_scalar(bias[0:n, 0:ns], caus, -1.0, BIG, ALU.add, ALU.mult)
            nc.vector.tensor_tensor(score[0:n, 0:ns], score[0:n, 0:ns], caus, ALU.mult)
            dve.drain()
            nc.vector.tensor_tensor(work[0:n, 0:ns], score[0:n, 0:ns], bias[0:n, 0:ns], ALU.add)
            dve.drain()
            for r in range(TOP_K // 8):
                yield order(c, 8 + r)
                nc.vector.max(top[0:n, :], work[0:n, 0:ns])
                dve.drain()
                nc.vector.match_replace(work[0:n, 0:ns], top[0:n, :], work[0:n, 0:ns], -3 * BIG)
                dve.drain()
            yield order(c, 16)
            nc.vector.scalar_tensor_tensor(keep[0:n, 0:ns], work[0:n, 0:ns], -2 * BIG, caus, ALU.is_lt, ALU.mult)
            dve.drain()
            nc.vector.tensor_scalar(bias[0:n, 0:ns], keep[0:n, 0:ns], -1.0, BIG, ALU.add, ALU.mult)
            dve.drain()
            if c:
                dve.wait_ge(S["s_pT"], c * NH)
            for h in range(NH):
                q = c * NH + h
                yield order(c, 16.5 + h)
                dve.wait_ge(S["s_logit"], q + 1)
                nc.vector.scalar_tensor_tensor(lg[0:n, h, 0:ns], ps[6 + h % 2][0:n, 0:ns], 0.125, bias[0:n, 0:ns], ALU.mult, ALU.add).then_inc(S["s_logit_sb"], 1)
            yield order(c, 24)
            dve.drain()
            nc.vector.tensor_reduce(mx[0:n, :], lg[0:n, :, 0:ns], AX.X, ALU.max)
            dve.drain()
            nc.vector.tensor_scalar(mx[0:n, :], mx[0:n, :], -1.0, None, ALU.mult)
            dve.drain().then_inc(S["s_max"], 1)
            yield order(c, 26)
            dve.wait_ge(S["s_exp"], c + 1)
            nc.vector.reciprocal(den[0:n, :], den[0:n, :])
            dve.drain()
            nc.vector.tensor_tensor(lg[0:n, :, 0:ns], lg[0:n, :, 0:ns], den[0:n, :].unsqueeze(2).to_broadcast([n, NH, ns]), ALU.mult)
            dve.drain().then_inc(S["s_prob"], 1)
            for h in range(NH):
                q = c * NH + h
                yield order(c, 27.3 + h)
                dve.wait_ge(S["s_pT"], q + 1)
                if q >= 2:
                    dve.wait_ge(S["s_pv"], q - 1)
                for j in range(c + 1):
                    w = TILES[j][1]
                    i = nc.vector.tensor_copy(pT[0:w, h % 2, j, 0:n], ps[6 + h % 2][0:w, j * P:j * P + n])
                i.then_inc(S["s_pT_sb"], 1)

    return on_tensor, on_scalar, on_vector

SPARSE_STEP = 0.3


def interleave(*streams):
    order = [next(s) for s in streams]
    while any(o is not None for o in order):
        i = min((o, i) for i, o in enumerate(order) if o is not None)[1]
        order[i] = next(streams[i], None)


def linear_and_sparse(nc, m, S):
    with ExitStack() as ctx:
        linear = delta_rule(nc, m, S, ctx)
        sparse = sparse_attention(nc, m, S, ctx)
        with nc.Block() as block:
            @block.tensor
            def _(pe):
                interleave(linear[0](pe), sparse[0](pe))

            @block.scalar
            def _(act):
                interleave(linear[1](act), sparse[1](act))

            @block.vector
            def _(dve):
                interleave(linear[2](dve), sparse[2](dve))




def layer_norm_steps(nc, m, signals, g0, b0):
    ready, mean, squares, var, rstd = signals
    centred, scratch = m.ln_x, m.ln_sq

    def on_tensor(pe):
        pe.wait_ge(ready, 1)
        for k in range(KT):
            mm = nc.tensor.matmul(m.ps[0][:, 0:T], m.mean_w[:, :], m.hT[:, k, :], start=(k == 0), stop=(k == KT - 1))
        mm.then_inc(mean, 1)
        for k in range(KT):
            pe.wait_ge(squares, k + 1)
            mm = nc.tensor.matmul(m.ps[1][:, 0:T], m.mean_w[:, :], scratch[:, k, :], start=(k == 0), stop=(k == KT - 1))
        mm.then_inc(var, 1)

    def on_scalar(act, centred_ready):
        for k in range(KT):
            act.wait_ge(centred_ready, k + 1)
            nc.scalar.activation(scratch[:, k, :], centred[:, k, :], ACT.Square).then_inc(squares, 1)
        act.wait_ge(var, 1)
        nc.scalar.activation(m.rstd[:, :], m.ps[1][:, 0:T], ACT.Ln, bias=m.eps5[:, 0:1])
        act.drain()
        nc.scalar.activation(m.rstd[:, :], m.rstd[:, :], ACT.Exp, scale=-0.5).then_inc(rstd, 1)

    def on_vector(dve, centred_ready):
        dve.wait_ge(mean, 1)
        for k in range(KT):
            nc.vector.tensor_tensor(centred[:, k, :], m.hT[:, k, :], m.ps[0][:, 0:T], ALU.subtract).then_inc(centred_ready, 1)
        dve.wait_ge(rstd, 1)
        for k in range(KT):
            nc.vector.scalar_tensor_tensor(centred[:, k, :], centred[:, k, :], m.prmT[:, g0 + k:g0 + k + 1], m.rstd[:, :], ALU.mult, ALU.mult)
        dve.drain()
        for k in range(KT):
            nc.vector.tensor_scalar(m.hT[:, k, :], centred[:, k, :], m.prmT[:, b0 + k:b0 + k + 1], None, ALU.add)

    return on_tensor, on_scalar, on_vector


def mix_and_route(nc, m, l, A, S):
    W, ring, ps = m.W, m.ring, m.ps
    w_out = A["w_out"].rearrange("l (k p) n -> l p k n", p=P)
    with ExitStack() as ctx:
        def sb(name, shape):
            return ctx.enter_context(nc.sbuf_tensor(name, shape, F32))

        m.ln_x = sb("ln_x", [P, KT, T])
        m.ln_sq = sb("ln_sq", [P, KT, T])
        m.rstd = sb("ln_rstd", [P, T])
        r = sb("r_tmp", [P, 12, 32])
        both = sb("r_both", [P, 3, 32])
        pick = sb("r_pick", [P, 3, 2, 32])
        val = sb("r_val", [P, 3, 4])
        spread = sb("r_spread", [P, 3, 4, P])
        slot0 = sb("r_slot0", [P, 32])
        place = sb("r_place", [P, 3, 2, 32])
        blocks = sb("r_blocks", [32, 8])
        few = sb("r_few", [32, 16])
        nbx = sb("r_nbx", [32, P])
        ended = sb("r_ended", [32, MAX_GROUPS * BLOCKS_GROUP])
        row = sb("r_row", [1, 80])
        NB_ROW = MAX_GROUPS * BLOCKS_GROUP
        on_pe, on_act, on_dve = layer_norm_steps(nc, m, (S["n1_ready"], S["n1_mean"], S["n1_squares"], S["n1_var"], S["n1_rstd"]), 49, 57)

        with nc.Block() as block:
            @block.sync
            def _(sp):
                for c in range(2):
                    name = f"out{c}"
                    sp.wait_ge(*ring.freed(name))
                    slot = ring.chunks[name][0]
                    w = W[:, slot, :].rearrange("p (k n) -> p k n", k=KT)
                    sp.dma_start(w, w_out[l, :, :, 512 * c:512 * c + 512]).then_inc(ring.loaded[slot], 16)

            @block.tensor
            def _(pe):
                for n in range(KT):
                    c = n // 4
                    if n % 4 == 0:
                        pe.wait_ge(*ring.arrived(f"out{c}"))
                    if n >= 4:
                        pe.wait_ge(S["o_added"], n - 3)
                    w = W[:, ring.chunks[f"out{c}"][0], :].rearrange("p (k n) -> p k n", k=KT)
                    for k in range(KT):
                        mm = nc.tensor.matmul(ps[n % 4][:, 0:T], w[:, k, n % 4 * P:n % 4 * P + P], m.mixT[:, k, :], start=(k == 0), stop=(k == KT - 1))
                    mm.then_inc(S["o_mm"], 1)
                    if n % 4 == 3:
                        nc.tensor.drain().then_inc(ring.used, 1)
                on_pe(pe)
                pe.wait_ge(S["n1_done"], 1)
                for c, (t0, n) in enumerate(TILES):
                    for k in range(KT):
                        mm = nc.tensor.matmul(ps[2 + c][0:n, 0:36], m.hT[:, k, t0:t0 + n], m.w_route[:, k, :], start=(k == 0), stop=(k == KT - 1))
                    mm.then_inc(S["r_logit"], 1)
                for c, (t0, n) in enumerate(TILES):
                    for y in range(2):
                        q = 2 * c + y
                        if q >= 2:
                            pe.wait_ge(S["r_rows_sb"], q - 1)
                        for k in range(4):
                            mm = nc.tensor.transpose(ps[q % 2][0:n, k * P:(k + 1) * P], m.hT[:, 4 * y + k, t0:t0 + n], m.ident[:, :])
                        mm.then_inc(S["r_rows"], 1)
                pe.wait_ge(S["r_masks"], 1)
                for c, (t0, n) in enumerate(TILES):
                    mm = nc.tensor.matmul(ps[5][0:32, 0:1], both[0:n, c, :], m.ones[0:n, 0:1], start=(c == 0), stop=(c == 2))
                mm.then_inc(S["r_counts"], 1)
                for c, (t0, n) in enumerate(TILES):
                    for b in range(c + 1):
                        lhs = m.cum[0:n, 0:n] if b == c else m.ones[:, 0:n]
                        mm = nc.tensor.matmul(ps[6][0:n, 32 * c:32 * c + 32], lhs, both[0:(n if b == c else P), b, :], start=(b == 0), stop=(b == c))
                mm.then_inc(S["r_ranks"], 1)
                pe.wait_ge(S["r_nb"], 1)
                nc.tensor.matmul(ps[7][:, 0:32], nbx[:, :], m.before[:, :], start=True, stop=True)
                nc.tensor.matmul(ps[7][0:32, 32:33], m.before[:, :], blocks[:, 1:2], start=True, stop=True)
                nc.tensor.matmul(ps[7][0:1, 40:41], blocks[:, 1:2], m.ones[0:32, 0:1], start=True, stop=True).then_inc(S["r_starts"], 1)
                pe.wait_ge(S["r_spread"], 1)
                nc.tensor.matmul(ps[7][0:1, 64:64 + NB_ROW], m.ones[0:32, 0:1], ended[:, :], start=True, stop=True)
                for v in range(4):
                    for c, (t0, n) in enumerate(TILES):
                        mm = nc.tensor.matmul(ps[v][:, t0:t0 + n], spread[0:n, c, v, :], m.ident[0:n, 0:n], start=True, stop=True)
                mm.then_inc(S["r_table"], 1)

            @block.scalar
            def _(act):
                on_act(act, S["n1_centred"])
                for c, (t0, n) in enumerate(TILES):
                    act.wait_ge(S["r_exp_in"], c + 1)
                    nc.scalar.activation(r[0:n, 3, 0:4], r[0:n, 0, 0:4], ACT.Exp, bias=r[0:n, 2, 0:1], accum_out=r[0:n, 2, 1:2])
                    nc.scalar.activation(r[0:n, 2, 4:5], r[0:n, 2, 3:4], ACT.Exp)
                    act.drain().then_inc(S["r_exp"], 1)

            @block.vector
            def _(dve):
                for n in range(KT):
                    dve.wait_ge(S["o_mm"], n + 1)
                    nc.vector.scalar_tensor_tensor(m.hT[:, n, :], m.hT[:, n, :], ALPHA, ps[n % 4][:, 0:T], ALU.mult, ALU.add).then_inc(S["o_added"], 1)
                dve.drain().then_inc(S["n1_ready"], 1)
                on_dve(dve, S["n1_centred"])
                dve.drain().then_inc(S["n1_done"], 1)
                nc.vector.tensor_scalar(m.yT[:, :, :], m.hT[:, :, :], ALPHA, None, ALU.mult)
                for c, (t0, n) in enumerate(TILES):
                    dve.wait_ge(S["r_logit"], c + 1)
                    lg, col = r[0:n, 0, :], r[0:n, 2, :]
                    el = r[0:n, 1, :]
                    nc.vector.tensor_tensor(lg[:, 0:4], ps[2 + c][0:n, 0:4], m.rows[0:n, 8:12], ALU.add)
                    nc.vector.tensor_tensor(el, ps[2 + c][0:n, 4:36], m.rows[0:n, 12:44], ALU.add)
                    dve.drain()
                    nc.vector.tensor_reduce(col[:, 8:9], lg[:, 0:4], AX.X, ALU.max)
                    dve.drain()
                    nc.vector.scalar_tensor_tensor(r[0:n, 4, 0:4], lg[:, 0:4], col[:, 8:9], m.rank4[0:n, :], ALU.is_equal, ALU.mult)
                    nc.vector.tensor_scalar(col[:, 0:1], col[:, 8:9], -1.0, None, ALU.mult)
                    dve.drain()
                    nc.vector.tensor_reduce(col[:, 9:10], r[0:n, 4, 0:4], AX.X, ALU.max)
                    dve.drain()
                    nc.vector.tensor_scalar(r[0:n, 5, 0:4], r[0:n, 4, 0:4], col[:, 9:10], None, ALU.is_equal)
                    dve.drain()
                    e48 = el.rearrange("p (g e) -> p g e", g=4)
                    g48 = r[0:n, 5, 0:4].unsqueeze(2).to_broadcast([n, 4, 8])
                    nc.vector.tensor_tensor(r[0:n, 6, :].rearrange("p (g e) -> p g e", g=4), e48, g48, ALU.mult)
                    dve.drain()
                    nc.vector.tensor_reduce(r[0:n, 7, 0:8], r[0:n, 6, :].rearrange("p (g e) -> p e g", g=4), AX.X, ALU.add)
                    dve.drain()
                    for s in range(2):
                        x = r[0:n, 7, 8 * s:8 * s + 8]
                        nc.vector.tensor_reduce(col[:, 10 + s:11 + s], x, AX.X, ALU.max)
                        dve.drain()
                        nc.vector.scalar_tensor_tensor(r[0:n, 8, 0:8], x, col[:, 10 + s:11 + s], m.rank8[0:n, :], ALU.is_equal, ALU.mult)
                        dve.drain()
                        nc.vector.tensor_reduce(col[:, 12:13], r[0:n, 8, 0:8], AX.X, ALU.max)
                        dve.drain()
                        nc.vector.tensor_scalar(r[0:n, 9, 8 * s:8 * s + 8], r[0:n, 8, 0:8], col[:, 12:13], None, ALU.is_equal)
                        dve.drain()
                        if s == 0:
                            nc.vector.scalar_tensor_tensor(r[0:n, 7, 8:16], r[0:n, 9, 0:8], -BIG, x, ALU.mult, ALU.add)
                            dve.drain()
                    nc.vector.tensor_tensor(col[:, 3:4], col[:, 11:12], col[:, 10:11], ALU.subtract)
                    dve.drain().then_inc(S["r_exp_in"], 1)
                    dve.wait_ge(S["r_exp"], c + 1)
                    nc.vector.scalar_tensor_tensor(col[:, 13:14], col[:, 4:5], 1.0, col[:, 1:2], ALU.add, ALU.mult)
                    dve.drain()
                    nc.vector.reciprocal(col[:, 14:15], col[:, 13:14])
                    dve.drain()
                    nc.vector.tensor_copy(val[0:n, c, 2:3], col[:, 14:15])
                    nc.vector.tensor_tensor(val[0:n, c, 3:4], col[:, 14:15], col[:, 4:5], ALU.mult)
                    for s in range(2):
                        nc.vector.tensor_tensor(pick[0:n, c, s, :].rearrange("p (g e) -> p g e", g=4),
                                                r[0:n, 9, 8 * s:8 * s + 8].unsqueeze(1).to_broadcast([n, 4, 8]), g48, ALU.mult)
                    dve.drain()
                    nc.vector.tensor_tensor(both[0:n, c, :], pick[0:n, c, 0, :], pick[0:n, c, 1, :], ALU.add)
                    dve.drain()
                dve.drain().then_inc(S["r_masks"], 1)
                for q in range(6):
                    n = TILES[q // 2][1]
                    dve.wait_ge(S["r_rows"], q + 1)
                    nc.vector.tensor_copy(m.rowsH[0:n, q // 2, 512 * (q % 2):512 * (q % 2) + 512], ps[q % 2][0:n, :]).then_inc(S["r_rows_sb"], 1)
                dve.wait_ge(S["r_counts"], 1)
                nc.vector.tensor_copy(blocks[:, 0:1], ps[5][0:32, 0:1])
                nc.vector.tensor_scalar(few[:, :], m.count[0:32, 0:16], float(SLOTS_BLOCK), None, ALU.mult)
                dve.drain()
                nc.vector.tensor_scalar(few[:, :], few[:, :], blocks[:, 0:1], None, ALU.is_lt)
                dve.drain()
                nc.vector.tensor_reduce(blocks[:, 1:2], few[:, :], AX.X, ALU.add)
                dve.drain()
                nc.vector.tensor_scalar(nbx[:, :], m.ones[0:32, :], blocks[:, 1:2], None, ALU.mult)
                dve.drain().then_inc(S["r_nb"], 1)
                dve.wait_ge(S["r_starts"], 1)
                nc.vector.tensor_scalar(slot0[:, :], ps[7][:, 0:32], float(SLOTS_BLOCK), -1.0, ALU.mult, ALU.add)
                nc.vector.tensor_tensor(blocks[:, 3:4], blocks[:, 1:2], ps[7][0:32, 32:33], ALU.add)
                nc.vector.tensor_copy(row[:, 64:65], ps[7][0:1, 40:41])
                dve.drain()
                nc.vector.tensor_scalar(ended[:, :], m.count[0:32, 0:NB_ROW], blocks[:, 3:4], None, ALU.is_ge)
                nc.vector.tensor_scalar(row[:, 0:16], m.count[0:1, 0:16], float(BLOCKS_GROUP), None, ALU.mult)
                dve.drain()
                nc.vector.tensor_scalar(row[:, 0:16], row[:, 0:16], row[:, 64:65], None, ALU.is_lt)
                dve.drain()
                nc.vector.tensor_reduce(row[:, 65:66], row[:, 0:16], AX.X, ALU.add)
                dve.wait_ge(S["r_ranks"], 1)
                for c, (t0, n) in enumerate(TILES):
                    nc.vector.tensor_tensor(place[0:n, c, 0, :], slot0[0:n, :], ps[6][0:n, 32 * c:32 * c + 32], ALU.add)
                    dve.drain()
                    nc.vector.tensor_copy(place[0:n, c, 1, :], place[0:n, c, 0, :])
                    dve.drain()
                    nc.vector.tensor_tensor(place[0:n, c, :, :], place[0:n, c, :, :], pick[0:n, c, :, :], ALU.mult)
                    dve.drain()
                    nc.vector.tensor_reduce(val[0:n, c, 0:2], place[0:n, c, :, :], AX.X, ALU.add)
                    dve.drain()
                    nc.vector.tensor_copy(m.slot_of[0:n, c, :], val[0:n, c, 0:2])
                    nc.vector.tensor_tensor(spread[0:n, c, :, :], m.ones[0:n, :].unsqueeze(1).to_broadcast([n, 4, P]),
                                            val[0:n, c, :].unsqueeze(2).to_broadcast([n, 4, P]), ALU.mult)
                dve.drain().then_inc(S["r_spread"], 1)
                dve.wait_ge(S["r_table"], 1)
                nc.vector.tensor_scalar(row[:, 0:NB_ROW], ps[7][0:1, 64:64 + NB_ROW], float(EXPERTS - 1), None, ALU.min)
                dve.drain()
                nc.vector.tensor_copy(m.table[:, 0:NB_ROW], row[:, 0:NB_ROW])
                nc.vector.tensor_copy(m.table[:, NB_ROW:NB_ROW + 1], row[:, 65:66])
                for v in range(4):
                    nc.vector.tensor_copy(m.token_row[:, v, :], ps[v][:, 0:T])


def experts(nc, m, l, A, S):
    ring, ps = m.ring, m.ps
    w1 = A["w1"].rearrange("l e (k p) f -> l e p k f", p=P)
    w3 = A["w3"].rearrange("l e (k p) f -> l e p k f", p=P)
    w2 = A["w2"].rearrange("l e (k p) d -> l e p k d", p=P)
    NB_ROW = MAX_GROUPS * BLOCKS_GROUP
    G = BLOCKS_GROUP
    with ExitStack() as ctx:
        def sb(name, shape):
            return ctx.enter_context(nc.sbuf_tensor(name, shape, F32))

        Wu = m.W[:, :, :].rearrange("p j (k n) -> p j k n", k=KT)
        Wd = sb("e_Wd", [P, G, 2, D])
        eq = sb("e_eq", [P, 3, 2, P])
        sel = sb("e_sel", [P, 3, P])
        back = sb("e_back", [P, 3, T])
        slot = sb("e_slot", [P, 1])
        hs = sb("e_hs", [P, KT, P])
        sil = sb("e_sil", [P, DE])
        hid = sb("e_hid", [P, DE])
        hidT = sb("e_hidT", [P, 2, P])
        y = sb("e_y", [P, D])
        m.ln_x = sb("ln2_x", [P, KT, T])
        m.ln_sq = sb("ln2_sq", [P, KT, T])
        m.rstd = sb("ln2_rstd", [P, T])
        on_pe, on_act, on_dve = layer_norm_steps(nc, m, (S["n2_ready"], S["n2_mean"], S["n2_squares"], S["n2_var"], S["n2_rstd"]), 65, 73)

        def groups(eng):
            return eng.value_load(m.table[0:1, NB_ROW:NB_ROW + 1], min_val=1, max_val=MAX_GROUPS)

        with nc.Block() as block:
            @block.sync
            def _(sp):
                n = groups(sp)
                with sp.Fori(0, n) as g:
                    ids = []
                    for j in range(G):
                        e = sp.value_load(m.table[0:1, bass.ds(g * G + j, 1)], min_val=0, max_val=EXPERTS - 1)
                        ids.append(e)
                        sp.wait_ge(S["e_up_free"], g * G + (j + 1))
                        sp.dma_start(Wu[:, j, :, 0:DE], w1[l, e, :, :, :]).then_inc(S[f"e_up_in{j}"], 16)
                        sp.dma_start(Wu[:, j, :, DE:2 * DE], w3[l, e, :, :, :]).then_inc(S[f"e_up_in{j}"], 16)
                    for j in range(G):
                        sp.wait_ge(S["e_down_free"], g * G + (j + 1))
                        sp.dma_start(Wd[:, j, :, :], w2[l, ids[j], :, :, :]).then_inc(S[f"e_down_in{j}"], 16)

            @block.tensor
            def _(pe):
                pe.drain().then_inc(S["e_up_free"], G)
                pe.drain().then_inc(S["e_down_free"], G)
                n = groups(pe)

                def gather(count):
                    pe.wait_ge(S["e_sel"], count)
                    for d in range(KT):
                        o = ps[d // 4][:, (d % 4) * P:(d % 4 + 1) * P]
                        for c, (t0, nt) in enumerate(TILES):
                            mm = nc.tensor.matmul(o, m.rowsH[0:nt, c, d * P:(d + 1) * P], sel[0:nt, c, :], start=(c == 0), stop=(c == 2))
                        if d == 3:
                            mm.then_inc(S["e_gather0"], 1)
                    mm.then_inc(S["e_gather1"], 1)

                def scatter(g):
                    pe.wait_ge(S["e_back"], g + 1)
                    pe.wait_ge(S["e_y"], g + 1)
                    for d in range(KT):
                        pe.wait_ge(S["e_y_free"], g * KT + (d + 1))
                        nc.tensor.matmul(ps[6 + d % 2][:, 0:T], y[:, d * P:(d + 1) * P], back[:, 0, :], start=True, stop=True).then_inc(S["e_part"], 1)

                gather(1)
                with pe.Fori(0, n) as g:
                    for h in range(2):
                        pe.wait_ge(S[f"e_hs{h}"], g + 1)
                    for j in range(G):
                        pe.wait_ge(S[f"e_up_in{j}"], g * 32 + 32)
                        for k in range(KT):
                            mm = nc.tensor.matmul(ps[2][32 * j:32 * j + 32, :], hs[:, k, 32 * j:32 * j + 32], Wu[:, j, k, :],
                                                  start=(k == 0), stop=(k == KT - 1))
                        mm.then_inc(S["e_up_free"], 1)
                    nc.tensor.drain().then_inc(S["e_up"], 1)
                    gather(g + 2)
                    pe.wait_ge(S["e_hid"], g + 1)
                    for f in range(2):
                        mm = nc.tensor.transpose(ps[3][:, f * P:(f + 1) * P], hid[:, f * P:(f + 1) * P], m.ident[:, :])
                    mm.then_inc(S["e_turn"], 1)
                    scatter(g)
                    pe.wait_ge(S["e_hidT"], g + 1)
                    for j in range(G):
                        pe.wait_ge(S[f"e_down_in{j}"], g * 16 + 16)
                        for h in range(2):
                            for f in range(2):
                                mm = nc.tensor.matmul(ps[4 + h][32 * j:32 * j + 32, :], hidT[:, f, 32 * j:32 * j + 32], Wd[:, j, f, 512 * h:512 * h + 512],
                                                      start=(f == 0), stop=(f == 1))
                        mm.then_inc(S["e_down_free"], 1)
                    nc.tensor.drain().then_inc(S["e_down"], 1)
                scatter(n)
                on_pe(pe)

            @block.scalar
            def _(act):
                n = groups(act)

                def copy_tokens(g):
                    act.wait_ge(S["e_gather0"], g + 1)
                    nc.scalar.activation(hs[:, 0:4, :], ps[0][:, :].rearrange("p (k s) -> p k s", k=4), ACT.Copy)
                    act.drain().then_inc(S["e_hs0"], 1)

                act.drain().then_inc(S["e_y"], 1)
                copy_tokens(0)
                with act.Fori(0, n) as g:
                    act.wait_ge(S["e_up"], g + 1)
                    nc.scalar.activation(sil[:, :], ps[2][:, 0:DE], ACT.Silu)
                    act.drain().then_inc(S["e_sil"], 1)
                    copy_tokens(g + 1)
                    act.wait_ge(S["e_down"], g + 1)
                    act.wait_ge(S["e_part"], g * KT + KT)
                    for h in range(2):
                        nc.scalar.activation(y[:, 512 * h:512 * h + 512], ps[4 + h][:, :], ACT.Copy)
                    act.drain().then_inc(S["e_y"], 1)
                on_act(act, S["n2_centred"])

            @block.vector
            def _(dve):
                n = groups(dve)
                dve.drain().then_inc(S["e_y_free"], 2)

                def select():
                    nc.vector.tensor_tensor(eq[:, :, :, :], m.slot_of[:, :, :].unsqueeze(3).to_broadcast([P, 3, 2, P]),
                                            m.count[:, :].unsqueeze(1).unsqueeze(1).to_broadcast([P, 3, 2, P]), ALU.is_equal)
                    dve.drain()
                    nc.vector.tensor_tensor(sel[:, :, :], eq[:, :, 0, :], eq[:, :, 1, :], ALU.add)
                    nc.vector.tensor_scalar(m.slot_of[:, :, :], m.slot_of[:, :, :], -float(P), None, ALU.add)
                    dve.drain().then_inc(S["e_sel"], 1)

                def gates_back():
                    for v in range(2):
                        nc.vector.scalar_tensor_tensor(back[:, 1 + v, :], m.token_row[:, v, :], slot[:, 0:1], m.token_row[:, 2 + v, :], ALU.is_equal, ALU.mult)
                    dve.drain()
                    nc.vector.tensor_tensor(back[:, 0, :], back[:, 1, :], back[:, 2, :], ALU.add)
                    nc.vector.tensor_scalar(slot[:, :], slot[:, :], float(P), None, ALU.add)
                    dve.drain()

                def copy_tokens(g):
                    dve.wait_ge(S["e_gather1"], g + 1)
                    nc.vector.tensor_copy(hs[:, 4:8, :], ps[1][:, :].rearrange("p (k s) -> p k s", k=4))
                    dve.drain().then_inc(S["e_hs1"], 1)

                def add_parts(g):
                    for d in range(KT):
                        dve.wait_ge(S["e_part"], g * KT + (d + 1))
                        nc.vector.tensor_tensor(m.yT[:, d, :], m.yT[:, d, :], ps[6 + d % 2][:, 0:T], ALU.add).then_inc(S["e_y_free"], 1)

                nc.vector.memset(y[:, :], 0.0)
                nc.vector.tensor_scalar(slot[:, :], m.slot_id[:, :], -float(P), None, ALU.add)
                dve.drain()
                select()
                copy_tokens(0)
                gates_back()
                dve.drain().then_inc(S["e_back"], 1)
                with dve.Fori(0, n) as g:
                    select()
                    dve.wait_ge(S["e_sil"], g + 1)
                    nc.vector.tensor_tensor(hid[:, :], sil[:, :], ps[2][:, DE:2 * DE], ALU.mult)
                    dve.drain().then_inc(S["e_hid"], 1)
                    copy_tokens(g + 1)
                    dve.wait_ge(S["e_turn"], g + 1)
                    nc.vector.tensor_copy(hidT[:, :, :], ps[3][:, 0:2 * P].rearrange("p (f s) -> p f s", f=2))
                    dve.drain().then_inc(S["e_hidT"], 1)
                    add_parts(g)
                    gates_back()
                    dve.drain().then_inc(S["e_back"], 1)
                add_parts(n)
                dve.drain()
                nc.vector.tensor_copy(m.hT[:, :, :], m.yT[:, :, :])
                dve.drain().then_inc(S["n2_ready"], 1)
                on_dve(dve, S["n2_centred"])


SEMS1 = """params_loaded params_turned rows_loaded proj proj_by_act proj_by_dve rope_in rope_mm rope_out conv conv_silu
d_squares d_norms d_ln d_rnorm d_normed d_gin d_gexp d_gcum d_gc d_dif d_decay d_kv d_kk d_LA d_LAT d_XY d_LX d_P d_PY d_YP
d_wu d_wT_sb d_wu_sb d_wS d_vnew d_oS d_state d_o d_osq d_onorm d_ornorm
s_idx s_rel s_acc s_logit s_logit_sb s_max s_exp s_prob s_pT s_pT_sb s_pv s_out
o_mm o_added n1_ready n1_centred n1_mean n1_squares n1_var n1_rstd n1_done r_logit r_exp_in r_exp r_masks r_rows r_rows_sb r_counts r_ranks r_nb r_starts r_spread r_table
e_up_free e_down_free e_up_in0 e_up_in1 e_up_in2 e_up_in3 e_down_in0 e_down_in1 e_down_in2 e_down_in3
e_sel e_gather0 e_gather1 e_hs0 e_hs1 e_up e_sil e_hid e_turn e_hidT e_down e_y e_y_free e_back e_part n2_ready n2_centred n2_mean n2_squares n2_var n2_rstd""".split()


def clear(nc, signals, ring):
    for s in signals + list(ring.loaded) + [ring.used]:
        nc.sync.sem_clear(s)
    nc.all_engine_barrier()


def first_block(nc, ps, xT, A, x, meta):
    with ExitStack() as ctx:
        def sb(name, shape):
            return ctx.enter_context(nc.sbuf_tensor(name, shape, F32))

        def sem(name):
            return ctx.enter_context(nc.semaphore(name))

        C = constants()
        start = sem("start")
        m = Buffers()
        m.ps, m.xT = ps, xT
        K = load_constants(nc, ctx, C)
        m.ident, m.ones, m.mean_w, m.cum = K["ident"], K["ones"], K["mean_w"], K["cum"]
        m.strict, m.incl, m.level0, m.levelsT = K["strict"], K["incl"], K["level0"], K["levelsT"]
        m.causal, m.rot, m.cos, m.sin = K["causal"], K["rot"], K["cos"], K["sin"]
        m.rank4, m.rank8, m.before, m.count, m.slot_id = K["rank4"], K["rank8"], K["before"], K["count"], K["slot_id"]
        m.W = sb("W", [P, SLOTS, SLOT])
        m.prm = sb("prm", [P, P])
        m.prmT = sb("prmT", [P, 96])
        m.rows = sb("rows", [P, 44])
        m.eps5 = sb("eps5", [P, 1])
        m.eps6 = sb("eps6", [P, 1])
        m.hT = sb("hT", [P, KT, T])
        m.w_route = sb("w_route", [P, KT, 36])
        m.table = ctx.enter_context(nc.sbuf_tensor("table", [1, MAX_GROUPS * BLOCKS_GROUP + 1], I32))

        turned, copied = sem("turned"), sem("copied")
        with nc.sbuf_tensor("x_tok", [P, 3, D], F32) as xt, nc.Block() as block:
            @block.sync
            def _(sp):
                sp.dma_start(xt[0:16, 0, :], meta[:, :]).then_inc(start, 16)
                sp.dma_start(xt[16:128, 0, :], x[0, 0:112, :]).then_inc(start, 16)
                sp.dma_start(xt[:, 1, :], x[0, 112:240, :]).then_inc(start, 16)
                sp.dma_start(xt[0:16, 2, :], x[0, 240:256, :]).then_inc(start, 16)

            @block.tensor
            def _(pe):
                pe.wait_ge(start, 64)
                for k in range(KT):
                    if k >= 4:
                        pe.wait_ge(copied, k - 3)
                    for c, (t0, n) in enumerate(TILES):
                        mm = nc.tensor.transpose(m.ps[k % 4][:, t0:t0 + n], xt[0:n, c, k * P:(k + 1) * P], m.ident[0:n, 0:n])
                    mm.then_inc(turned, 1)

            @block.vector
            def _(dve):
                nc.vector.memset(m.eps5[:, :], 1e-5)
                nc.vector.memset(m.eps6[:, :], 1e-6)
                for k in range(KT):
                    dve.wait_ge(turned, k + 1)
                    nc.vector.tensor_copy(m.hT[:, k, :], m.ps[k % 4][:, 0:T]).then_inc(copied, 1)

        ring = m.ring = WeightRing([sem(f"loaded{i}") for i in range(SLOTS)], sem("used"))
        for c in range(8):
            ring.add(f"in{c}", c % 4)
        ring.add("in8", 0, dmas=4)
        ring.add("out0", 1)
        ring.add("out1", 2)
        signals = {name: sem(name) for name in SEMS1}
        S = signals
        with nc.Fori(0, DEPTH) as l:
            with nc.sbuf_tensor("mixT", [P, 8, T], F32) as m.mixT:
                with ExitStack() as lay:
                    def lsb(name, shape):
                        return lay.enter_context(nc.sbuf_tensor(name, shape, F32))

                    m.qkvT = lsb("qkvT", [P, 12, T])
                    m.zT = lsb("zT", [P, 4, T])
                    m.bai = lsb("bai", [P, 3, 16])
                    m.sqT = lsb("sqT", [P, 4, T])
                    m.skT = lsb("skT", [P, 4, T])
                    m.iqT = lsb("iqT", [P, 4, T])
                    m.ikT = lsb("ikT", [P, T])
                    m.sv = lsb("sv", [P, 3, 512])
                    with nc.sbuf_tensor("xpad", [P, 3, 3 + T], F32) as m.xpad, nc.sbuf_tensor("conv_out", [P, 2, T], F32) as m.conv_out, \
                            nc.sbuf_tensor("rope_tmp", [P, 2, 2, T], F32) as m.rope_tmp:
                        nc.vector.memset(m.xpad[:, :, 0:3], 0.0)
                        nc.vector.memset(m.bai[:, :, :], 0.0)
                        nc.vector.drain()
                        projections(nc, m, l, A, S)
                    linear_and_sparse(nc, m, S)
                with ExitStack() as lay:
                    def lsb(name, shape):
                        return lay.enter_context(nc.sbuf_tensor(name, shape, F32))

                    m.yT = lsb("yT", [P, KT, T])
                    m.rowsH = lsb("rowsH", [P, 3, D])
                    m.slot_of = lsb("slot_of", [P, 3, 2])
                    m.token_row = lsb("token_row", [P, 4, T])
                    nc.vector.memset(m.slot_of[:, :, :], -1e6)
                    nc.vector.drain()
                    mix_and_route(nc, m, l, A, S)
                    experts(nc, m, l, A, S)
            clear(nc, list(signals.values()), ring)
        nc.vector.tensor_copy(m.xT[:, :, :], m.hT[:, :, N_META:T])
        nc.all_engine_barrier()


NAMES1 = "w_in conv_w a_log dt_bias dn_norm_g w_out ln1_g ln1_b w_grp b_grp w_rtr b_rtr w1 w3 w2 ln2_g ln2_b".split()





S2 = SEQ
N_CMP = (SEQ - 32) // 16 + 1
HIDDEN = 4 * D
IN2 = dict(q=0, kc=512, vc=640, ks=768, vs=896, kw=1024, vw=1152, g=1280, gq=1304, gk=1560, gv=1816, gr=2328,
           glow=2840, mq=2856, merge=3368)


def constants2():
    i = np.arange(P)
    c = {"ident": np.eye(P), "mean_w": np.full((P, P), 1.0 / D), "mean128": np.full((P, P), 1.0 / P)}
    c["mean64"] = (i[:, None] // 64 == i[None, :] // 64) / 64.0
    rot = np.zeros((P, P))
    for h in (0, 64):
        for d in range(8):
            rot[h + d + 8, h + d] = -1.0
            rot[h + d, h + d + 8] = 1.0
    c["rot"] = rot
    t = np.arange(S2)
    qpos = np.stack([i, i + P], 1)
    c["causal_bias"] = np.where(t[None, None, :] <= qpos[:, :, None], 0.0, -BIG)
    ends = np.arange(N_CMP) * 16 + 31
    c["cmp_mask"] = ends[None, None, :] <= qpos[:, :, None]
    c["cmp_bias"] = np.where(c["cmp_mask"], 0.0, -BIG)
    inv = np.power(np.float32(500000.0), -np.arange(8, dtype=np.float32) / np.float32(8)).astype(np.float32)
    c["inv_freq"] = np.where(i % 64 < 16, inv[i % 8], 0.0)[:, None]
    sums = np.zeros((P, 9, P))
    for lv in range(7):
        mid = ((i >> (lv + 1)) << (lv + 1)) + (1 << lv)
        up = i >= mid
        u = i[:, None]
        sums[:, lv, :] = np.where(up[None, :], (u >= mid[None, :]) & (u <= i[None, :]), (u > i[None, :]) & (u < mid[None, :]))
    sums[:, 7, :] = i[:, None] > i[None, :]
    sums[:, 8, :] = i[:, None] <= i[None, :]
    c["sums"] = sums
    pairs = np.zeros((P, 8, P))
    for lv in range(7):
        pairs[:, lv, :] = ((i[None, :] >> lv) == (i[:, None] >> lv) + 1) & ((i[None, :] >> lv) % 2 == 1)
    pairs[:, 7, :] = np.eye(P)
    c["pairs"] = pairs * 64 ** -0.5
    return {k: np.ascontiguousarray(v, np.float32) for k, v in c.items()}


def rms_steps(nc, m, signals, g0):
    sq, ms, rstd, done = signals

    def on_scalar(act):
        for k in range(KT):
            nc.scalar.activation(m.hT[:, k, :], m.xT[:, k, :], ACT.Square).then_inc(sq, 1)
        act.wait_ge(ms, 1)
        nc.scalar.activation(m.rstd[:, :], m.ps[7][:, 0:S2], ACT.Ln, bias=m.eps6[:, 0:1])
        act.drain()
        nc.scalar.activation(m.rstd[:, :], m.rstd[:, :], ACT.Exp, scale=-0.5)
        act.drain().then_inc(rstd, 1)

    def on_tensor(pe):
        for k in range(KT):
            pe.wait_ge(sq, k + 1)
            mm = nc.tensor.matmul(m.ps[7][:, 0:S2], m.mean_w[:, :], m.hT[:, k, :], start=(k == 0), stop=(k == KT - 1))
        mm.then_inc(ms, 1)

    def on_vector(dve):
        dve.wait_ge(rstd, 1)
        for k in range(KT):
            i = nc.vector.scalar_tensor_tensor(m.hT[:, k, :], m.xT[:, k, :], m.prmT[:, g0 + k:g0 + k + 1], m.rstd[:, :], ALU.mult, ALU.mult)
            i.then_inc(done, 1)

    return on_scalar, on_tensor, on_vector


class Loads:

    def __init__(self, ring, items):
        self.ring, self.items, self.at = ring, items, 0

    def upto(self, sp, name):
        while True:
            n, dmas = self.items[self.at]
            free = self.ring.freed(n)
            if free:
                sp.wait_ge(*free)
            slot = self.ring.chunks[n][0]
            for dst, src in dmas:
                sp.dma_start(dst, src).then_inc(self.ring.loaded[slot], 16)
            self.at += 1
            if n == name:
                return


def weights2(nc, m, l, A, ring):
    W = m.W
    w_in = A["w_in_2"].rearrange("l (k p) n -> l p k n", p=P)
    w_kv = A["mem_w_kv_2"].rearrange("l (k p) n -> l p k n", p=P)
    w_out = A["w_out_2"].rearrange("l (k p) n -> l p k n", p=P)
    w_up = A["w_up_2"].rearrange("l (k p) n -> l p k n", p=P)
    w_down = A["w_down_2"].rearrange("l (c k p) n -> l c p k n", p=P, k=4)
    cmp1 = A["cmp_w1_2"].rearrange("l x (k p) e -> l x p k e", p=P)
    br0 = A["w_branch_2"].rearrange("l b (a t d) n -> l b a d t n", a=2, t=4)
    br = A["w_branch_2"].rearrange("l b (k p) n -> l b p k n", p=P)
    used, loads, slot_of = [], {}, {}

    def view(slot, k):
        return W[:, slot, :].rearrange("p (k n) -> p k n", k=k)

    def add(name, slot, dmas):
        ring.add(name, slot, dmas=len(dmas))
        loads[name] = dmas

    s = 0

    def plain(name, c0, n=512, extra=()):
        nonlocal s
        w = view(s % 4, KT)
        dmas = [(w[:, :, 0:n], w_in[l, :, :, c0:c0 + n])]
        dmas += [(w[:, :, a:a + k], w_in[l, :, :, b:b + k]) for a, b, k in extra]
        add(name, s % 4, dmas)
        s += 1

    wq = W[:, 0, :].rearrange("p (k t a d) -> p k t a d", k=KT, t=4, a=2)
    src = A["w_in_2"].rearrange("l (k p) n -> l p k n", p=P)[l, :, :, 0:512].rearrange("p k (a t d) -> p k t a d", a=2, t=4)
    add("q", 0, [(wq[:, :, t, a, :], src[:, :, t, a, :]) for t in range(4) for a in range(2)])
    s += 1
    plain("nkv", 512)
    plain("nkw", 1024, 280, [(280, IN2["glow"], 16)])
    plain("gqk", IN2["gq"])
    plain("gv", IN2["gv"])
    plain("gr", IN2["gr"])
    plain("mq", IN2["mq"])
    for x in range(2):
        add(f"cmp{x}", s % 4, [(view(s % 4, 16), cmp1[l, x, :, :, :])])
        s += 1
    for x in range(2):
        add(f"kv{x}", s % 4, [(view(s % 4, KT), w_kv[l, :, :, 512 * x:512 * x + 512])])
        s += 1
    order = list(loads)
    for b in range(3):
        plain(f"mg{2 * b}", IN2["merge"] + 1024 * b)
        plain(f"mg{2 * b + 1}", IN2["merge"] + 1024 * b + 512)
        w = view(s % 4, 4)
        if b == 0:
            add("br0", s % 4, [(w[0:64, :, :], br0[l, 0, 0, :, :, :]), (w[64:128, :, :], br0[l, 0, 1, :, :, :])])
        else:
            add(f"br{b}", s % 4, [(w, br[l, b, :, :, :])])
        s += 1
        order += [f"mg{2 * b}", f"br{b}", f"mg{2 * b + 1}"]
    for c in range(2):
        add(f"wo{c}", s % 4, [(view(s % 4, KT), w_out[l, :, :, 512 * c:512 * c + 512])])
        order.append(f"wo{c}")
        s += 1
    m.used_before_mlp = ring.n
    m.mlp_slots = []
    for c in range(2):
        m.mlp_slots.append((s % 4, (s + 1) % 4))
        add(f"mu{c}", s % 4, [(view(s % 4, KT), w_up[l, :, :, 512 * c:512 * c + 512])])
        add(f"md{c}", (s + 1) % 4, [(view((s + 1) % 4, 4), w_down[l, c, :, :, :])])
        order += [f"mu{c}", f"md{c}"]
        s += 2
    return Loads(ring, [(n, loads[n]) for n in order])


def project2(nc, m, l, A, S, loads):
    ring, ps, W = m.ring, m.ps, m.W
    plan = [("q", True, ("pair", j), m.raw[:, j, :]) for j in range(4)]
    plan += [("nkv", True, (0, P), m.kcv[:, 0, :]), ("nkv", True, (P, P), m.kcv[:, 1, :]), ("nkv", True, (2 * P, P), m.raw[:, 4, :])]
    plan += [("nkv", False, (3 * P, P), m.vs[:, j, :]) for j in range(2)]
    plan += [("nkw", True, (0, P), m.raw[:, 5, :])]
    plan += [("nkw", False, (P, P), m.vw[:, j, :]) for j in range(2)]
    plan += [("nkw", False, (256, 24), m.ngate[:, j, :]) for j in range(2)]
    plan += [("nkw", True, (280, 16), m.glow[:, :])]
    plan += [("gqk", True, (P * j, P), m.gqk[:, j, :]) for j in range(4)]
    plan += [("gv", False, (0, 512), m.gv[:, j, :]) for j in range(2)]
    plan += [("gr", True, (P * j, P), m.gr[:, j, :]) for j in range(4)]
    plan += [("mq", True, (P * j, P), m.raw[:, 6 + j, :]) for j in range(4)]
    tok = {i: sum(1 for p in plan[:i] if p[0] == plan[i][0] and not p[1] and p[2] == plan[i][2]) for i in range(len(plan)) if not plan[i][1]}
    on_act, on_pe, on_dve = rms_steps(nc, m, (S["p_sq"], S["p_ms"], S["p_rstd"], S["p_done"]), 0)

    def shape(i):
        _, fm, (a, w), _ = plan[i]
        w = P if a == "pair" else w
        return (w, S2) if fm else (P, w)

    with nc.Block() as block:
        @block.sync
        def _(sp):
            pr = m.prm

            def v(name, c=P):
                return A[name].rearrange("l (t f) -> l t f", f=c)[l]

            kn = A["nsa_k_norm_2"]
            for r0, n, ap in [(0, 8, v("ln_mix_2")), (8, 24, A["b_merge_2"].rearrange("l b (t f) -> l (b t) f", f=P)[l]),
                              (32, 8, v("mem_norm_2")), (40, 8, v("ln_mlp_2")), (48, 1, v("gla_norm_2")),
                              (49, 1, v("mem_q_norm_2")), (50, 1, v("mem_k_norm_2")),
                              (55, 32, A["cmp_pe_2"].rearrange("l x (k a) d -> l (x k) (a d)", a=2)[l])]:
                sp.dma_start(pr[r0:r0 + n, :], ap).then_inc(S["params_loaded"], 16)
            for a in (0, 64):
                sp.dma_start(pr[51:52, a:a + 64], v("nsa_q_norm_2", 64)).then_inc(S["params_loaded"], 16)
                sp.dma_start(pr[52:55, a:a + 64], kn[l, :, :]).then_inc(S["params_loaded"], 16)
            sp.dma_start(m.w_gate[:, :], A["gla_w_gate_2"][l, :, :]).then_inc(S["small_loaded"], 16)
            sp.dma_start(m.b_gate[:, :], A["gla_b_gate_2"].rearrange("l (a n) -> l a n", a=1)[l]).then_inc(S["small_loaded"], 16)
            sp.dma_start(m.w_cmp2[:, :, :, :], A["cmp_w2_2"].rearrange("l x (k p) d -> l p x k d", p=P)[l]).then_inc(S["small_loaded"], 16)
            loads.upto(sp, "kv1")

        @block.tensor
        def _(pe):
            pe.wait_ge(S["params_loaded"], 16 * 12)
            nc.tensor.transpose(ps[6][:, 0:87], m.prm[0:87, :], m.ident[0:87, 0:87]).then_inc(S["params_turned"], 1)
            on_pe(pe)
            pe.wait_ge(S["p_done"], KT)
            for i, (chunk, fm, (a, w), _) in enumerate(plan):
                wv = W[:, ring.chunks[chunk][0], :].rearrange("p (k n) -> p k n", k=KT)
                if i == 0 or plan[i - 1][0] != chunk:
                    pe.wait_ge(*ring.arrived(chunk))
                if i >= 6:
                    pe.wait_ge(S["p_dve"] if i % 2 == 0 else S["p_act"], (i - 6) // 2 + 1)
                rows, cols = shape(i)
                o = ps[i % 6][0:rows, 0:cols]
                for k in range(KT):
                    st = dict(start=(k == 0), stop=(k == KT - 1))
                    if a == "pair":
                        mm = nc.tensor.matmul(o, wv[:, k, w * P:(w + 1) * P], m.hT[:, k, :], **st)
                    elif fm:
                        mm = nc.tensor.matmul(o, wv[:, k, a:a + w], m.hT[:, k, :], **st)
                    else:
                        t0 = P * tok[i]
                        mm = nc.tensor.matmul(o, m.hT[:, k, t0:t0 + P], wv[:, k, a:a + w], **st)
                mm.then_inc(S["p_mm"], 1)
                if i + 1 == len(plan) or plan[i + 1][0] != chunk:
                    nc.tensor.drain().then_inc(ring.used, 1)

        @block.scalar
        def _(act):
            on_act(act)
            for i in range(1, len(plan), 2):
                act.wait_ge(S["p_mm"], i + 1)
                rows, cols = shape(i)
                nc.scalar.activation(plan[i][3], ps[i % 6][0:rows, 0:cols], ACT.Copy).then_inc(S["p_act"], 1)

        @block.vector
        def _(dve):
            dve.wait_ge(S["params_turned"], 1)
            nc.vector.tensor_copy(m.prmT[:, 0:87], ps[6][:, 0:87])
            dve.drain()
            on_dve(dve)
            for i in range(0, len(plan), 2):
                dve.wait_ge(S["p_mm"], i + 1)
                rows, cols = shape(i)
                nc.vector.tensor_copy(plan[i][3], ps[i % 6][0:rows, 0:cols]).then_inc(S["p_dve"], 1)


def heads2(nc, m, l, A, S, loads):
    ring, ps, W = m.ring, m.ps, m.W
    with ExitStack() as ctx:
        def sb(name, shape):
            return ctx.enter_context(nc.sbuf_tensor(name, shape, F32))

        rs = sb("h_rs", [P, 10, S2])
        xs = sb("h_xs", [P, 2, 6, S2])
        kk = sb("h_kk", [P, 2, 2, S2])
        win = sb("h_win", [P, 2, 16, 2 * N_CMP])
        hid = sb("h_hid", [2 * N_CMP, 2, 256])
        gl = sb("h_gl", [2 * N_CMP, 2, 256])
        hidT = sb("h_hidT", [P, 2, 2, 2 * N_CMP])
        kq = sb("h_kq", [P, 5, N_CMP])
        NC2 = 2 * N_CMP

        def cols(ap):
            return ap[:, 31:S2:16]

        with nc.Block() as block:
            @block.sync
            def _(sp):
                for lp in range(2):
                    for g in range(2):
                        sp.dma_start(kk[64 * lp:64 * lp + 64, :, g, 0:S2 - 1], m.kcv[64 * g:64 * g + 64, :, lp:lp + S2 - 1]).then_inc(S["h_kk"], 16)

            @block.tensor
            def _(pe):
                for j in range(5):
                    pe.wait_ge(S["h_sq"], 1)
                    mm = nc.tensor.matmul(ps[j][:, :], (m.mean64 if j < 3 else m.mean128)[:, :], rs[:, 2 * j:2 * j + 2, :], start=True, stop=True)
                mm.then_inc(S["h_ms"], 1)
                for x in range(2):
                    pe.wait_ge(*ring.arrived(f"cmp{x}"))
                    pe.wait_ge(S["h_win"], x + 1)
                    w = W[:, ring.chunks[f"cmp{x}"][0], :].rearrange("p (k n) -> p k n", k=16)
                    for k in range(16):
                        mm = nc.tensor.matmul(ps[5 + x][0:NC2, 0:256], win[:, x, k, :], w[:, k, :], start=(k == 0), stop=(k == 15))
                    mm.then_inc(S["h_hid"], 1)
                    nc.tensor.drain().then_inc(ring.used, 1)
                pe.wait_ge(S["h_xs"], 1)
                for j in range(3):
                    nc.tensor.matmul(ps[j][:, :], m.rot[:, :], xs[:, 0, 2 * j:2 * j + 2, :], start=True, stop=False)
                    mm = nc.tensor.matmul(ps[j][:, :], m.ident[:, :], xs[:, 1, 2 * j:2 * j + 2, :], start=False, stop=True)
                mm.then_inc(S["h_rope"], 1)
                pe.wait_ge(S["h_gelu"], 1)
                for x in range(2):
                    for e in range(2):
                        c0 = (2 * x + e) * 32
                        mm = nc.tensor.transpose(ps[7][:, c0:c0 + NC2], gl[:, x, e * P:(e + 1) * P], m.ident[0:NC2, 0:NC2])
                mm.then_inc(S["h_turn"], 1)
                pe.wait_ge(S["small_loaded"], 48)
                pe.wait_ge(S["h_hidT"], 1)
                for g in range(2):
                    for e in range(2):
                        nc.tensor.matmul(ps[3][64 * g:64 * g + 64, 0:N_CMP], m.w_cmp2[:, 0, e, :], hidT[:, 0, e, g * N_CMP:(g + 1) * N_CMP],
                                         start=(e == 0), stop=(e == 1))
                for g in range(2):
                    for e in range(2):
                        mm = nc.tensor.matmul(ps[4][0:N_CMP, 64 * g:64 * g + 64], hidT[:, 1, e, g * N_CMP:(g + 1) * N_CMP], m.w_cmp2[:, 1, e, :],
                                              start=(e == 0), stop=(e == 1))
                mm.then_inc(S["h_comp"], 1)
                pe.wait_ge(S["h_ksq"], 1)
                nc.tensor.matmul(ps[5][:, 0:N_CMP], m.mean64[:, :], kq[:, 1, :], start=True, stop=True).then_inc(S["h_kms"], 1)
                pe.wait_ge(S["h_kxs"], 1)
                nc.tensor.matmul(ps[6][:, 0:N_CMP], m.rot[:, :], kq[:, 3, :], start=True, stop=False)
                nc.tensor.matmul(ps[6][:, 0:N_CMP], m.ident[:, :], kq[:, 4, :], start=False, stop=True).then_inc(S["h_krope"], 1)

            @block.scalar
            def _(act):
                nc.scalar.activation(rs[:, :, :], m.raw[:, :, :], ACT.Square)
                act.drain().then_inc(S["h_sq"], 1)
                act.wait_ge(S["h_ms"], 1)
                for j in range(5):
                    nc.scalar.activation(rs[:, 2 * j:2 * j + 2, :], ps[j][:, :].rearrange("p (a t) -> p a t", a=2), ACT.Ln, bias=m.eps6[:, 0:1])
                act.drain()
                nc.scalar.activation(rs[:, :, :], rs[:, :, :], ACT.Exp, scale=-0.5)
                act.drain().then_inc(S["h_rs"], 1)
                act.wait_ge(S["h_gin"], 1)
                nc.scalar.activation(gl[:, :, :], gl[:, :, :], ACT.Exp, scale=-1.5957691216057308)
                act.drain().then_inc(S["h_gexp"], 1)
                act.wait_ge(S["h_rope"], 1)
                for j in range(3):
                    nc.scalar.activation(m.qk[:, 2 * j:2 * j + 2, :], ps[j][:, :].rearrange("p (a t) -> p a t", a=2), ACT.Copy)
                act.wait_ge(S["h_comp"], 1)
                nc.scalar.activation(kq[:, 0, :], ps[3][:, 0:N_CMP], ACT.Copy)
                nc.scalar.activation(kq[:, 1, :], ps[3][:, 0:N_CMP], ACT.Square)
                act.drain().then_inc(S["h_ksq"], 1)
                act.wait_ge(S["h_kms"], 1)
                nc.scalar.activation(kq[:, 2, :], ps[5][:, 0:N_CMP], ACT.Ln, bias=m.eps6[:, 0:1])
                act.drain()
                nc.scalar.activation(kq[:, 2, :], kq[:, 2, :], ACT.Exp, scale=-0.5)
                act.drain().then_inc(S["h_krs"], 1)
                act.wait_ge(S["h_krope"], 1)
                nc.scalar.activation(m.kcmp[:, :], ps[6][:, 0:N_CMP], ACT.Copy)

            @block.vector
            def _(dve):
                dve.wait_ge(S["h_kk"], 64)
                for x in range(2):
                    for g in range(2):
                        base = kk[:, x, g, 0:S2]
                        src = bass.AP(base.tensor, base.offset, [list(base.ap[0]), [2, 16], [16, N_CMP]])
                        pe_ = m.prmT[:, 55 + 16 * x:71 + 16 * x].unsqueeze(2).to_broadcast([P, 16, N_CMP])
                        nc.vector.tensor_tensor(win[:, x, :, g * N_CMP:(g + 1) * N_CMP], src, pe_, ALU.add)
                    dve.drain().then_inc(S["h_win"], 1)
                dve.wait_ge(S["h_rs"], 1)
                for j in range(10):
                    g = 51 if j < 4 else 49 if j >= 6 else 53 + j - 4
                    dst = m.raw[:, j, :]
                    nc.vector.scalar_tensor_tensor(dst, m.raw[:, j, :], m.prmT[:, g:g + 1], rs[:, j, :], ALU.mult, ALU.mult)
                dve.drain()
                for y, tab in ((0, m.sin), (1, m.cos)):
                    nc.vector.tensor_tensor(xs[:, y, :, :], m.raw[:, 0:6, :], tab[:, :].unsqueeze(1).to_broadcast([P, 6, S2]), ALU.mult)
                dve.drain().then_inc(S["h_xs"], 1)
                for x in range(2):
                    dve.wait_ge(S["h_hid"], x + 1)
                    nc.vector.tensor_copy(hid[:, x, :], ps[5 + x][0:NC2, 0:256])
                dve.drain()
                nc.vector.tensor_tensor(gl[:, :, :], hid[:, :, :], hid[:, :, :], ALU.mult)
                dve.drain()
                nc.vector.tensor_scalar(gl[:, :, :], gl[:, :, :], 0.044715, 1.0, ALU.mult, ALU.add)
                dve.drain()
                nc.vector.tensor_tensor(gl[:, :, :], gl[:, :, :], hid[:, :, :], ALU.mult)
                dve.drain()
                nc.vector.tensor_scalar(gl[:, :, :], gl[:, :, :], -50.0, None, ALU.max)
                dve.drain().then_inc(S["h_gin"], 1)
                dve.wait_ge(S["h_gexp"], 1)
                nc.vector.tensor_scalar(gl[:, :, :], gl[:, :, :], 1.0, None, ALU.add)
                dve.drain()
                nc.vector.reciprocal(gl[:, :, :], gl[:, :, :])
                dve.drain()
                nc.vector.tensor_tensor(gl[:, :, :], gl[:, :, :], hid[:, :, :], ALU.mult)
                dve.drain().then_inc(S["h_gelu"], 1)
                dve.wait_ge(S["h_turn"], 1)
                nc.vector.tensor_copy(hidT[:, :, :, :], ps[7][:, 0:128].rearrange("p (x e n) -> p x e n", x=2, e=2)[:, :, :, 0:NC2])
                dve.drain().then_inc(S["h_hidT"], 1)
                dve.wait_ge(S["h_comp"], 1)
                nc.vector.tensor_copy(m.vcmp[:, :], ps[4][0:N_CMP, 0:P])
                dve.wait_ge(S["h_krs"], 1)
                nc.vector.scalar_tensor_tensor(kq[:, 0, :], kq[:, 0, :], m.prmT[:, 52:53], kq[:, 2, :], ALU.mult, ALU.mult)
                dve.drain()
                nc.vector.tensor_tensor(kq[:, 3, :], kq[:, 0, :], cols(m.sin), ALU.mult)
                nc.vector.tensor_tensor(kq[:, 4, :], kq[:, 0, :], cols(m.cos), ALU.mult)
                dve.drain().then_inc(S["h_kxs"], 1)


def native_sparse(nc, m, S, ctx):
    ps = m.ps
    def sb(name, shape):
        return ctx.enter_context(nc.sbuf_tensor(name, shape, F32))

    p = sb("n_p", [P, 4, 2, S2])
    pc = sb("n_pc", [P, 4, N_CMP])
    mx = sb("n_mx", [P, 4, 3])
    den = sb("n_den", [P, 4, 3])
    gt = sb("n_gt", [P, 2, 24])
    pT = sb("n_pT", [P, 2, 4, P])
    pcT = sb("n_pcT", [N_CMP, 4 * P])
    GROUP = [(c, g) for c in range(2) for g in range(2)]
    cmp_bank, out_bank = ps[2], ps[3]

    def order(u, k):
        return NATIVE_STEP * (15 * u + k)

    def on_tensor(pe):
        for u, (c, g) in enumerate(GROUP):
            hs = slice(64 * g, 64 * g + 64)
            ns = P * (c + 1)
            yield order(u, 0)
            if u:
                pe.wait_ge(S["n_pcT_sb"], u)
            for r in range(4):
                mm = nc.tensor.matmul(cmp_bank[:, 16 * r:16 * r + N_CMP], m.qk[hs, r, c * P:(c + 1) * P], m.kcmp[hs, :], start=True, stop=True)
            mm.then_inc(S["n_clogit"], 1)
            for r in range(4):
                yield order(u, r)
                if r >= 2:
                    pe.wait_ge(S["n_bias"], 4 * u + r - 1)
                elif u and r == 0:
                    pe.wait_ge(S["n_pT_sb"], 4 * u)
                qh = m.qk[hs, r, c * P:(c + 1) * P]
                nc.tensor.matmul(ps[r % 2][:, 0:ns], qh, m.qk[hs, 4, 0:ns], start=True, stop=True)
                nc.tensor.matmul(ps[r % 2][:, S2:S2 + ns], qh, m.qk[hs, 5, 0:ns], start=True, stop=True).then_inc(S["n_logit"], 1)
            yield order(u, 9)
            pe.wait_ge(S["n_prob"], u + 1)
            for r in range(4):
                mm = nc.tensor.transpose(cmp_bank[0:N_CMP, r * P:(r + 1) * P], pc[:, r, :], m.ident[:, :])
            mm.then_inc(S["n_pcT"], 1)
            for r in range(4):
                q = 4 * u + r
                yield order(u, 10 + r)
                if r >= 2:
                    pe.wait_ge(S["n_pT_sb"], q - 1)
                for y in range(2):
                    for j in range(c + 1):
                        mm = nc.tensor.transpose(ps[r % 2][:, (2 * y + j) * P:(2 * y + j + 1) * P], p[:, r, y, j * P:(j + 1) * P], m.ident[:, :])
                mm.then_inc(S["n_pT"], 1)
                yield order(u, 10.6 + r)
                pe.wait_ge(S["n_pT_sb"], q + 1)
                if r == 0:
                    pe.wait_ge(S["n_pcT_sb"], u + 1)
                    if u:
                        pe.wait_ge(S["n_out"], u)
                o = out_bank[hs, r * P:(r + 1) * P]
                for y, v in ((0, m.vs), (1, m.vw)):
                    for j in range(c + 1):
                        nc.tensor.matmul(o, v[:, j, hs], pT[:, r % 2, 2 * y + j, :], start=(y == 0 and j == 0), stop=False)
                nc.tensor.matmul(o, m.vcmp[:, hs], pcT[:, r * P:(r + 1) * P], start=False, stop=True).then_inc(S["n_pv"], 1)

    def on_scalar(act):
        yield 0
        act.wait_ge(S["n_gin"], 1)
        nc.scalar.activation(gt[:, :, :], m.ngate[:, :, :], ACT.Exp, scale=-1.0)
        act.drain().then_inc(S["n_gexp"], 1)
        for u, (c, g) in enumerate(GROUP):
            ns = P * (c + 1)
            yield order(u, 6)
            act.wait_ge(S["n_max"], u + 1)
            for r in range(4):
                for y in range(2):
                    nc.scalar.activation(p[:, r, y, 0:ns], p[:, r, y, 0:ns], ACT.Exp, bias=mx[:, r, y:y + 1], scale=0.125,
                                         accum_out=den[:, r, y:y + 1])
                nc.scalar.activation(pc[:, r, :], pc[:, r, :], ACT.Exp, bias=mx[:, r, 2:3], scale=0.125)
            act.drain().then_inc(S["n_exp"], 1)
            yield order(u, 14)
            act.wait_ge(S["n_pv"], 4 * u + 4)
            hs = slice(64 * g, 64 * g + 64)
            nc.scalar.activation(m.o_nsa[hs, :, c * P:(c + 1) * P], out_bank[hs, :].rearrange("p (r q) -> p r q", r=4), ACT.Copy).then_inc(S["n_out"], 1)

    def on_vector(dve):
        yield 0
        nc.vector.tensor_scalar(m.ngate[:, :, :], m.ngate[:, :, :], -80.0, None, ALU.max)
        dve.drain().then_inc(S["n_gin"], 1)
        dve.wait_ge(S["n_gexp"], 1)
        nc.vector.tensor_scalar(gt[:, :, :], gt[:, :, :], 1.0, None, ALU.add)
        dve.drain()
        nc.vector.reciprocal(gt[:, :, :], gt[:, :, :])
        dve.drain()
        for u, (c, g) in enumerate(GROUP):
            ns = P * (c + 1)
            for r in range(4):
                yield order(u, r + 0.3)
                dve.wait_ge(S["n_logit"], 4 * u + r + 1)
                nc.vector.tensor_tensor(p[:, r, :, 0:ns], ps[r % 2][:, :].rearrange("p (y s) -> p y s", y=2)[:, :, 0:ns],
                                        m.causal_bias[:, c, 0:ns].unsqueeze(1).to_broadcast([P, 2, ns]), ALU.add).then_inc(S["n_bias"], 1)
            yield order(u, 4)
            dve.wait_ge(S["n_clogit"], u + 1)
            nc.vector.tensor_tensor(pc[:, :, :], cmp_bank[:, 0:64].rearrange("p (r n) -> p r n", r=4)[:, :, 0:N_CMP],
                                    m.cmp_mask[:, c, :].unsqueeze(1).to_broadcast([P, 4, N_CMP]), ALU.mult)
            dve.drain()
            nc.vector.tensor_tensor(pc[:, :, :], pc[:, :, :], m.cmp_bias[:, c, :].unsqueeze(1).to_broadcast([P, 4, N_CMP]), ALU.add)
            nc.vector.tensor_reduce(mx[:, :, 0:2], p[:, :, :, 0:ns], AX.X, ALU.max)
            dve.drain()
            nc.vector.tensor_reduce(mx[:, :, 2:3], pc[:, :, :], AX.X, ALU.max)
            dve.drain()
            nc.vector.tensor_scalar(mx[:, :, :], mx[:, :, :], -0.125, None, ALU.mult)
            dve.drain().then_inc(S["n_max"], 1)
            yield order(u, 8)
            dve.wait_ge(S["n_exp"], u + 1)
            nc.vector.tensor_tensor(pc[:, :, :], pc[:, :, :], m.cmp_mask[:, c, :].unsqueeze(1).to_broadcast([P, 4, N_CMP]), ALU.mult)
            dve.drain()
            nc.vector.tensor_reduce(den[:, :, 2:3], pc[:, :, :], AX.X, ALU.add)
            dve.drain()
            nc.vector.tensor_scalar(den[:, :, 2:3], den[:, :, 2:3], 1e-30, None, ALU.max)
            dve.drain()
            nc.vector.reciprocal(den[:, :, :], den[:, :, :])
            dve.drain()
            gh = gt[:, c, 12 * g:12 * g + 12].rearrange("p (r b) -> p r b", b=3)
            nc.vector.tensor_tensor(den[:, :, 0:2], den[:, :, 0:2], gh[:, :, 1:3], ALU.mult)
            nc.vector.tensor_tensor(den[:, :, 2:3], den[:, :, 2:3], gh[:, :, 0:1], ALU.mult)
            dve.drain()
            nc.vector.tensor_tensor(pc[:, :, :], pc[:, :, :], den[:, :, 2:3].to_broadcast([P, 4, N_CMP]), ALU.mult)
            for r in range(4):
                nc.vector.tensor_tensor(p[:, r, :, 0:ns], p[:, r, :, 0:ns], den[:, r, 0:2].unsqueeze(2).to_broadcast([P, 2, ns]), ALU.mult)
            dve.drain().then_inc(S["n_prob"], 1)
            yield order(u, 9.3)
            dve.wait_ge(S["n_pcT"], u + 1)
            nc.vector.tensor_copy(pcT[:, :], cmp_bank[0:N_CMP, :])
            dve.drain().then_inc(S["n_pcT_sb"], 1)
            for r in range(4):
                q = 4 * u + r
                yield order(u, 10.3 + r)
                dve.wait_ge(S["n_pT"], q + 1)
                if q >= 2:
                    dve.wait_ge(S["n_pv"], q - 1)
                for y in range(2):
                    i = nc.vector.tensor_copy(pT[:, r % 2, 2 * y:2 * y + c + 1, :], ps[r % 2][:, 2 * y * P:(2 * y + c + 1) * P].rearrange("p (j q) -> p j q", q=P))
                i.then_inc(S["n_pT_sb"], 1)

    return on_tensor, on_scalar, on_vector


def memory2(nc, m, S, ctx, room):
    ring, ps, W = m.ring, m.ps, m.W
    def sb(name, shape):
        return ctx.enter_context(nc.sbuf_tensor(name, shape, F32))

    mx = sb("m_mx", [P, 4])
    den = sb("m_den", [P, 4])
    SC = float(P) ** -0.5
    take = Room(room)
    memn, kT, rs = take(KT, S2), take(4, S2), take(4, S2)
    v, p, pT = take(2, 512), take(4, S2), take(2, 2, P)
    B = ps[4:8]
    LOGITS = 14

    def order(c, k):
        return LOGITS + 11 * c + k

    def on_tensor(pe):
        yield 1
        pe.wait_ge(S["m_memn"], 1)
        for x in range(2):
            pe.wait_ge(*ring.arrived(f"kv{x}"))
            w = W[:, ring.chunks[f"kv{x}"][0], :].rearrange("p (k n) -> p k n", k=KT)
            if x == 0:
                for j in range(4):
                    yield 1 + j
                    for k in range(KT):
                        mm = nc.tensor.matmul(B[j // 2][:, j % 2 * S2:j % 2 * S2 + S2], w[:, k, j * P:(j + 1) * P], memn[:, k, :], start=(k == 0), stop=(k == KT - 1))
                    mm.then_inc(S["m_kv"], 1)
            else:
                for c in range(2):
                    yield 5 + 3 * c
                    for k in range(KT):
                        mm = nc.tensor.matmul(B[2 + c][:, :], memn[:, k, c * P:(c + 1) * P], w[:, k, :], start=(k == 0), stop=(k == KT - 1))
                    mm.then_inc(S["m_kv"], 1)
            nc.tensor.drain().then_inc(ring.used, 1)
        yield 11
        pe.wait_ge(S["m_ksq"], 1)
        pe.wait_ge(S["m_v"], 1)
        for j in range(2):
            mm = nc.tensor.matmul(B[2 + j][:, :], m.mean128[:, :], rs[:, 2 * j:2 * j + 2, :], start=True, stop=True)
        mm.then_inc(S["m_kms"], 1)
        yield LOGITS
        pe.wait_ge(S["m_k"], 1)
        for c in range(2):
            yield order(c, 0)
            if c:
                pe.wait_ge(S["m_out"], c)
            for h in range(4):
                mm = nc.tensor.matmul(B[h // 2][:, 256 * (h % 2):256 * (h % 2) + 256], m.raw[:, 6 + h, c * P:(c + 1) * P], kT[:, h, :], start=True, stop=True)
            mm.then_inc(S["m_logit"], 1)
            yield order(c, 5)
            pe.wait_ge(S["m_prob"], c + 1)
            for h in range(4):
                q = 4 * c + h
                yield order(c, 5 + h)
                if q >= 2:
                    pe.wait_ge(S["m_pT_sb"], q - 1)
                for j in range(2):
                    mm = nc.tensor.transpose(B[2 + h % 2][:, j * P:(j + 1) * P], p[:, h, j * P:(j + 1) * P], m.ident[:, :])
                mm.then_inc(S["m_pT"], 1)
                yield order(c, 5.6 + h)
                pe.wait_ge(S["m_pT_sb"], q + 1)
                for j in range(2):
                    mm = nc.tensor.matmul(B[0][:, h * P:(h + 1) * P], v[:, j, h * P:(h + 1) * P], pT[:, h % 2, j, :], start=(j == 0), stop=(j == 1))
                mm.then_inc(S["m_pv"], 1)

    def on_scalar(act):
        for j in range(2):
            yield 2.5 + 2 * j
            act.wait_ge(S["m_kv"], 2 * j + 2)
            nc.scalar.activation(rs[:, 2 * j:2 * j + 2, :], B[j][:, :].rearrange("p (a t) -> p a t", a=2), ACT.Square)
        act.drain().then_inc(S["m_ksq"], 1)
        for c in range(2):
            yield 7.5 + 3 * c
            act.wait_ge(S["m_kv"], 5 + c)
            nc.scalar.activation(v[:, c, :], B[2 + c][:, :], ACT.Copy)
        act.drain().then_inc(S["m_v"], 1)
        yield 12
        act.wait_ge(S["m_kms"], 1)
        for j in range(2):
            nc.scalar.activation(rs[:, 2 * j:2 * j + 2, :], B[2 + j][:, :].rearrange("p (a t) -> p a t", a=2), ACT.Ln, bias=m.eps6[:, 0:1])
        act.drain()
        nc.scalar.activation(rs[:, :, :], rs[:, :, :], ACT.Exp, scale=-0.5)
        act.drain().then_inc(S["m_krs"], 1)
        for c in range(2):
            yield order(c, 2)
            act.wait_ge(S["m_max"], c + 1)
            for h in range(4):
                nc.scalar.activation(p[:, h, :], B[h // 2][:, 256 * (h % 2):256 * (h % 2) + 256], ACT.Exp, bias=mx[:, h:h + 1], scale=SC,
                                     accum_out=den[:, h:h + 1])
            act.drain().then_inc(S["m_exp"], 1)
            yield order(c, 9)
            act.wait_ge(S["m_pv"], 4 * c + 4)
            nc.scalar.activation(m.o_mem[:, :, c * P:(c + 1) * P], B[0][:, :].rearrange("p (h q) -> p h q", h=4), ACT.Copy).then_inc(S["m_out"], 1)

    def on_vector(dve):
        yield 0
        for k in range(KT):
            nc.vector.scalar_tensor_tensor(memn[:, k, :], m.memT[:, k, :], m.prmT[:, 32 + k:33 + k], m.mem_rstd[:, :], ALU.mult, ALU.mult)
        dve.drain().then_inc(S["m_memn"], 1)
        yield 13
        dve.wait_ge(S["m_krs"], 1)
        for j in range(4):
            nc.vector.scalar_tensor_tensor(kT[:, j, :], B[j // 2][:, j % 2 * S2:j % 2 * S2 + S2], m.prmT[:, 50:51], rs[:, j, :], ALU.mult, ALU.mult)
        dve.drain().then_inc(S["m_k"], 1)
        for c in range(2):
            yield order(c, 1)
            dve.wait_ge(S["m_logit"], c + 1)
            for x in range(2):
                nc.vector.tensor_reduce(mx[:, 2 * x:2 * x + 2], B[x][:, :].rearrange("p (a t) -> p a t", a=2), AX.X, ALU.max)
            dve.drain()
            nc.vector.tensor_scalar(mx[:, :], mx[:, :], -SC, None, ALU.mult)
            dve.drain().then_inc(S["m_max"], 1)
            yield order(c, 4)
            dve.wait_ge(S["m_exp"], c + 1)
            nc.vector.reciprocal(den[:, :], den[:, :])
            dve.drain()
            nc.vector.tensor_tensor(p[:, :, :], p[:, :, :], den[:, :].unsqueeze(2).to_broadcast([P, 4, S2]), ALU.mult)
            dve.drain().then_inc(S["m_prob"], 1)
            for h in range(4):
                q = 4 * c + h
                yield order(c, 5.3 + h)
                dve.wait_ge(S["m_pT"], q + 1)
                if q >= 2:
                    dve.wait_ge(S["m_pv"], q - 1)
                nc.vector.tensor_copy(pT[:, h % 2, :, :], B[2 + h % 2][:, 0:256].rearrange("p (j q) -> p j q", j=2)).then_inc(S["m_pT_sb"], 1)

    return on_tensor, on_scalar, on_vector


def gated_linear(nc, m, S, ctx, room, first):
    ps = m.ps
    def sb(name, shape):
        return ctx.enter_context(nc.sbuf_tensor(name, shape, F32))

    take = Room(room)
    la, t1 = take(2, 256), take(2, 256)
    ex, qs, ks, prod = take(8, P), take(8, P), take(8, P), take(8, P)
    far = take(2, 2, P)
    att = take(4, 3, P)
    oT = m.o_gla
    rs = ks.rearrange("p (h a) i -> p h (a i)", h=4)
    B = ps[4:8]
    END = first + 26

    def order(u, k):
        return first + 2 + 6 * u + k
    UNITS = [(f, t) for f in range(2) for t in range(2)]

    def on_tensor(pe):
        yield first
        pe.wait_ge(S["small_loaded"], 48)
        pe.wait_ge(S["m_out"], 2)
        for t in range(2):
            nc.tensor.matmul(B[0][:, 256 * t:256 * t + 256], m.glow[:, t * P:(t + 1) * P], m.w_gate[:, :], start=True, stop=False)
            mm = nc.tensor.matmul(B[0][:, 256 * t:256 * t + 256], m.ones[0:1, :], m.b_gate[:, :], start=False, stop=True)
        mm.then_inc(S["g_gate"], 1)
        yield first + 2
        pe.wait_ge(S["g_la"], 1)
        for u, (f, t) in enumerate(UNITS):
            yield order(u, 0)
            if u:
                pe.wait_ge(S["g_ex"], u)
                if t == 0:
                    pe.wait_ge(S["g_far_sb"], f)
            lhs = la[:, t, f * P:(f + 1) * P]
            nc.tensor.matmul(B[0][:, :], lhs, m.sums[:, 0:4, :], start=True, stop=True)
            nc.tensor.matmul(B[1][:, 0:384], lhs, m.sums[:, 4:7, :], start=True, stop=True)
            nc.tensor.matmul(B[1][:, 384:512], lhs, m.sums[:, 7 + t, :], start=True, stop=True).then_inc(S["g_sums"], 1)
            yield order(u, 3)
            pe.wait_ge(S["g_qk"], u + 1)
            for a in range(2):
                hs = slice(64 * a, 64 * a + 64)
                yield order(u, 3 + a)
                if u or a:
                    pe.wait_ge(S["g_prod"], 2 * u + a)
                for lv in range(8):
                    mm = nc.tensor.matmul(B[2 + lv // 4][:, lv % 4 * P:(lv % 4 + 1) * P], ks[hs, lv, :], qs[hs, lv, :], start=True, stop=True)
                mm.then_inc(S["g_pairs"], 1)
                if t == 1:
                    mm = nc.tensor.matmul(B[a][:, 0:P], far[hs, f, 0, :], far[hs, f, 1, :], start=True, stop=True)
                    mm.then_inc(S["g_far"], 1)
        yield END
        pe.wait_ge(S["g_att"], 1)
        for h in range(4):
            o = B[h % 2]
            yield END + 1 + h
            if h >= 2:
                pe.wait_ge(S["g_o_sb"], h - 1)
            v0, v1 = m.gv[:, 0, h * P:(h + 1) * P], m.gv[:, 1, h * P:(h + 1) * P]
            nc.tensor.matmul(o[:, 0:P], v0, att[:, h, 0, :], start=True, stop=True)
            nc.tensor.matmul(o[:, P:2 * P], v1, att[:, h, 1, :], start=True, stop=False)
            nc.tensor.matmul(o[:, P:2 * P], v0, att[:, h, 2, :], start=False, stop=True).then_inc(S["g_o"], 1)
        yield END + 6
        pe.wait_ge(S["g_osq"], 1)
        for j in range(2):
            mm = nc.tensor.matmul(B[2 + j][:, :], m.mean128[:, :], rs[:, 2 * j:2 * j + 2, :], start=True, stop=True)
        mm.then_inc(S["g_oms"], 1)

    def on_scalar(act):
        yield first + 1
        act.wait_ge(S["g_abs"], 1)
        nc.scalar.activation(t1[:, :, :], t1[:, :, :], ACT.Exp, scale=-1.0)
        act.drain()
        nc.scalar.activation(t1[:, :, :], t1[:, :, :], ACT.Ln, bias=1.0)
        act.drain().then_inc(S["g_ln"], 1)
        for u, (f, t) in enumerate(UNITS):
            yield order(u, 1)
            act.wait_ge(S["g_sums"], u + 1)
            if u:
                act.wait_ge(S["g_qk"], u)
            nc.scalar.activation(ex[:, 0:4, :], B[0][:, :].rearrange("p (l i) -> p l i", l=4), ACT.Exp, scale=1.0 / 16)
            nc.scalar.activation(ex[:, 4:8, :], B[1][:, :].rearrange("p (l i) -> p l i", l=4), ACT.Exp, scale=1.0 / 16)
            act.drain().then_inc(S["g_ex"], 1)
            if t == 1:
                yield order(u, 5)
                act.wait_ge(S["g_far"], 2 * f + 2)
                for a in range(2):
                    nc.scalar.activation(att[:, 2 * f + a, 2, :], B[a][:, 0:P], ACT.Copy, scale=0.125)
                act.drain().then_inc(S["g_far_sb"], 1)
        for h in range(4):
            yield END + 1.5 + h
            act.wait_ge(S["g_o"], h + 1)
            nc.scalar.activation(oT[:, h, :], B[h % 2][:, 0:S2], ACT.Copy).then_inc(S["g_o_sb"], 1)
        act.drain()
        nc.scalar.activation(rs[:, :, :], oT[:, :, :], ACT.Square)
        act.drain().then_inc(S["g_osq"], 1)
        yield END + 7
        act.wait_ge(S["g_oms"], 1)
        for j in range(2):
            nc.scalar.activation(rs[:, 2 * j:2 * j + 2, :], B[2 + j][:, :].rearrange("p (a t) -> p a t", a=2), ACT.Ln, bias=m.eps6[:, 0:1])
        act.drain()
        nc.scalar.activation(rs[:, :, :], rs[:, :, :], ACT.Exp, scale=-0.5)
        nc.scalar.activation(m.gr[:, :, :], m.gr[:, :, :], ACT.Silu)
        act.drain().then_inc(S["g_ors"], 1)

    def on_vector(dve):
        yield first + 0.5
        dve.wait_ge(S["g_gate"], 1)
        nc.vector.tensor_copy(la[:, :, :], B[0][:, :].rearrange("p (t n) -> p t n", t=2))
        dve.drain()
        nc.vector.tensor_scalar(t1[:, :, :], la[:, :, :], -1.0, None, ALU.mult)
        dve.drain()
        nc.vector.tensor_tensor(t1[:, :, :], t1[:, :, :], la[:, :, :], ALU.max)
        dve.drain().then_inc(S["g_abs"], 1)
        yield first + 1.5
        dve.wait_ge(S["g_ln"], 1)
        nc.vector.scalar_tensor_tensor(la[:, :, :], la[:, :, :], 0.0, t1[:, :, :], ALU.min, ALU.subtract)
        dve.drain().then_inc(S["g_la"], 1)
        for u, (f, t) in enumerate(UNITS):
            yield order(u, 2)
            dve.wait_ge(S["g_ex"], u + 1)
            if u:
                dve.wait_ge(S["g_pairs"], 2 * u)
            q, k = m.gqk[:, f, t * P:(t + 1) * P], m.gqk[:, 2 + f, t * P:(t + 1) * P]
            nc.vector.tensor_tensor(qs[:, 0:7, :], ex[:, 0:7, :], q.unsqueeze(1).to_broadcast([P, 7, P]), ALU.mult)
            nc.vector.tensor_tensor(ks[:, 0:7, :], ex[:, 0:7, :], k.unsqueeze(1).to_broadcast([P, 7, P]), ALU.mult)
            nc.vector.tensor_copy(qs[:, 7, :], q)
            nc.vector.tensor_copy(ks[:, 7, :], k)
            nc.vector.tensor_tensor(far[:, f, t, :], ex[:, 7, :], q if t else k, ALU.mult)
            dve.drain().then_inc(S["g_qk"], 1)
            for a in range(2):
                yield order(u, 3.5 + a)
                dve.wait_ge(S["g_pairs"], 2 * u + a + 1)
                for b in range(2):
                    nc.vector.tensor_tensor(prod[:, 4 * b:4 * b + 4, :], B[2 + b][:, :].rearrange("p (l i) -> p l i", l=4), m.pairs[:, 4 * b:4 * b + 4, :], ALU.mult)
                dve.drain().then_inc(S["g_prod"], 1)
                nc.vector.tensor_reduce(att[:, 2 * f + a, t, :], prod[:, :, :].rearrange("p l i -> p i l"), AX.X, ALU.add)
                dve.drain()
        yield END
        dve.wait_ge(S["g_far_sb"], 2)
        dve.drain().then_inc(S["g_att"], 1)
        yield END + 8
        dve.wait_ge(S["g_ors"], 1)
        nc.vector.tensor_tensor(oT[:, :, :], oT[:, :, :], rs[:, :, :], ALU.mult)
        dve.drain()
        nc.vector.scalar_tensor_tensor(m.o_gla[:, :, :], oT[:, :, :], m.prmT[:, 48:49], m.gr[:, :, :], ALU.mult, ALU.mult)

    return on_tensor, on_scalar, on_vector


NATIVE_STEP = 1.15
GATED_FIRST = 36
ROOM = 28 * 256


class Room:

    def __init__(self, room):
        self.room, self.at = room, 0

    def __call__(self, *shape):
        n = int(np.prod(shape))
        flat = self.room[:, self.at:self.at + n]
        self.at += n
        if len(shape) == 2:
            return flat.rearrange("p (a b) -> p a b", a=shape[0])
        return flat.rearrange("p (a b c) -> p a b c", a=shape[0], b=shape[1])


def branches2(nc, m, S, loads):
    with ExitStack() as ctx:
        room = ctx.enter_context(nc.sbuf_tensor("b_room", [P, ROOM], F32))
        sparse = native_sparse(nc, m, S, ctx)
        memory = memory2(nc, m, S, ctx, room)
        gated = gated_linear(nc, m, S, ctx, room, GATED_FIRST)

        def both(i, eng):
            yield from memory[i](eng)
            yield from gated[i](eng)

        with nc.Block() as block:
            @block.sync
            def _(sp):
                loads.upto(sp, "mg1")

            @block.tensor
            def _(pe):
                interleave(sparse[0](pe), both(0, pe))

            @block.scalar
            def _(act):
                interleave(sparse[1](act), both(1, act))

            @block.vector
            def _(dve):
                interleave(sparse[2](dve), both(2, dve))


def merge2(nc, m, l, A, S, loads):
    ring, ps, W = m.ring, m.ps, m.W
    with ExitStack() as ctx:
        def sb(name, shape):
            return ctx.enter_context(nc.sbuf_tensor(name, shape, F32))

        gate = sb("x_gate", [P, 2, S2])
        term = sb("x_term", [P, 2, S2])
        acc = sb("x_acc", [P, KT, S2])
        branch = [m.o_nsa, m.o_gla, m.o_mem]

        with nc.Block() as block:
            @block.sync
            def _(sp):
                loads.upto(sp, "md1")

            @block.tensor
            def _(pe):
                for b in range(3):
                    wb = W[:, ring.chunks[f"br{b}"][0], :].rearrange("p (k n) -> p k n", k=4)
                    for n in range(KT):
                        q = KT * b + n
                        mg = f"mg{2 * b + n // 4}"
                        if n % 4 == 0:
                            pe.wait_ge(*ring.arrived(mg))
                        wm = W[:, ring.chunks[mg][0], :].rearrange("p (k n) -> p k n", k=KT)
                        if q >= 2:
                            pe.wait_ge(S["x_gate"], q - 1)
                        for k in range(KT):
                            mm = nc.tensor.matmul(ps[q % 2][:, 0:S2], wm[:, k, n % 4 * P:n % 4 * P + P], m.hT[:, k, :], start=(k == 0), stop=(k == KT - 1))
                        mm.then_inc(S["x_merge"], 1)
                        if n == 0:
                            pe.wait_ge(*ring.arrived(f"br{b}"))
                        if q >= 2:
                            pe.wait_ge(S["x_term"], q - 1)
                        for k in range(4):
                            mm = nc.tensor.matmul(ps[2 + q % 2][:, 0:S2], wb[:, k, n * P:(n + 1) * P], branch[b][:, k, :], start=(k == 0), stop=(k == 3))
                        mm.then_inc(S["x_branch"], 1)
                        if n == 3:
                            nc.tensor.drain().then_inc(ring.used, 1)
                    nc.tensor.drain().then_inc(ring.used, 2)
                pe.wait_ge(S["x_acc"], 1)
                for n in range(KT):
                    if n % 4 == 0:
                        pe.wait_ge(*ring.arrived(f"wo{n // 4}"))
                    w = W[:, ring.chunks[f"wo{n // 4}"][0], :].rearrange("p (k n) -> p k n", k=KT)
                    if n >= 4:
                        pe.wait_ge(S["x_res"], n - 3)
                    for k in range(KT):
                        mm = nc.tensor.matmul(ps[4 + n % 4][:, 0:S2], w[:, k, n % 4 * P:n % 4 * P + P], acc[:, k, :], start=(k == 0), stop=(k == KT - 1))
                    mm.then_inc(S["x_out"], 1)
                    if n % 4 == 3:
                        nc.tensor.drain().then_inc(ring.used, 1)

            @block.scalar
            def _(act):
                for q in range(3 * KT):
                    act.wait_ge(S["x_merge"], q + 1)
                    if q >= 2:
                        act.wait_ge(S["x_term"], q - 1)
                    nc.scalar.activation(gate[:, q % 2, :], ps[q % 2][:, 0:S2], ACT.Sigmoid, bias=m.prmT[:, 8 + q:9 + q]).then_inc(S["x_gate"], 1)

            @block.vector
            def _(dve):
                for q in range(3 * KT):
                    n = q % KT
                    dve.wait_ge(S["x_gate"], q + 1)
                    dve.wait_ge(S["x_branch"], q + 1)
                    if q < KT:
                        nc.vector.tensor_tensor(acc[:, n, :], gate[:, q % 2, :], ps[2 + q % 2][:, 0:S2], ALU.mult)
                        dve.drain().then_inc(S["x_term"], 1)
                    else:
                        nc.vector.tensor_tensor(term[:, q % 2, :], gate[:, q % 2, :], ps[2 + q % 2][:, 0:S2], ALU.mult)
                        dve.drain().then_inc(S["x_term"], 1)
                        nc.vector.tensor_tensor(acc[:, n, :], acc[:, n, :], term[:, q % 2, :], ALU.add)
                dve.drain().then_inc(S["x_acc"], 1)
                for n in range(KT):
                    dve.wait_ge(S["x_out"], n + 1)
                    nc.vector.tensor_tensor(m.xT[:, n, :], m.xT[:, n, :], ps[4 + n % 4][:, 0:S2], ALU.add).then_inc(S["x_res"], 1)


def mlp2(nc, m, l, A, S):
    ring, ps, W = m.ring, m.ps, m.W
    w_up = A["w_up_2"].rearrange("l (k p) (c n) -> l c p k n", p=P, n=512)
    w_down = A["w_down_2"].rearrange("l (c k p) n -> l c p k n", p=P, k=4)
    PAIRS = HIDDEN // 1024
    used0 = m.used_before_mlp
    slots = m.mlp_slots
    first = [(ring.arrived(f"mu{x}")[1], ring.arrived(f"md{x}")[1]) for x in range(2)]
    with ExitStack() as ctx:
        def sb(name, shape):
            return ctx.enter_context(nc.sbuf_tensor(name, shape, F32))

        hid = sb("u_hid", [P, 2, 4, S2])
        rel = sb("u_rel", [P, 2, S2])
        on_act, on_pe, on_dve = rms_steps(nc, m, (S["u_sq"], S["u_ms"], S["u_rstd"], S["u_done"]), 40)

        with nc.Block() as block:
            @block.sync
            def _(sp):
                with sp.Fori(0, PAIRS - 1) as it:
                    for x in range(2):
                        a, b = slots[x]
                        sp.wait_ge(ring.used, it * 4 + (used0 + 2 * x + 1))
                        sp.dma_start(W[:, a, :].rearrange("p (k n) -> p k n", k=KT), w_up[l, it * 2 + (2 + x), :, :, :]).then_inc(ring.loaded[a], 16)
                        sp.wait_ge(ring.used, it * 4 + (used0 + 2 * x + 2))
                        sp.dma_start(W[:, b, :].rearrange("p (k n) -> p k n", k=4), w_down[l, it * 2 + (2 + x), :, :, :]).then_inc(ring.loaded[b], 16)

            @block.tensor
            def _(pe):
                on_pe(pe)
                pe.wait_ge(S["u_done"], KT)
                with pe.Fori(0, PAIRS) as it:
                    for x in range(2):
                        wa = W[:, slots[x][0], :].rearrange("p (k n) -> p k n", k=KT)
                        wb = W[:, slots[x][1], :].rearrange("p (k n) -> p k n", k=4)
                        pe.wait_ge(ring.loaded[slots[x][0]], it * 16 + first[x][0])
                        for j in range(4):
                            pe.wait_ge(S["u_h_free"], it * 8 + (4 * x + j + 1))
                            for k in range(KT):
                                mm = nc.tensor.matmul(ps[j % 2][:, 0:S2], wa[:, k, j * P:(j + 1) * P], m.hT[:, k, :], start=(k == 0), stop=(k == KT - 1))
                            mm.then_inc(S["u_h"], 1)
                        nc.tensor.drain().then_inc(ring.used, 1)
                        pe.wait_ge(ring.loaded[slots[x][1]], it * 16 + first[x][1])
                        pe.wait_ge(S["u_hid"], it * 8 + (4 * x + 4))
                        for n in range(KT):
                            pe.wait_ge(S["u_y_free"], it * 16 + (8 * x + n + 1))
                            for k in range(4):
                                mm = nc.tensor.matmul(ps[4 + n % 2][:, 0:S2], wb[:, k, n * P:(n + 1) * P], hid[:, x, k, :], start=(k == 0), stop=(k == 3))
                            mm.then_inc(S["u_y"], 1)
                        nc.tensor.drain().then_inc(ring.used, 1)

            @block.scalar
            def _(act):
                on_act(act)
                with act.Fori(0, PAIRS) as it:
                    for x in range(2):
                        for j in range(4):
                            act.wait_ge(S["u_h"], it * 8 + (4 * x + j + 1))
                            nc.scalar.activation(rel[:, j % 2, :], ps[j % 2][:, 0:S2], ACT.Relu)
                            act.drain().then_inc(S["u_h_free"], 1)
                            nc.scalar.activation(hid[:, x, j, :], rel[:, j % 2, :], ACT.Square)
                            act.drain().then_inc(S["u_hid"], 1)

            @block.vector
            def _(dve):
                dve.drain().then_inc(S["u_h_free"], 2)
                dve.drain().then_inc(S["u_y_free"], 2)
                on_dve(dve)
                with dve.Fori(0, PAIRS) as it:
                    for x in range(2):
                        for n in range(KT):
                            dve.wait_ge(S["u_y"], it * 16 + (8 * x + n + 1))
                            nc.vector.tensor_tensor(m.xT[:, n, :], m.xT[:, n, :], ps[4 + n % 2][:, 0:S2], ALU.add).then_inc(S["u_y_free"], 1)


SEMS2 = """params_loaded params_turned small_loaded p_sq p_ms p_rstd p_done p_mm p_act p_dve
h_kk h_sq h_ms h_win h_hid h_xs h_rope h_gelu h_turn h_hidT h_comp h_ksq h_kms h_kxs h_krope h_rs h_gin h_gexp h_krs
n_pT_sb n_clogit n_bias n_logit n_prob n_pcT n_pT n_pcT_sb n_out n_pv n_gin n_gexp n_max n_exp
m_memn m_v m_kv m_ksq m_kms m_k m_exp m_logit m_prob m_pT_sb m_pT m_out m_pv m_krs m_max
g_gate g_la g_ex g_sums g_qk g_prod g_pairs g_far g_att g_o_sb g_o g_osq g_oms g_abs g_ln g_far_sb g_ors
x_gate x_merge x_term x_branch x_acc x_res x_out
u_sq u_ms u_rstd u_done u_h_free u_h u_hid u_y_free u_y""".split()


def second_block(nc, ps, xT, A, out):
    with ExitStack() as ctx:
        def sb(name, shape, dt=F32):
            return ctx.enter_context(nc.sbuf_tensor(name, shape, dt))

        def sem(name):
            return ctx.enter_context(nc.semaphore(name))

        C = constants2()
        m = Buffers()
        m.ps, m.xT = ps, xT
        K = load_constants(nc, ctx, C, "2")
        m.ident, m.mean_w, m.mean128, m.mean64 = K["ident"], K["mean_w"], K["mean128"], K["mean64"]
        m.rot, m.causal_bias, m.cmp_mask, m.cmp_bias = K["rot"], K["causal_bias"], K["cmp_mask"], K["cmp_bias"]
        m.inv_freq, m.sums, m.pairs = K["inv_freq"], K["sums"], K["pairs"]
        m.ones = sb("ones2", [1, P])
        m.W = sb("W2", [P, SLOTS, SLOT])
        m.prm = sb("prm2", [P, P])
        m.prmT = sb("prmT2", [P, 96])
        m.eps6 = sb("eps6_2", [P, 1])
        m.memT = sb("memT", [P, KT, S2])
        m.mem_rstd = sb("mem_rstd", [P, S2])
        m.rstd = sb("rstd2", [P, S2])
        m.cos = sb("cos2", [P, S2])
        m.sin = sb("sin2", [P, S2])
        m.w_gate = sb("w_gate", [16, 256])
        m.b_gate = sb("b_gate", [1, 256])
        m.w_cmp2 = sb("w_cmp2", [P, 2, 2, 64])
        m.hT = sb("hT2", [P, KT, S2])
        mem_loaded, mem_turned, mem_copied, pos_loaded = sem("mem_loaded"), sem("mem_turned"), sem("mem_copied"), sem("pos_loaded")
        mem_sq, mem_ms, angles = sem("mem_sq"), sem("mem_ms"), sem("angles")
        with nc.sbuf_tensor("mem_tok", [P, 2, D], F32) as mt, nc.sbuf_tensor("pos_i", [P, S2], I32) as pos_i, \
                nc.sbuf_tensor("ang", [P, 4, S2], F32) as ang, nc.sbuf_tensor("turns", [P, S2], I32) as turns, nc.Block() as block:
            @block.sync
            def _(sp):
                sp.dma_start(mt[:, :, :], A["mem_2"].rearrange("a (t p) d -> p (a t) d", p=P)).then_inc(mem_loaded, 16)
                sp.dma_start(pos_i[:, :], A["positions_2"].to_broadcast([P, S2])).then_inc(pos_loaded, 16)

            @block.tensor
            def _(pe):
                pe.wait_ge(mem_loaded, 16)
                for k in range(KT):
                    if k >= 4:
                        pe.wait_ge(mem_copied, k - 3)
                    for t in range(2):
                        mm = nc.tensor.transpose(m.ps[k % 4][:, t * P:(t + 1) * P], mt[:, t, k * P:(k + 1) * P], m.ident[:, :])
                    mm.then_inc(mem_turned, 1)
                for k in range(KT):
                    pe.wait_ge(mem_sq, k + 1)
                    mm = nc.tensor.matmul(m.ps[4][:, 0:S2], m.mean_w[:, :], m.hT[:, k, :], start=(k == 0), stop=(k == KT - 1))
                mm.then_inc(mem_ms, 1)

            @block.scalar
            def _(act):
                for k in range(KT):
                    act.wait_ge(mem_copied, k + 1)
                    nc.scalar.activation(m.hT[:, k, :], m.memT[:, k, :], ACT.Square).then_inc(mem_sq, 1)
                act.wait_ge(mem_ms, 1)
                nc.scalar.activation(m.mem_rstd[:, :], m.ps[4][:, 0:S2], ACT.Ln, bias=m.eps6[:, 0:1])
                act.drain()
                nc.scalar.activation(m.mem_rstd[:, :], m.mem_rstd[:, :], ACT.Exp, scale=-0.5)
                act.wait_ge(angles, 1)
                nc.scalar.activation(m.sin[:, :], ang[:, 2, :], ACT.Sin)
                nc.scalar.activation(m.cos[:, :], ang[:, 3, :], ACT.Sin)

            @block.vector
            def _(dve):
                nc.vector.memset(m.eps6[:, :], 1e-6)
                nc.vector.memset(m.ones[:, :], 1.0)
                dve.drain()
                for k in range(KT):
                    dve.wait_ge(mem_turned, k + 1)
                    nc.vector.tensor_copy(m.memT[:, k, :], m.ps[k % 4][:, 0:S2])
                    dve.drain().then_inc(mem_copied, 1)
                dve.wait_ge(pos_loaded, 16)
                nc.vector.tensor_copy(ang[:, 0, :], pos_i[:, :])
                dve.drain()
                nc.vector.tensor_scalar(ang[:, 0, :], ang[:, 0, :], m.inv_freq[:, 0:1], None, ALU.mult)
                dve.drain()
                for row, quarter in ((2, 0.0), (3, 0.25)):
                    nc.vector.tensor_scalar(ang[:, 1, :], ang[:, 0, :], float(1 / (2 * np.pi)), quarter, ALU.mult, ALU.add)
                    dve.drain()
                    nc.vector.tensor_copy(turns[:, :], ang[:, 1, :])
                    dve.drain()
                    nc.vector.tensor_copy(ang[:, 1, :], turns[:, :])
                    dve.drain()
                    nc.vector.scalar_tensor_tensor(ang[:, row, :], ang[:, 1, :], -TURN[0], ang[:, 0, :], ALU.mult, ALU.add)
                    dve.drain()
                    for part in TURN[1:]:
                        nc.vector.scalar_tensor_tensor(ang[:, row, :], ang[:, 1, :], -part, ang[:, row, :], ALU.mult, ALU.add)
                        dve.drain()
                    if quarter:
                        nc.vector.tensor_scalar(ang[:, row, :], ang[:, row, :], float(np.pi / 2), None, ALU.add)
                        dve.drain()
                    for cmp, sign in ((ALU.is_gt, -1.0), (ALU.is_lt, 1.0)):
                        nc.vector.tensor_scalar(ang[:, 1, :], ang[:, row, :], -sign * PI, sign * 2 * np.pi, cmp, ALU.mult)
                        dve.drain()
                        nc.vector.tensor_tensor(ang[:, row, :], ang[:, row, :], ang[:, 1, :], ALU.add)
                        dve.drain()
                    nc.vector.tensor_scalar(ang[:, row, :], ang[:, row, :], PI, -PI, ALU.min, ALU.max)
                    dve.drain()
                dve.drain().then_inc(angles, 1)

        signals = {name: sem("b_" + name) for name in SEMS2}
        S = signals
        loaded = [sem(f"loaded2_{i}") for i in range(SLOTS)]
        used = sem("used2")
        with nc.Fori(0, DEPTH) as l:
            ring = m.ring = WeightRing(loaded, used)
            loads = weights2(nc, m, l, A, ring)
            with ExitStack() as lay:
                def lsb(name, shape):
                    return lay.enter_context(nc.sbuf_tensor(name, shape, F32))

                m.raw = lsb("b_raw", [P, 10, S2])
                m.vs = lsb("b_vs", [P, 2, P])
                m.vw = lsb("b_vw", [P, 2, P])
                m.ngate = lsb("b_ngate", [P, 2, 24])
                m.glow = lsb("b_glow", [16, S2])
                m.gqk = lsb("b_gqk", [P, 4, S2])
                m.gv = lsb("b_gv", [P, 2, 512])
                m.gr = lsb("b_gr", [P, 4, S2])
                m.kcmp = lsb("b_kcmp", [P, N_CMP])
                m.vcmp = lsb("b_vcmp", [N_CMP, P])
                m.o_nsa = lsb("b_o_nsa", [P, 4, S2])
                m.o_gla = lsb("b_o_gla", [P, 4, S2])
                m.o_mem = lsb("b_o_mem", [P, 4, S2])
                with nc.sbuf_tensor("b_qk", [P, 6, S2], F32) as m.qk:
                    with nc.sbuf_tensor("b_kcv", [P, 2, S2], F32) as m.kcv:
                        project2(nc, m, l, A, S, loads)
                        heads2(nc, m, l, A, S, loads)
                    branches2(nc, m, S, loads)
                merge2(nc, m, l, A, S, loads)
            mlp2(nc, m, l, A, S)
            clear(nc, list(signals.values()), ring)

        turned, copied, stored = sem("out_turned"), sem("out_copied"), sem("stored")
        with nc.sbuf_tensor("out_tok", [P, 2, D], F32) as ot, nc.Block() as block:
            @block.tensor
            def _(pe):
                for i in range(4):
                    t, half = i // 2, i % 2
                    for k in range(4):
                        mm = nc.tensor.transpose(m.ps[i][:, k * P:(k + 1) * P], m.xT[:, 4 * half + k, t * P:(t + 1) * P], m.ident[:, :])
                    mm.then_inc(turned, 1)

            @block.vector
            def _(dve):
                for i in range(4):
                    dve.wait_ge(turned, i + 1)
                    nc.vector.tensor_copy(ot[:, i // 2, 512 * (i % 2):512 * (i % 2) + 512], m.ps[i][:, :]).then_inc(copied, 1)

            @block.sync
            def _(sp):
                for t in range(2):
                    sp.wait_ge(copied, 2 * t + 2)
                    sp.dma_start(out[0, t * P:(t + 1) * P, :], ot[:, t, :]).then_inc(stored, 16)
                sp.wait_ge(stored, 32)


PI = float(np.nextafter(np.float32(np.pi), np.float32(0)))
TURN = [6.28125, 0.0019350051879882812, 3.019916050561733e-07]
NAMES2 = """mem_2 positions_2 ln_mix_2 w_in_2 b_merge_2 nsa_q_norm_2 nsa_k_norm_2 cmp_pe_2 cmp_w1_2 cmp_w2_2 gla_w_gate_2 gla_b_gate_2
gla_norm_2 mem_norm_2 mem_w_kv_2 mem_q_norm_2 mem_k_norm_2 w_branch_2 w_out_2 ln_mlp_2 w_up_2 w_down_2""".split()


def program(nc, A, out):
    with ExitStack() as ctx:
        ps = [ctx.enter_context(nc.psum_tensor(f"bank{i}", [P, 512], F32)) for i in range(8)]
        xT = ctx.enter_context(nc.sbuf_tensor("xT", [P, KT, SEQ], F32))
        first_block(nc, ps, xT, A, A["x"], A["meta_tokens"])
        second_block(nc, ps, xT, A, out)


def kernel(**inputs):
    import numpy as _np
    import concourse.bacc as _bacc
    from concourse import mybir as _mybir
    from concourse.bass_utils import run_bass_kernel_spmd as _run

    nc = _bacc.Bacc("TRN2", target_bir_lowering=False, num_devices=1)
    arrays, A = {}, {}
    for name in ["x", "meta_tokens"] + NAMES1 + NAMES2:
        a = _np.ascontiguousarray(inputs[name])
        arrays["in_" + name] = a
        A[name] = nc.dram_tensor("in_" + name, a.shape, _mybir.dt.from_np(a.dtype), kind="ExternalInput").ap()
    out = nc.dram_tensor("out", (1, SEQ, D), _mybir.dt.float32, kind="ExternalOutput").ap()
    program(nc, A, out)
    return _run(nc, [arrays], core_ids=[0]).results[0]["out"]
```
